# Optimizing a Trainium2 kernel written in Bass

```python
import math
import jax, jax.numpy as jnp
from jax import lax
import numpy as np

D_MODEL = 1024
BATCH = 1
SEQ = 1024
DEPTH = 1

CTX_LEN = 256
GRID_W = 64
DN_HEADS = 8
DN_HEAD_DIM = 128
DN_WIDTH = DN_HEADS * DN_HEAD_DIM
DN_CONV = 4
CHUNK = 64
LRU_WIDTH = 1024
LRU_BLOCKS = 16
LRU_BLOCK_DIM = LRU_WIDTH // LRU_BLOCKS
LRU_CONV = 4
LRU_C = 8.0
N_DIRS = 2
N_BRANCH = 2
D_FF = 4 * D_MODEL
FFN_CONV = 3
EPS = 1e-6
IN_SIZES = (DN_WIDTH, DN_WIDTH, DN_WIDTH, DN_WIDTH, N_DIRS * DN_HEADS, N_DIRS * DN_HEADS,
            LRU_WIDTH, LRU_WIDTH, N_BRANCH * D_MODEL)
D_IN = sum(IN_SIZES)

kernel_name = "hybrid_deltanet_rglru_convffn_dit"

def rmsnorm(u, gain):
    u32 = u.astype(jnp.float32)
    y = u32 * lax.rsqrt(jnp.mean(u32 * u32, axis=-1, keepdims=True) + EPS)
    return (y * gain.astype(jnp.float32)).astype(u.dtype)

def l2norm(u):
    return u * lax.rsqrt(jnp.sum(u * u, axis=-1, keepdims=True) + EPS)

def modulate(u, shift_c, scale_c, shift_x, scale_x, n_ctx):
    return jnp.concatenate([u[:, :n_ctx] * (1 + scale_c) + shift_c,
                            u[:, n_ctx:] * (1 + scale_x[:, None]) + shift_x[:, None]], axis=1)

def gate_rows(v, gate_c, gate_x, n_ctx):
    return jnp.concatenate([v[:, :n_ctx] * gate_c, v[:, n_ctx:] * gate_x[:, None]], axis=1)

def dwconv1d(u, w, pad_left):
    K, C = w.shape
    return lax.conv_general_dilated(u, w[:, None, :].astype(u.dtype), (1,), [(pad_left, K - 1 - pad_left)],
                                    dimension_numbers=('NWC', 'WIO', 'NWC'), feature_group_count=C)

def seg_dwconv1d(u, w, n_ctx, pad_left):
    return jnp.concatenate([dwconv1d(u[:, :n_ctx], w, pad_left), dwconv1d(u[:, n_ctx:], w, pad_left)], axis=1)

def ffn_dwconv(u, w, n_ctx, rows):
    B, T, C = u.shape
    lat = lax.conv_general_dilated(u[:, n_ctx:].reshape(B, rows, GRID_W, C), w[:, :, None, :].astype(u.dtype),
                                   (1, 1), 'SAME', dimension_numbers=('NHWC', 'HWIO', 'NHWC'),
                                   feature_group_count=C).reshape(B, T - n_ctx, C)
    if n_ctx == 0:
        return lat
    ctx_part = dwconv1d(u[:, :n_ctx], w[FFN_CONV // 2], FFN_CONV // 2)
    return jnp.concatenate([ctx_part, lat], axis=1)

def seg_flip(u, n_ctx):
    return jnp.concatenate([jnp.flip(u[:, :n_ctx], axis=1), jnp.flip(u[:, n_ctx:], axis=1)], axis=1)

def to_dirs(u_fwd, u_bwd, n_ctx):
    return jnp.stack([u_fwd, seg_flip(u_bwd, n_ctx)])

def from_dirs(o, n_ctx):
    return o[0] + seg_flip(o[1], n_ctx)

def delta_rule_chunked(q, k, v, g, beta):
    *lead, T, dk = q.shape
    dv = v.shape[-1]
    n = T // CHUNK
    q = q.reshape(*lead, n, CHUNK, dk)
    k = k.reshape(*lead, n, CHUNK, dk)
    v = v.reshape(*lead, n, CHUNK, dv)
    beta = beta.reshape(*lead, n, CHUNK)
    g = jnp.cumsum(g.reshape(*lead, n, CHUNK), axis=-1)
    incl = jnp.tril(jnp.ones((CHUNK, CHUNK), bool))
    strict = jnp.tril(jnp.ones((CHUNK, CHUNK), bool), -1)
    decay = jnp.exp(jnp.where(incl, g[..., :, None] - g[..., None, :], -jnp.inf))
    k_beta = k * beta[..., None]
    lower = jnp.where(strict, jnp.einsum('...ik,...jk->...ij', k_beta, k) * decay, 0.0)
    eye = jnp.eye(CHUNK, dtype=q.dtype)
    t_inv = lax.linalg.triangular_solve(eye + lower, jnp.broadcast_to(eye, lower.shape),
                                        left_side=True, lower=True, unit_diagonal=True)
    w = t_inv @ (k_beta * jnp.exp(g)[..., None])
    u = t_inv @ (v * beta[..., None])
    attn = jnp.where(incl, jnp.einsum('...ik,...jk->...ij', q, k) * decay, 0.0)

    def step(state, xs):
        qc, kc, uc, wc, ac, gc = xs
        v_new = uc - wc @ state
        out = (qc * jnp.exp(gc)[..., None]) @ state + ac @ v_new
        g_last = gc[..., -1:]
        state = state * jnp.exp(g_last)[..., None] + jnp.einsum(
            '...ck,...cv->...kv', kc * jnp.exp(g_last - gc)[..., None], v_new)
        return state, out

    xs = tuple(jnp.moveaxis(t, len(lead), 0) for t in (q, k, u, w, attn, g))
    state0 = jnp.zeros((*lead, dk, dv), q.dtype)
    _, out = lax.scan(step, state0, xs)
    return jnp.moveaxis(out, 0, len(lead)).reshape(*lead, T, dv)

def gated_deltanet(q, k, v, z, a, b, w_conv, a_log, dt_bias, onorm, n_ctx):
    B, T, _ = q.shape
    out_dtype = q.dtype
    f32 = jnp.float32
    qkv = jax.nn.silu(seg_dwconv1d(jnp.concatenate([q, k, v], axis=-1), w_conv, n_ctx, DN_CONV // 2))
    q, k, v = jnp.split(qkv.astype(f32), 3, axis=-1)
    heads = lambda t: t.reshape(B, T, DN_HEADS, DN_HEAD_DIM)
    q = l2norm(heads(q)) * DN_HEAD_DIM ** -0.5
    k = l2norm(heads(k))
    v = heads(v)
    g = -jnp.exp(a_log.astype(f32)) * jax.nn.softplus(a.astype(f32) + dt_bias.astype(f32))
    beta = jax.nn.sigmoid(b.astype(f32))
    tth = lambda t: jnp.moveaxis(t, 2, 3)
    o = delta_rule_chunked(tth(to_dirs(q, q, n_ctx)), tth(to_dirs(k, k, n_ctx)), tth(to_dirs(v, v, n_ctx)),
                           tth(to_dirs(g[:, :, 0], g[:, :, 1], n_ctx)),
                           tth(to_dirs(beta[:, :, 0], beta[:, :, 1], n_ctx)))
    o = from_dirs(jnp.moveaxis(o, 3, 2), n_ctx)
    o = rmsnorm(o, onorm) * jax.nn.silu(heads(z).astype(f32))
    return o.reshape(B, T, DN_WIDTH).astype(out_dtype)

def rg_lru(xb, yb, w_conv, b_conv, w_rg, b_rg, w_ig, b_ig, lam, n_ctx):
    B, T, W = xb.shape
    out_dtype = xb.dtype
    f32 = jnp.float32
    xc = (seg_dwconv1d(xb, w_conv, n_ctx, LRU_CONV // 2) + b_conv).astype(f32)
    xd = to_dirs(xc, xc, n_ctx)
    blocks = xd.reshape(N_DIRS, B, T, LRU_BLOCKS, LRU_BLOCK_DIM)

    def gate(w, bias):
        y = jnp.einsum('dbthi,dhij->dbthj', blocks, w.astype(f32)).reshape(N_DIRS, B, T, W)
        return jax.nn.sigmoid(y + bias.astype(f32)[:, None, None])

    r = gate(w_rg, b_rg)
    i = gate(w_ig, b_ig)
    log_a = -LRU_C * r * jax.nn.softplus(-lam.astype(f32))[:, None, None]
    a = jnp.exp(log_a)
    inp = jnp.sqrt(-jnp.expm1(2.0 * log_a)) * (i * xd)
    _, h = lax.associative_scan(lambda e, l: (e[0] * l[0], l[0] * e[1] + l[1]), (a, inp), axis=2)
    h = from_dirs(h, n_ctx)
    return (h * jax.nn.gelu(yb.astype(f32))).astype(out_dtype)

def setup_inputs(seed: int = 0) -> dict:
    key = jax.random.key(seed)
    ks = jax.random.split(key, 32)
    f32 = jnp.float32
    L = DEPTH
    nrm = lambda k, shape, scale: jax.random.normal(k, shape, f32) * scale
    x = nrm(ks[0], (BATCH, SEQ, D_MODEL), 1.0)
    c = nrm(ks[1], (BATCH, D_MODEL), 1.0)
    ctx = nrm(ks[2], (BATCH, CTX_LEN, D_MODEL), 1.0)
    c_ctx = nrm(ks[3], (D_MODEL,), 1.0)
    w_ada = nrm(ks[4], (L, D_MODEL, 6 * D_MODEL), 0.5 * D_MODEL ** -0.5)
    b_ada = nrm(ks[5], (L, 6 * D_MODEL), 0.02)
    g_pre_mix = 1.0 + nrm(ks[6], (L, D_MODEL), 0.05)
    g_post_mix = 1.0 + nrm(ks[7], (L, D_MODEL), 0.05)
    g_pre_ffn = 1.0 + nrm(ks[8], (L, D_MODEL), 0.05)
    g_post_ffn = 1.0 + nrm(ks[9], (L, D_MODEL), 0.05)
    w_in = nrm(ks[10], (L, D_MODEL, D_IN), D_MODEL ** -0.5)
    b_merge = nrm(ks[11], (L, N_BRANCH * D_MODEL), 0.02)
    dn_conv = nrm(ks[12], (L, DN_CONV, 3 * DN_WIDTH), DN_CONV ** -0.5)
    dn_a_log = jnp.log(jax.random.uniform(ks[13], (L, N_DIRS, DN_HEADS), f32, 1.0, 16.0))
    dt = jnp.exp(jax.random.uniform(ks[14], (L, N_DIRS, DN_HEADS), f32, math.log(1e-3), math.log(1e-1)))
    dn_dt_bias = dt + jnp.log(-jnp.expm1(-dt))
    dn_onorm = 1.0 + nrm(ks[15], (L, DN_HEAD_DIM), 0.05)
    lru_conv = nrm(ks[16], (L, LRU_CONV, LRU_WIDTH), LRU_CONV ** -0.5)
    lru_conv_b = nrm(ks[17], (L, LRU_WIDTH), 0.02)
    lru_w_rg = nrm(ks[18], (L, N_DIRS, LRU_BLOCKS, LRU_BLOCK_DIM, LRU_BLOCK_DIM), LRU_BLOCK_DIM ** -0.5)
    lru_b_rg = nrm(ks[19], (L, N_DIRS, LRU_WIDTH), 0.02)
    lru_w_ig = nrm(ks[20], (L, N_DIRS, LRU_BLOCKS, LRU_BLOCK_DIM, LRU_BLOCK_DIM), LRU_BLOCK_DIM ** -0.5)
    lru_b_ig = nrm(ks[21], (L, N_DIRS, LRU_WIDTH), 0.02)
    a0 = jax.random.uniform(ks[22], (L, N_DIRS, LRU_WIDTH), f32, 0.9, 0.999)
    s = a0 ** (1.0 / LRU_C)
    lru_lambda = jnp.log(s) - jnp.log1p(-s)
    w_branch_dn = nrm(ks[23], (L, DN_WIDTH, D_MODEL), DN_WIDTH ** -0.5)
    w_branch_lru = nrm(ks[24], (L, LRU_WIDTH, D_MODEL), LRU_WIDTH ** -0.5)
    w_out = nrm(ks[25], (L, D_MODEL, D_MODEL), D_MODEL ** -0.5)
    w_up = nrm(ks[26], (L, D_MODEL, 2 * D_FF), D_MODEL ** -0.5)
    ffn_dw = nrm(ks[27], (L, FFN_CONV, FFN_CONV, D_FF), 1.0 / FFN_CONV)
    ffn_dw_b = nrm(ks[28], (L, D_FF), 0.02)
    w_down = nrm(ks[29], (L, D_FF, D_MODEL), D_FF ** -0.5)
    return {"x": x, "c": c, "ctx": ctx, "c_ctx": c_ctx, "w_ada": w_ada, "b_ada": b_ada,
            "g_pre_mix": g_pre_mix, "g_post_mix": g_post_mix, "g_pre_ffn": g_pre_ffn, "g_post_ffn": g_post_ffn,
            "w_in": w_in, "b_merge": b_merge, "dn_conv": dn_conv, "dn_a_log": dn_a_log,
            "dn_dt_bias": dn_dt_bias, "dn_onorm": dn_onorm, "lru_conv": lru_conv, "lru_conv_b": lru_conv_b,
            "lru_w_rg": lru_w_rg, "lru_b_rg": lru_b_rg, "lru_w_ig": lru_w_ig, "lru_b_ig": lru_b_ig,
            "lru_lambda": lru_lambda, "w_branch_dn": w_branch_dn, "w_branch_lru": w_branch_lru,
            "w_out": w_out, "w_up": w_up, "ffn_dw": ffn_dw, "ffn_dw_b": ffn_dw_b, "w_down": w_down}

def reference(x, c, ctx, c_ctx, w_ada, b_ada, g_pre_mix, g_post_mix, g_pre_ffn, g_post_ffn, w_in, b_merge,
              dn_conv, dn_a_log, dn_dt_bias, dn_onorm, lru_conv, lru_conv_b, lru_w_rg, lru_b_rg, lru_w_ig,
              lru_b_ig, lru_lambda, w_branch_dn, w_branch_lru, w_out, w_up, ffn_dw, ffn_dw_b, w_down):
    n_ctx = ctx.shape[1]
    rows = x.shape[1] // GRID_W
    B = x.shape[0]
    split_at = [int(s) for s in np.cumsum(IN_SIZES)[:-1]]
    h = jnp.concatenate([ctx, x], axis=1)
    silu_c = jax.nn.silu(c)
    silu_cc = jax.nn.silu(c_ctx)
    for l in range(DEPTH):
        last = l == DEPTH - 1
        m_x = jnp.split(silu_c @ w_ada[l] + b_ada[l], 6, axis=-1)
        m_c = jnp.split(silu_cc @ w_ada[l] + b_ada[l], 6, axis=-1)
        u = modulate(rmsnorm(h, g_pre_mix[l]), m_c[0], m_c[1], m_x[0], m_x[1], n_ctx)
        T = u.shape[1]
        q, k, v, z, a, b, xl, yl, mg = jnp.split(u @ w_in[l], split_at, axis=-1)
        y_dn = gated_deltanet(q, k, v, z, a.reshape(B, T, N_DIRS, DN_HEADS), b.reshape(B, T, N_DIRS, DN_HEADS),
                              dn_conv[l], dn_a_log[l], dn_dt_bias[l], dn_onorm[l], n_ctx)
        y_lru = rg_lru(xl, yl, lru_conv[l], lru_conv_b[l], lru_w_rg[l], lru_b_rg[l], lru_w_ig[l], lru_b_ig[l],
                       lru_lambda[l], n_ctx)
        drop = n_ctx if last else 0
        n_cur = n_ctx - drop
        h, y_dn, y_lru, mg = h[:, drop:], y_dn[:, drop:], y_lru[:, drop:], mg[:, drop:]
        g_dn, g_lru = jnp.split(jax.nn.sigmoid(mg + b_merge[l]), N_BRANCH, axis=-1)
        mix = (g_dn * (y_dn @ w_branch_dn[l]) + g_lru * (y_lru @ w_branch_lru[l])) @ w_out[l]
        h = h + gate_rows(rmsnorm(mix, g_post_mix[l]), m_c[2], m_x[2], n_cur)
        u = modulate(rmsnorm(h, g_pre_ffn[l]), m_c[3], m_c[4], m_x[3], m_x[4], n_cur)
        f_gate, f_val = jnp.split(u @ w_up[l], 2, axis=-1)
        f_gate = ffn_dwconv(f_gate, ffn_dw[l], n_cur, rows) + ffn_dw_b[l]
        f = jax.nn.gelu(f_gate) * f_val
        h = h + gate_rows(rmsnorm(f @ w_down[l], g_post_ffn[l]), m_c[5], m_x[5], n_cur)
    return h


_drawn_inputs = setup_inputs


def setup_inputs(seed=0):
    import zlib

    import numpy as np

    out = dict(_drawn_inputs(seed))
    spreads = {}
    factors = {'ctx': 3.287,
     'g_pre_mix': 3.089,
     'g_post_mix': 3.66,
     'g_pre_ffn': 3.008,
     'g_post_ffn': 3.79,
     'b_merge': 8.0,
     'dn_a_log': 4.024,
     'dn_onorm': 8.0,
     'lru_conv_b': 2.672,
     'lru_b_rg': 44.49,
     'lru_b_ig': 33.361,
     'ffn_dw_b': 8.0}
    for name, (base, spread) in spreads.items():
        noise = np.random.default_rng([zlib.crc32(name.encode()), seed]).standard_normal(out[name].shape)
        drawn = base * np.exp(spread * noise) if base else spread * noise
        out[name] = __import__('jax').numpy.asarray(drawn.astype(out[name].dtype))
    for name, factor in factors.items():
        out[name] = (out[name] * factor).astype(out[name].dtype)
    return out
```

```python
from contextlib import ExitStack

import concourse.bass as bass
from concourse import mybir

F32 = mybir.dt.float32
F32R = mybir.dt.float32r
BF16 = mybir.dt.bfloat16
ALU = mybir.AluOpType
ACT = mybir.ActivationFunctionType
AX_X = mybir.AxisListType.X

P = 128
D = 1024
KT = D // P
N_CTX = 256
SEQ = 1024
T = N_CTX + SEQ
HEADS = 8
CH = 128
NCH = T // CH
CTX_CH = N_CTX // CH
W_CONV = 4
PAD_LEFT = 2
D_FF = 4 * D
FF_TILES = D_FF // P
GRID_W = 64
ROWS = SEQ // GRID_W
EPS = 1e-6
LRU_C = 8.0
OFF = -1e30

SEG_ALL = [(0, 256), (256, 512), (768, 512)]
SEG_LAT = [(256, 512), (768, 512)]

COL_Q, COL_K, COL_V, COL_Z = 0, D, 2 * D, 3 * D
COL_AB = 4 * D
COL_XL = COL_AB + 32
COL_YL = COL_XL + D
COL_MG = COL_YL + D

PB_ADA, P_PRE_MIX, P_POST_MIX, P_PRE_FFN, P_POST_FFN, P_B_MERGE, P_C, P_C_CTX = 0, 48, 56, 64, 72, 80, 96, 104
P_LRU_CONV, P_LRU_CONV_B, P_B_RG, P_B_IG, P_LAM, P_ONORM = 112, 144, 152, 168, 184, 200
P_DN_CONV, P_FFN_DW, P_FFN_DW_B = 201, 297, 585
N_PAR = 617


class Shared:
    pass


def end_phase(nc, sh):
    nc.clear_and_free_semaphores(sh.held)
    sh.held.clear()
    nc.all_engine_barrier()


def weight_view(w):
    return w.rearrange("(k p) n -> p k n", p=P)


def norm_and_modulate(nc, sh, io):
    with ExitStack() as ctx:
        sb = lambda n, s, d=F32: ctx.enter_context(nc.sbuf_tensor(n, s, d))
        sem = sh.sem
        rows = sb("a_rows", [P, 7, P])
        ada_w = sb("a_ada_w", [P, 2, KT, 512])
        tok = sb("a_tok", [P, NCH, D])
        sq_junk = sb("a_sq", [P, D])
        silu_c = sb("a_silu_c", [P, KT, 2])
        ss = sb("a_ss", [P, NCH])
        rms = sb("a_rms", [P, NCH])
        rstd = sb("a_rstd", [P, NCH])
        ut = sb("a_ut", [P, 2, 512])
        ps_par = [ctx.enter_context(nc.psum_tensor(f"a_ps_par{i}", [P, 512], F32)) for i in range(2)]
        ps_m = ctx.enter_context(nc.psum_tensor("a_ps_m", [P, 512], F32))
        ps_t = [ctx.enter_context(nc.psum_tensor(f"a_ps_t{i}", [P, 512], F32)) for i in range(4)]
        rows_in = sem("a_rows_in")
        tok_in = sem("a_tok_in")
        ada_in = [sem(f"a_ada_in{i}") for i in range(2)]
        ada_used = sem("a_ada_used")
        consts = sem("a_consts")
        par_t = sem("a_par_transposed")
        par_ok = sem("a_par_ready")
        silu_ok = sem("a_silu_ready")
        m_ok = sem("a_m_ready")
        vec_ok = sem("a_vectors_ready")
        sq_ok = sem("a_squares_ready")
        rms_ok = sem("a_rms_ready")
        rstd_ok = sem("a_rstd_ready")
        scaled = sem("a_rows_scaled")
        tr_ok = sem("a_tile_transposed")
        ut_ok = sem("a_u_ready")
        uh_ok = sem("a_u_high_ready")
        ul_ok = sem("a_u_low_ready")
        block = ctx.enter_context(nc.Block())

        row = lambda name: io[name].rearrange("l (r p) -> (l r) p", p=P)
        row_loads = [
            (0, 0, row("b_ada")), (0, 48, row("g_pre_mix")), (0, 56, row("g_post_mix")),
            (0, 64, row("g_pre_ffn")), (0, 72, row("g_post_ffn")), (0, 80, row("b_merge")),
            (0, 96, row("c")), (0, 104, io["c_ctx"].rearrange("(r p) -> r p", p=P)),
            (1, 0, io["lru_conv"].rearrange("l k (r p) -> (l k r) p", p=P)), (1, 32, row("lru_conv_b")),
            (1, 40, io["lru_b_rg"].rearrange("l d (r p) -> (l d r) p", p=P)),
            (1, 56, io["lru_b_ig"].rearrange("l d (r p) -> (l d r) p", p=P)),
            (1, 72, io["lru_lambda"].rearrange("l d (r p) -> (l d r) p", p=P)),
            (1, 88, row("dn_onorm")),
            (2, 0, io["dn_conv"].rearrange("l k (r p) -> (l k r) p", p=P)),
        ]
        dw = io["ffn_dw"].rearrange("l a b (r p) -> (l a b r) p", p=P)
        row_loads += [(3 + i, 0, dw[96 * i:96 * i + 96]) for i in range(3)]
        row_loads.append((6, 0, row("ffn_dw_b")))
        row_tiles = [(0, 112, 0, 0), (1, 89, 0, 112), (2, 96, 0, P_DN_CONV), (3, 96, 0, P_FFN_DW),
                     (4, 96, 0, P_FFN_DW + 96), (5, 96, 1, 0), (6, 32, 1, 96)]
        split = P_FFN_DW + 192

        @block.sync
        def _(e):
            for tile, r0, src in row_loads:
                e.dma_start(rows[r0:r0 + src.shape[0], tile, :], src).then_inc(rows_in, 16)
            ada = weight_view(io["w_ada"][0])
            with e.Fori(0, 6) as i:
                for s in range(2):
                    e.wait_ge(ada_used, i * 2 + s + 1)
                    e.dma_start(ada_w[:, s], ada[:, :, bass.ds(i * 1024 + s * 512, 512)]).then_inc(ada_in[s], 16)

        @block.scalar
        def _(e):
            e.dma_start(tok[:, 0:CTX_CH, :], io["ctx"][0].rearrange("(t p) d -> p t d", p=P)).then_inc(tok_in, 16)
            e.dma_start(tok[:, CTX_CH:, :], io["x"][0].rearrange("(t p) d -> p t d", p=P)).then_inc(tok_in, 16)
            e.wait_ge(par_ok, 2)
            e.activation(silu_c[:, :, 0], sh.par[:, P_C:P_C + KT], ACT.Silu).then_inc(silu_ok, 1)
            e.activation(silu_c[:, :, 1], sh.par[:, P_C_CTX:P_C_CTX + KT], ACT.Silu).then_inc(silu_ok, 1)
            e.wait_ge(tok_in, 32)
            for t in range(NCH):
                if t:
                    e.wait_ge(sq_ok, t)
                e.activation(sq_junk[:], tok[:, t, :], ACT.Square, accum_out=ss[:, t:t + 1]).then_inc(sq_ok, 1)
            e.wait_ge(sq_ok, NCH)
            e.wait_ge(consts, 6)
            e.activation(rms[:], ss[:], ACT.Sqrt, bias=sh.eps[:, 0:1], scale=1.0 / D).then_inc(rms_ok, 1)
            e.wait_ge(vec_ok, 5)
            n = 0
            for k in range(KT):
                for t0, tn in SEG_ALL:
                    s = 1 if t0 == 0 else 0
                    e.wait_ge(tr_ok, n + 1)
                    if n >= 2:
                        e.wait_ge(ul_ok, n - 1)
                    e.activation(ut[:, n % 2, 0:tn], ps_t[n % 4][:, 0:tn], ACT.Identity,
                                 bias=sh.m[:, k, s:s + 1], scale=sh.pre_mix[:, s, k:k + 1]).then_inc(ut_ok, 1)
                    n += 1

        @block.gpsimd
        def _(e):
            build_constants(e, sh, consts)

        @block.tensor
        def _(e):
            e.wait_ge(rows_in, 16 * len(row_loads))
            e.wait_ge(consts, 6)
            for tile, nr, bank, c0 in row_tiles:
                e.transpose(ps_par[bank][:, c0:c0 + nr], rows[0:nr, tile, :], sh.ident[0:nr, 0:nr]).then_inc(par_t, 1)
            e.sem_inc(ada_used, 2)
            e.wait_ge(silu_ok, 2)
            with e.Fori(0, 6) as i:
                for s in range(2):
                    e.wait_ge(ada_in[s], i * 16 + 16)
                    for b in range(4):
                        for k in range(KT):
                            mm = e.matmul(ps_m[:, bass.ds(i * 16 + s * 8 + b * 2, 2)], ada_w[:, s, k, b * P:b * P + P],
                                          silu_c[:, k, :], start=(k == 0), stop=(k == KT - 1))
                    mm.then_inc(ada_used, 1)
            e.wait_ge(scaled, NCH)
            n = 0
            for k in range(KT):
                for t0, tn in SEG_ALL:
                    if n >= 4:
                        e.wait_ge(ut_ok, n - 3)
                    for j in range(tn // P):
                        tr = e.transpose(ps_t[n % 4][:, j * P:j * P + P], tok[:, t0 // P + j, k * P:k * P + P],
                                         sh.ident[:])
                    tr.then_inc(tr_ok, 1)
                    n += 1

        @block.vector
        def _(e):
            e.memset(sh.eps[:, 0:1], EPS).then_inc(consts, 1)
            e.memset(sh.eps[:, 1:2], P * EPS).then_inc(consts, 1)
            e.wait_ge(par_t, len(row_tiles))
            e.tensor_copy(sh.par[:, 0:split], ps_par[0][:, 0:split]).then_inc(par_ok, 1)
            e.tensor_copy(sh.par[:, split:N_PAR], ps_par[1][:, 0:P]).then_inc(par_ok, 1)
            e.wait_ge(rms_ok, 1)
            e.reciprocal(rstd[:], rms[:]).then_inc(rstd_ok, 1)
            e.wait_ge(rstd_ok, 1)
            for t in range(NCH):
                e.tensor_scalar(tok[:, t, :], tok[:, t, :], rstd[:, t:t + 1], None, ALU.mult).then_inc(scaled, 1)
            e.wait_ge(par_ok, 2)
            e.wait_ge(ada_used, 14)
            e.tensor_tensor(sh.m[:], ps_m[:, 0:96].rearrange("p (n s) -> p n s", s=2),
                            sh.par[:, PB_ADA:PB_ADA + 48].unsqueeze(2).broadcast_to([P, 48, 2]), ALU.add).then_inc(m_ok, 1)
            e.wait_ge(m_ok, 1)
            m = sh.m
            for s in range(2):
                e.scalar_tensor_tensor(out=sh.pre_mix[:, s, :], in0=m[:, KT:2 * KT, s], scalar=1.0,
                                       in1=sh.par[:, P_PRE_MIX:P_PRE_MIX + KT], op0=ALU.add, op1=ALU.mult).then_inc(vec_ok, 1)
            e.tensor_tensor(sh.post_mix[:], m[:, 2 * KT:3 * KT, 0], sh.par[:, P_POST_MIX:P_POST_MIX + KT],
                            ALU.mult).then_inc(vec_ok, 1)
            e.scalar_tensor_tensor(out=sh.pre_ffn[:], in0=m[:, 4 * KT:5 * KT, 0], scalar=1.0,
                                   in1=sh.par[:, P_PRE_FFN:P_PRE_FFN + KT], op0=ALU.add, op1=ALU.mult).then_inc(vec_ok, 1)
            e.tensor_tensor(sh.post_ffn[:], m[:, 5 * KT:6 * KT, 0], sh.par[:, P_POST_FFN:P_POST_FFN + KT],
                            ALU.mult).then_inc(vec_ok, 1)
            n = 0
            for k in range(KT):
                for t0, tn in SEG_ALL:
                    e.wait_ge(ut_ok, n + 1)
                    e.tensor_copy(sh.u_hi[:, k, t0:t0 + tn], ut[:, n % 2, 0:tn]).then_inc(uh_ok, 1)
                    e.wait_ge(uh_ok, n + 1)
                    e.tensor_tensor(sh.u_lo[:, k, t0:t0 + tn], ut[:, n % 2, 0:tn],
                                    sh.u_hi[:, k, t0:t0 + tn].bitcast(F32), ALU.subtract).then_inc(ul_ok, 1)
                    n += 1


def build_constants(e, sh, consts):
    e.memset(sh.ident[:], 0.0).then_inc(consts, 1)
    e.memset(sh.ones[:], 1.0).then_inc(consts, 1)
    e.wait_ge(consts, 4)
    e.affine_select(out=sh.ident[:], in_=sh.ident[:], compare_op=ALU.not_equal, fill=1.0, base=0,
                    pattern=[[-1, P]], channel_multiplier=1).then_inc(consts, 1)
    e.memset(sh.warm[:], 0.0).then_inc(consts, 1)


def build_triangles(e, sh, consts, base):
    e.memset(sh.tri[:], 1.0)
    e.memset(sh.off[:], 0.0)
    e.memset(sh.strict[:], 1.0)
    e.memset(sh.last_row[:], 1.0)
    e.memset(sh.level[:], 0.0).then_inc(consts, 1)
    e.wait_ge(consts, base + 1)
    for d, sign in ((0, 1), (1, -1)):
        for tile, shift, fill in ((sh.tri, 0, 0.0), (sh.off, 0, OFF), (sh.strict, -1, 0.0)):
            e.affine_select(out=tile[:, d], in_=tile[:, d], compare_op=ALU.is_ge, fill=fill, base=shift,
                            pattern=[[sign, P]], channel_multiplier=-sign)
        end = P - 1 if d == 0 else 0
        e.affine_select(out=sh.last_row[:, d], in_=sh.last_row[:, d], compare_op=ALU.is_equal, fill=0.0,
                        base=-end, pattern=[[0, P]], channel_multiplier=1)
    for d in range(2):
        for l in range(7):
            b = 1 << l
            half = 1 - d
            view = sh.level[:, d, l, :].rearrange("p (n t b) -> p n t b", t=2, b=b)[:, :, half, :]
            last = e.memset(view, 1.0)
    last.then_inc(consts, 1)
    e.wait_ge(consts, base + 2)
    for step in range(2):
        for d in range(2):
            for l in range(7):
                b = 1 << l
                half = 1 - d
                view = sh.level[:, d, l, :].rearrange("p (n t b) -> p n t b", t=2, b=b)[:, :, half, :]
                low = 0 if d == 0 else b
                if step == 0:
                    last = e.affine_select(out=view, in_=view, compare_op=ALU.is_ge, fill=0.0, base=-low,
                                           pattern=[[-2 * b, P // (2 * b)], [0, b]], channel_multiplier=1)
                else:
                    last = e.affine_select(out=view, in_=view, compare_op=ALU.is_ge, fill=0.0, base=low + b - 1,
                                           pattern=[[2 * b, P // (2 * b)], [0, b]], channel_multiplier=-1)
        last.then_inc(consts, 1)
        e.wait_ge(consts, base + 3 + step)


def decay_gates(nc, sh, io):
    with ExitStack() as ctx:
        sb = lambda n, s, d=F32: ctx.enter_context(nc.sbuf_tensor(n, s, d))
        sem = sh.sem
        raw = sb("g_raw", [P, KT, P])
        w_hi = sb("g_w_hi", [P, KT, P], F32R)
        w_lo = sb("g_w_lo", [P, KT, P], F32R)
        a_log = sb("g_a_log", [32, 1])
        dt_b = sb("g_dt_bias", [32, 1])
        neg_a = sb("g_neg_a", [32, 1])
        ab = sb("g_ab", [32, T])
        x = sb("g_x", [32, T])
        em = sb("g_em", [32, T])
        up = sb("g_up", [32, T])
        ln = sb("g_ln", [32, T])
        rec = sb("g_rec", [32, T])
        beta_r = sb("g_beta_r", [32, T])
        gb = sb("g_gb", [P, NCH, 64])
        diff = sb("g_diff", [P, NCH, 16])
        ps = ctx.enter_context(nc.psum_tensor("g_ps", [P, 3, 512], F32))
        ps_gb = ctx.enter_context(nc.psum_tensor("g_ps_gb", [P, 2, 512], F32))
        ps_c = ctx.enter_context(nc.psum_tensor("g_ps_c", [P, 512], F32))
        loaded, small_in, hi, lo = sem("g_loaded"), sem("g_small_in"), sem("g_hi"), sem("g_lo")
        consts, zeroed = sem("g_consts"), sem("g_zeroed")
        ab_mm, dve, act = sem("g_ab_mm"), sem("g_dve_step"), sem("g_act_step")
        gb_t, cum_mm, tot_mm, row_t = sem("g_gb_t"), sem("g_cum_mm"), sem("g_tot_mm"), sem("g_row_t")
        block = ctx.enter_context(nc.Block())

        @block.sync
        def _(e):
            e.dma_start(raw[:], weight_view(io["w_in"][0])[:, :, COL_AB:COL_AB + P]).then_inc(loaded, 16)
            e.wait_ge(zeroed, 2)
            e.dma_start(a_log[0:16, :], io["dn_a_log"][0].rearrange("d (h o) -> (d h) o", o=1)).then_inc(small_in, 16)
            e.dma_start(dt_b[0:16, :], io["dn_dt_bias"][0].rearrange("d (h o) -> (d h) o", o=1)).then_inc(small_in, 16)

        @block.gpsimd
        def _(e):
            e.memset(a_log[:], 0.0).then_inc(zeroed, 1)
            e.memset(dt_b[:], 0.0).then_inc(zeroed, 1)
            build_triangles(e, sh, consts, 0)

        @block.tensor
        def _(e):
            e.wait_ge(lo, 1)
            for s, (t0, tn) in enumerate(SEG_ALL):
                n = 0
                for k in range(KT):
                    for w, u in ((w_hi, sh.u_hi), (w_lo, sh.u_hi), (w_hi, sh.u_lo)):
                        mm = e.matmul(ps[:, s, 0:tn], w[:, k, :], u[:, k, t0:t0 + tn], start=(n == 0), stop=(n == 23))
                        n += 1
                mm.then_inc(ab_mm, 1)
            e.wait_ge(dve, 12)
            e.wait_ge(act, 5)
            for c in range(NCH):
                for half, src in ((0, x), (32, beta_r)):
                    o = (c % 5) * 64 + half
                    tr = e.transpose(ps_gb[:, c // 5, o:o + 32], src[:, c * P:c * P + P], sh.ident[0:32, 0:32])
            tr.then_inc(gb_t, 1)
            e.wait_ge(dve, 14)
            e.wait_ge(consts, 4)
            for d in range(2):
                mm = e.matmul(ps_c[:, d * 80:d * 80 + 80], sh.tri[:, d, :], gb[:, :, d * 8:d * 8 + 8],
                              start=True, stop=True)
            mm.then_inc(cum_mm, 1)
            e.wait_ge(dve, 16)
            for d in range(2):
                mm = e.matmul(ps_c[:, 160 + d * 80:240 + d * 80], sh.last_row[:, d, :], sh.gcol[:, :, d * 8:d * 8 + 8],
                              start=True, stop=True)
            mm.then_inc(tot_mm, 1)
            for c in range(NCH):
                tr = e.transpose(ps[0:16, c // 4, (c % 4) * P:(c % 4) * P + P], sh.gcol[:, c, :], sh.ident[:])
            tr.then_inc(row_t, 1)

        @block.vector
        def _(e):
            e.wait_ge(loaded, 16)
            e.tensor_copy(w_hi[:], raw[:]).then_inc(hi, 1)
            e.wait_ge(hi, 1)
            e.tensor_tensor(w_lo[:], raw[:], w_hi[:].bitcast(F32), ALU.subtract).then_inc(lo, 1)
            for s, (t0, tn) in enumerate(SEG_ALL):
                e.wait_ge(ab_mm, s + 1)
                e.tensor_copy(ab[:, t0:t0 + tn], ps[0:32, s, 0:tn]).then_inc(dve, 1)
            e.wait_ge(dve, 3)
            e.wait_ge(small_in, 32)
            e.tensor_scalar(x[:], ab[:], dt_b[:, 0:1], None, ALU.add).then_inc(dve, 1)
            e.wait_ge(act, 2)
            e.tensor_scalar(up[:], em[:], 1.0, None, ALU.add).then_inc(dve, 1)
            e.wait_ge(dve, 5)
            e.reciprocal(rec[:], up[:]).then_inc(dve, 1)
            e.scalar_tensor_tensor(out=em[:], in0=up[:], scalar=-1.0, in1=em[:], op0=ALU.add, op1=ALU.subtract).then_inc(dve, 1)
            e.wait_ge(dve, 7)
            e.scalar_tensor_tensor(out=em[:], in0=em[:], scalar=-1.0, in1=rec[:], op0=ALU.mult, op1=ALU.mult).then_inc(dve, 1)
            e.wait_ge(act, 3)
            e.wait_ge(dve, 8)
            e.tensor_tensor(ln[:], ln[:], em[:], ALU.add).then_inc(dve, 1)
            e.wait_ge(dve, 9)
            e.scalar_tensor_tensor(out=x[:], in0=x[:], scalar=0.0, in1=ln[:], op0=ALU.max, op1=ALU.add).then_inc(dve, 1)
            e.wait_ge(act, 4)
            e.tensor_scalar(neg_a[:], neg_a[:], -1.0, None, ALU.mult).then_inc(dve, 1)
            e.wait_ge(dve, 11)
            e.tensor_scalar(x[:], x[:], neg_a[:, 0:1], None, ALU.mult).then_inc(dve, 1)
            e.wait_ge(gb_t, 1)
            for i in range(2):
                e.tensor_copy(gb[:, 5 * i:5 * i + 5, :], ps_gb[:, i, 0:320].rearrange("p (c n) -> p c n", c=5)).then_inc(dve, 1)
            e.wait_ge(dve, 14)
            e.wait_ge(cum_mm, 1)
            for d in range(2):
                e.tensor_copy(sh.gcol[:, :, d * 8:d * 8 + 8], ps_c[:, d * 80:d * 80 + 80].rearrange("p (c h) -> p c h", c=NCH)).then_inc(dve, 1)
            e.tensor_copy(sh.beta[:], gb[:, :, 48:64]).then_inc(dve, 1)
            e.tensor_scalar(sh.neg_beta[:], gb[:, :, 48:64], -1.0, None, ALU.mult).then_inc(dve, 1)
            e.wait_ge(tot_mm, 1)
            e.wait_ge(dve, 16)
            for d in range(2):
                e.tensor_tensor(diff[:, :, d * 8:d * 8 + 8], ps_c[:, 160 + d * 80:240 + d * 80].rearrange("p (c h) -> p c h", c=NCH),
                                sh.gcol[:, :, d * 8:d * 8 + 8], ALU.subtract).then_inc(dve, 1)
            e.wait_ge(act, 6)
            e.tensor_scalar(sh.neg_eg[:], sh.eg[:], -1.0, None, ALU.mult).then_inc(dve, 1)
            e.wait_ge(row_t, 1)
            e.tensor_copy(sh.grow[:], ps[0:16, :, :].rearrange("p b n -> p (b n)")[:, 0:T]).then_inc(dve, 1)
            e.tensor_copy(sh.ident_r[:, 0], sh.ident[:])
            e.tensor_scalar(sh.ident_r[:, 1], sh.ident[:], -1.0, None, ALU.mult)

        @block.scalar
        def _(e):
            e.wait_ge(dve, 4)
            e.activation(em[:], x[:], ACT.Abs).then_inc(act, 1)
            e.wait_ge(act, 1)
            e.activation(em[:], em[:], ACT.Exp, scale=-1.0).then_inc(act, 1)
            e.wait_ge(dve, 5)
            e.activation(ln[:], up[:], ACT.Ln).then_inc(act, 1)
            e.wait_ge(small_in, 32)
            e.activation(neg_a[:], a_log[:], ACT.Exp).then_inc(act, 1)
            e.activation(beta_r[:], ab[:], ACT.Sigmoid).then_inc(act, 1)
            e.wait_ge(dve, 16)
            e.activation(sh.eg[:], sh.gcol[:], ACT.Exp).then_inc(act, 1)
            e.wait_ge(dve, 20)
            for d in range(2):
                e.activation(sh.eg_tot[:, :, d * 8:d * 8 + 8], ps_c[:, 160 + d * 80:240 + d * 80].rearrange("p (c h) -> p c h", c=NCH), ACT.Exp)
            e.activation(sh.k_decay[:], diff[:], ACT.Exp).then_inc(act, 1)


BLOCKS = [[0, 1, 2, 3], [4, 5, 6, 7], [8, 9]]
BATCHES = [(d, b) for b in range(3) for d in range(2)]
FWD_ORDER = list(range(NCH))
BWD_ORDER = [1, 0] + list(range(NCH - 1, CTX_CH - 1, -1))


def deltanet(nc, sh, io):
    with ExitStack() as ctx:
        sb = lambda n, s, d=F32: ctx.enter_context(nc.sbuf_tensor(n, s, d))
        sem = sh.sem
        raw = sb("d_raw", [P, 2, KT, P])
        w_hi = sb("d_w_hi", [P, 2, KT, P], F32R)
        w_lo = sb("d_w_lo", [P, 2, KT, P], F32R)
        PADN = N_CTX + SEQ + 6
        CVN = PADN - 3
        LAT0 = N_CTX + 3
        pad = sb("d_pad", [P, PADN])
        cv = sb("d_cv", [P, CVN])
        qt = sb("d_qt", [P, T])
        kt = sb("d_kt", [P, T])
        nt = sb("d_nt", [P, T])
        krow = sb("d_krow", [P, NCH, P])
        vrow = sb("d_vrow", [P, NCH, P])
        uf = sb("d_uf", [P, 2, NCH, P])
        att = sb("d_att", [P, 2, NCH - CTX_CH, P])
        sel = sb("d_sel", [16, P])
        dec = sb("d_dec", [P, 4, P])
        at = sb("d_at", [P, 4, P])
        ah = sb("d_ah", [P, 4, P], F32R)
        al = sb("d_al", [P, 4, P], F32R)
        am = sb("d_am", [P, 2, 4, P], F32R)
        tt = sb("d_tt", [P, 4, P], F32R)
        ut = sb("d_ut", [P, 4, P], F32R)
        xs = sb("d_xs", [P, 4, P], F32R)
        st = sb("d_state", [P, 2, P])
        rr = sb("d_rr", [P, 2, P])
        vn = sb("d_vn", [P, 2, P])
        kd = sb("d_kd", [P, 2, 2, P])
        o = sb("d_o", [P, NCH - CTX_CH, P])
        oss = sb("d_oss", [P, NCH - CTX_CH])
        ors = sb("d_ors", [P, NCH - CTX_CH])
        ps_d = [ctx.enter_context(nc.psum_tensor(f"d_ps_d{i}", [P, 512], F32)) for i in range(4)]
        ps_x = ctx.enter_context(nc.psum_tensor("d_ps_x", [P, 4, 512], F32))
        xflat = ps_x[:].rearrange("p b n -> p (b n)")

        w_in_ok = [sem(f"d_w_in{i}") for i in range(2)]
        w_hi_ok, w_split = sem("d_w_hi_ok"), sem("d_w_split")
        mm_ok, evac = sem("d_mm_ok"), sem("d_evac")
        pad0, conv_step, conv_ok, silu_ok = sem("d_pad0"), sem("d_conv_step"), sem("d_conv_ok"), sem("d_silu_ok")
        nsq, nmm, nln, nex, nrm = (sem(f"d_norm_{x}") for x in ("sq", "mm", "ln", "exp", "ok"))
        row_t, row_ok = sem("d_row_t"), sem("d_row_ok")
        sel_ok, rb_ok, dd_ok, dec_ok, kk_ok, at_step, attn_ok = (
            sem(f"d_{x}") for x in ("sel_ok", "rb_ok", "dd_ok", "dec_ok", "kk_ok", "at_ok", "attn_ok"))
        ats_ok, ah_ok, al_ok, am_ok = (sem(f"d_{x}") for x in ("ats_ok", "ah_ok", "al_ok", "am_ok"))
        u1_ok, t1_ps, tt_ok, x_ps, xs_ok, t_ps, u_ps, ut_ok, uf_ps, uf_ok = (
            sem(f"d_{x}") for x in ("u1_ok", "t1_ps", "tt_ok", "x_ps", "xs_ok", "t_ps", "u_ps", "ut_ok", "uf_ps", "uf_ok"))
        st_ok, ks_ps, r_ok, y_ps, vn_ok, o_ps, su_ps, kd_ok, o_step = (
            sem(f"d_{x}") for x in ("state_ok", "ks_ps", "r_ok", "y_ps", "vn_ok", "o_ps", "su_ps", "kd_ok", "o_step"))
        osq, oln, oex, ot_ps, y_step, y_out = (sem(f"d_{x}") for x in ("osq", "oln", "oex", "ot_ps", "y_step", "y_out"))
        block = ctx.enter_context(nc.Block())

        jobs = [(COL_Q, SEG_ALL), (COL_K, SEG_ALL), (COL_V, SEG_ALL), (COL_Z, SEG_LAT)]
        JOBS = len(jobs)
        groups = [(j, t0, tn) for j, (_, segs) in enumerate(jobs) for t0, tn in segs]
        GROUPS = len(groups)
        w_in = weight_view(io["w_in"][0])

        def bank_free(g):
            return g - 4 + 1 + GROUPS if g >= 4 else max(x for x in range(GROUPS) if x % 4 == g) + 1

        def cols(c):
            c0 = c * P if c < CTX_CH else LAT0 + (c - CTX_CH) * P
            return slice(c0, c0 + P)

        @block.sync
        def _(e):
            with e.Fori(0, HEADS) as h:
                for j, (col, _) in enumerate(jobs):
                    e.wait_ge(w_split, h * JOBS + j + 1)
                    e.dma_start(raw[:, j % 2], w_in[:, :, bass.ds(h * P + col, P)]).then_inc(w_in_ok[j % 2], 16)

        @block.gpsimd
        def _(e):
            e.sem_inc(w_split, 2)
            e.memset(pad[:], 0.0).then_inc(pad0, 1)

            def split(h, j):
                e.wait_ge(w_in_ok[j % 2], h * 32 + 16 * (j // 2) + 16)
                e.wait_ge(mm_ok, h * GROUPS + (9, 11, 14, 17)[j])
                e.tensor_tensor(w_hi[:, j % 2], raw[:, j % 2], sh.ones[:].unsqueeze(1).broadcast_to([P, KT, P]), ALU.mult).then_inc(w_hi_ok, 1)
                e.wait_ge(w_hi_ok, h * JOBS + j + 1)
                e.tensor_tensor(w_lo[:, j % 2], raw[:, j % 2], w_hi[:, j % 2].bitcast(F32), ALU.subtract).then_inc(w_split, 1)

            def square(h, i, src):
                e.wait_ge(silu_ok, h * 3 + i + 1)
                if i:
                    e.wait_ge(nrm, h * 2 + 1)
                else:
                    e.wait_ge(y_step, h * 2 + 2)
                e.tensor_tensor(nt[:], src[:], src[:], ALU.mult).then_inc(nsq, 1)

            def inverse(h, b):
                d, blk = BATCHES[b]
                n = len(BLOCKS[blk])
                mask = lambda m: m.unsqueeze(1).broadcast_to([P, n, P])
                e.wait_ge(at_step, h * 6 + b + 1)
                e.tensor_tensor(at[:, 0:n], at[:, 0:n], mask(sh.strict[:, d]), ALU.mult).then_inc(ats_ok, 1)
                e.wait_ge(ats_ok, h * 6 + b + 1)
                e.wait_ge(uf_ps, h * 6 + b + 1)
                e.tensor_tensor(ah[:, 0:n], at[:, 0:n], mask(sh.ones[:]), ALU.mult).then_inc(ah_ok, 1)
                e.wait_ge(ah_ok, h * 6 + b + 1)
                for l in range(7):
                    if l == 2:
                        e.wait_ge(u1_ok, h * 6 + b + 1)
                    elif l > 2:
                        e.wait_ge(x_ps, h * 42 + b * 7 + l - 2)
                    e.tensor_tensor(am[:, l % 2, 0:n], ah[:, 0:n].bitcast(F32), mask(sh.level[:, d, l]), ALU.mult).then_inc(am_ok, 1)
                    if l == 1:
                        e.tensor_tensor(al[:, 0:n], at[:, 0:n], ah[:, 0:n].bitcast(F32), ALU.subtract).then_inc(al_ok, 1)

            def key_decay(h, s):
                if s >= 2:
                    e.wait_ge(su_ps, h * NCH + s - 1)
                    e.wait_ge(pad0, 1)
                for d, order in enumerate((FWD_ORDER, BWD_ORDER)):
                    c = order[s]
                    k = e.tensor_tensor(kd[:, s % 2, d], krow[:, c], sh.k_decay[:, c, bass.ds(h + d * 8, 1)].broadcast_to([P, P]),
                                        ALU.mult)
                k.then_inc(kd_ok, 1)

            with e.Fori(0, HEADS) as h:
                for j in range(JOBS):
                    split(h, j)
                square(h, 0, qt)
                square(h, 1, kt)
                for b in range(6):
                    inverse(h, b)
                for s in range(NCH):
                    key_decay(h, s)

        @block.tensor
        def _(e):
            def project(h, g):
                j, t0, tn = groups[g]
                if g == 0 or groups[g - 1][0] != j:
                    e.wait_ge(w_split, h * JOBS + j + 3)
                e.wait_ge(evac, h * GROUPS + bank_free(g))
                n = 0
                for k in range(KT):
                    for w, u in ((w_hi, sh.u_hi), (w_lo, sh.u_hi), (w_hi, sh.u_lo)):
                        mm = e.matmul(ps_d[g % 4][:, 0:tn], w[:, j % 2, k, :], u[:, k, t0:t0 + tn],
                                      start=(n == 0), stop=(n == 3 * KT - 1))
                        n += 1
                mm.then_inc(mm_ok, 1)

            def norm_sums(h, i):
                e.wait_ge(nsq, h * 2 + i + 1)
                if i:
                    e.wait_ge(nln, h * 2 + 1)
                else:
                    e.wait_ge(y_step, h * 2 + 2)
                for x0, xn in ((0, 512), (512, 512), (1024, 256)):
                    mm = e.matmul(xflat[:, x0:x0 + xn], sh.ones[:], nt[:, x0:x0 + xn], start=True, stop=True)
                mm.then_inc(nmm, 1)

            def to_rows(h, i):
                if i == 0:
                    e.wait_ge(nrm, h * 2 + 2)
                else:
                    e.wait_ge(silu_ok, h * 3 + 3)
                    e.wait_ge(row_ok, h * 2 + 1)
                for c in range(NCH):
                    src = kt[:, c * P:c * P + P] if i == 0 else cv[:, cols(c)]
                    tr = e.transpose(xflat[:, c * P:c * P + P], src, sh.ident[:])
                tr.then_inc(row_t, 1)

            def inverse(h, b):
                d, blk = BATCHES[b]
                chunks = BLOCKS[blk]
                n = len(chunks)
                t0 = chunks[0] * P
                q = lambda bank, i: ps_x[:, bank, i * P:i * P + P]
                if b == 0:
                    e.wait_ge(row_ok, h * 2 + 2)
                else:
                    e.wait_ge(uf_ok, h * 6 + b)
                e.wait_ge(sel_ok, h * 6 + b + 1)
                e.matmul(ps_x[:, 0, 0:n * P], sel[:], sh.grow[:, t0:t0 + n * P], start=True, stop=True).then_inc(rb_ok, 1)
                for bank, m in ((1, kt), (2, qt)):
                    for i, c in enumerate(chunks):
                        mm = e.matmul(q(bank, i), kt[:, c * P:c * P + P], m[:, c * P:c * P + P], start=True, stop=True)
                mm.then_inc(kk_ok, 1)
                e.wait_ge(u1_ok, h * 6 + b + 1)
                for i in range(n):
                    tr = e.transpose(q(1, i), ut[:, i].bitcast(F32), sh.ident[:])
                tr.then_inc(t1_ps, 1)
                for l in range(1, 7):
                    e.wait_ge(am_ok, h * 42 + b * 7 + l + 1)
                    e.wait_ge(tt_ok, h * 42 + b * 7 + l)
                    for i in range(n):
                        mm = e.matmul(q(3, i), am[:, l % 2, i], tt[:, i], start=True, stop=True)
                    mm.then_inc(x_ps, 1)
                    e.wait_ge(xs_ok, h * 42 + b * 7 + l)
                    if l > 1:
                        e.wait_ge(ut_ok, h * 36 + b * 6 + l - 1)
                    for i in range(n):
                        e.matmul(q(1, i), sh.ident_r[:, 0], tt[:, i], start=True, stop=False)
                        mm = e.matmul(q(1, i), ut[:, i], xs[:, i], start=False, stop=True)
                    mm.then_inc(t_ps, 1)
                    if l < 6:
                        if l == 1:
                            e.wait_ge(attn_ok, h * 6 + b + 1)
                        for i in range(n):
                            e.matmul(q(2, i), sh.ident_r[:, 0], ut[:, i], start=True, stop=False)
                            mm = e.matmul(q(2, i), xs[:, i], ut[:, i], start=False, stop=True)
                        mm.then_inc(u_ps, 1)
                e.wait_ge(tt_ok, h * 42 + b * 7 + 7)
                e.wait_ge(al_ok, h * 6 + b + 1)
                for i in range(n):
                    tr = e.transpose(q(2, i), tt[:, i].bitcast(F32), sh.ident[:])
                tr.then_inc(u_ps, 1)
                for i in range(n):
                    e.matmul(q(3, i), sh.ident_r[:, 0], sh.ident_r[:, 0], start=True, stop=False)
                    e.matmul(q(3, i), sh.ident_r[:, 1], tt[:, i], start=False, stop=False)
                    e.matmul(q(3, i), ah[:, i], tt[:, i], start=False, stop=False)
                    mm = e.matmul(q(3, i), al[:, i], tt[:, i], start=False, stop=True)
                mm.then_inc(x_ps, 1)
                e.wait_ge(xs_ok, h * 42 + b * 7 + 7)
                e.wait_ge(ut_ok, h * 36 + b * 6 + 6)
                for i in range(n):
                    e.matmul(q(1, i), sh.ident_r[:, 0], ut[:, i], start=True, stop=False)
                    mm = e.matmul(q(1, i), xs[:, i], ut[:, i], start=False, stop=True)
                mm.then_inc(uf_ps, 1)

            def scan_step(h, s):
                cs = (FWD_ORDER[s], BWD_ORDER[s])
                half = lambda bank, d: ps_x[:, bank, d * P:d * P + P]
                kc = lambda src, c: src[:, c * P:c * P + P]
                if s == 0:
                    e.wait_ge(uf_ok, h * 6 + 6)
                e.wait_ge(st_ok, h * NCH + s + 1)
                for d, c in enumerate(cs):
                    mm = e.matmul(half(0, d), kc(kt, c), st[:, d], start=True, stop=True)
                mm.then_inc(ks_ps, 1)
                if cs[0] >= CTX_CH:
                    e.wait_ge(o_step, h * 32 + max(0, s - CTX_CH) * 4 + 32)
                    for d, c in enumerate(cs):
                        e.matmul(half(2, d), kc(qt, c), st[:, d], start=True, stop=True)
                e.wait_ge(r_ok, h * NCH + s + 1)
                for d, c in enumerate(cs):
                    mm = e.matmul(half(1, d), uf[:, d, c], rr[:, d], start=True, stop=True)
                mm.then_inc(y_ps, 1)
                e.wait_ge(vn_ok, h * NCH + s + 1)
                e.wait_ge(kd_ok, h * NCH + s + 1)
                for d, c in enumerate(cs):
                    mm = e.matmul(half(3, d), kd[:, s % 2, d], vn[:, d], start=True, stop=True)
                mm.then_inc(su_ps, 1)
                if cs[0] >= CTX_CH:
                    for d, c in enumerate(cs):
                        mm = e.matmul(half(2, d + 2), att[:, d, c - CTX_CH], vn[:, d], start=True, stop=True)
                    mm.then_inc(o_ps, 1)

            with e.Fori(0, HEADS) as h:
                for g in range(9):
                    project(h, g)
                norm_sums(h, 0)
                norm_sums(h, 1)
                to_rows(h, 0)
                to_rows(h, 1)
                for g in range(9, GROUPS):
                    project(h, g)
                for b in range(6):
                    inverse(h, b)
                for s in range(NCH):
                    scan_step(h, s)
                e.wait_ge(y_step, h * 2 + 3)
                for c in range(NCH - CTX_CH):
                    tr = e.transpose(xflat[:, c * P:c * P + P], o[:, c], sh.ident[:])
                tr.then_inc(ot_ps, 1)

        @block.vector
        def _(e):
            e.sem_inc(mm_ok, GROUPS)
            e.sem_inc(y_step, 2)
            e.sem_inc(uf_ps, 1)
            e.sem_inc(o_step, 32)
            e.sem_inc(evac, GROUPS)

            def conv(h, i):
                e.wait_ge(evac, h * GROUPS + 3 * i + 3 + GROUPS)
                if i:
                    e.wait_ge(silu_ok, h * 3 + i)
                src, dst = pad, cv[:]
                w = lambda t: sh.par[:, bass.ds(h + P_DN_CONV + t * 24 + i * 8, 1)]
                e.tensor_scalar(dst, src[:, 0:CVN], w(0), None, ALU.mult).then_inc(conv_step, 1)
                for t in range(1, W_CONV):
                    e.wait_ge(conv_step, h * 9 + 3 * i + t)
                    e.scalar_tensor_tensor(out=dst, in0=src[:, t:t + CVN], scalar=w(t), in1=dst, op0=ALU.mult,
                                           op1=ALU.add).then_inc(conv_ok if t == W_CONV - 1 else conv_step, 1)

            def normalise(h, i, dst):
                e.wait_ge(nex, h * 2 + i + 1)
                e.tensor_tensor(dst[:], dst[:], nt[:], ALU.mult).then_inc(nrm, 1)

            def inverse(h, b):
                d, blk = BATCHES[b]
                chunks = BLOCKS[blk]
                n = len(chunks)
                bank = lambda i: ps_x[:, i, 0:n * P].rearrange("p (c n) -> p c n", n=P)
                e.wait_ge(rb_ok, h * 6 + b + 1)
                for i, c in enumerate(chunks):
                    x = e.scalar_tensor_tensor(out=dec[:, i], in0=bank(0)[:, i], scalar=sh.gcol[:, c, bass.ds(h + d * 8, 1)],
                                               in1=sh.off[:, d], op0=ALU.subtract, op1=ALU.min)
                x.then_inc(dd_ok, 1)
                if b < 5:
                    choose(h, b + 1)
                e.wait_ge(dec_ok, h * 6 + b + 1)
                e.wait_ge(kk_ok, h * 6 + b + 1)
                for i, c in enumerate(chunks):
                    x = e.scalar_tensor_tensor(out=at[:, i], in0=bank(1)[:, i], scalar=sh.neg_beta[:, c, bass.ds(h + d * 8, 1)],
                                               in1=dec[:, i], op0=ALU.mult, op1=ALU.mult)
                x.then_inc(at_step, 1)
                lat = [i for i, c in enumerate(chunks) if c >= CTX_CH]
                c0 = chunks[lat[0]] - CTX_CH
                e.tensor_tensor(att[:, d, c0:c0 + len(lat)], bank(2)[:, lat[0]:n], dec[:, lat[0]:n], ALU.mult).then_inc(attn_ok, 1)
                e.wait_ge(am_ok, h * 42 + b * 7 + 1)
                e.tensor_tensor(ut[:, 0:n], am[:, 0, 0:n].bitcast(F32), sh.ident[:].unsqueeze(1).broadcast_to([P, n, P]),
                                ALU.add).then_inc(u1_ok, 1)
                for l in range(1, 7):
                    e.wait_ge(t_ps, h * 36 + b * 6 + l)
                    e.tensor_copy(tt[:, 0:n], bank(1)).then_inc(tt_ok, 1)
                e.wait_ge(uf_ps, h * 6 + b + 2)
                e.tensor_copy(uf[:, d, chunks[0]:chunks[0] + n], bank(1)).then_inc(uf_ok, 1)

            def choose(h, b):
                d = BATCHES[b][0]
                if b:
                    e.wait_ge(rb_ok, h * 6 + b)
                e.tensor_scalar(sel[:], sh.ones[0:16, :], sh.ident[0:16, bass.ds(h + d * 8, 1)], None, ALU.mult).then_inc(sel_ok, 1)

            def scan_step(h, s):
                cs = (FWD_ORDER[s], BWD_ORDER[s])
                e.wait_ge(ks_ps, h * NCH + s + 1)
                for d, c in enumerate(cs):
                    x = e.scalar_tensor_tensor(out=rr[:, d], in0=ps_x[:, 0, d * P:d * P + P], scalar=sh.neg_eg[:, c, bass.ds(h + d * 8, 1)],
                                               in1=vrow[:, c], op0=ALU.mult, op1=ALU.add)
                x.then_inc(r_ok, 1)
                if s < NCH - 1:
                    e.wait_ge(su_ps, h * NCH + s + 1)
                    for d, c in enumerate(cs):
                        x = e.scalar_tensor_tensor(out=st[:, d], in0=st[:, d], scalar=sh.eg_tot[:, c, bass.ds(h + d * 8, 1)],
                                                   in1=ps_x[:, 3, d * P:d * P + P], op0=ALU.mult, op1=ALU.add)
                    x.then_inc(st_ok, 1)
                if cs[0] >= CTX_CH:
                    e.wait_ge(o_ps, h * 8 + s - CTX_CH + 1)
                    o0 = h * 32 + (s - CTX_CH) * 4 + 32
                    e.wait_ge(o_step, o0)
                    for d, c in enumerate(cs):
                        oc = o[:, c - CTX_CH]
                        g = sh.eg[:, c, bass.ds(h + d * 8, 1)]
                        first = c < 6 if d == 0 else c >= 6
                        if first:
                            e.tensor_scalar(oc, ps_x[:, 2, d * P:d * P + P], g, None, ALU.mult).then_inc(o_step, 1)
                        else:
                            e.scalar_tensor_tensor(out=oc, in0=ps_x[:, 2, d * P:d * P + P], scalar=g, in1=oc,
                                                   op0=ALU.mult, op1=ALU.add).then_inc(o_step, 1)
                    for d, c in enumerate(cs):
                        oc = o[:, c - CTX_CH]
                        e.wait_ge(o_step, o0 + 1 + d)
                        e.tensor_tensor(oc, oc, ps_x[:, 2, (d + 2) * P:(d + 3) * P], ALU.add).then_inc(o_step, 1)

            with e.Fori(0, HEADS) as h:
                e.memset(st[:], 0.0).then_inc(st_ok, 1)
                choose(h, 0)
                for i in range(3):
                    conv(h, i)
                normalise(h, 0, qt)
                normalise(h, 1, kt)
                for b in range(6):
                    inverse(h, b)
                for s in range(NCH):
                    scan_step(h, s)
                e.wait_ge(o_step, h * 32 + 64)
                sqv = nt[:, 0:SEQ].rearrange("p (c n) -> p c n", n=P)
                e.tensor_tensor(sqv, o[:], o[:], ALU.mult).then_inc(osq, 1)
                e.wait_ge(osq, h * 2 + 1)
                e.tensor_reduce(oss[:], sqv, AX_X, ALU.add).then_inc(osq, 1)
                e.wait_ge(oex, h + 1)
                e.tensor_tensor(o[:], o[:], ors[:].unsqueeze(2).broadcast_to([P, NCH - CTX_CH, P]), ALU.mult).then_inc(y_step, 1)
                e.wait_ge(ot_ps, h + 1)
                e.scalar_tensor_tensor(out=nt[:, 0:SEQ], in0=xflat[:, 0:SEQ], scalar=sh.par[:, P_ONORM:P_ONORM + 1],
                                       in1=cv[:, 0:SEQ], op0=ALU.mult, op1=ALU.mult).then_inc(y_step, 1)

        @block.scalar
        def _(e):
            e.wait_ge(pad0, 1)

            def evacuate(h, g):
                j, t0, tn = groups[g]
                e.wait_ge(mm_ok, h * GROUPS + g + 1 + GROUPS)
                if j == 3:
                    e.activation(cv[:, t0 - N_CTX:t0 - N_CTX + tn], ps_d[g % 4][:, 0:tn], ACT.Silu).then_inc(evac, 1)
                    return
                c0 = t0 + PAD_LEFT if t0 < N_CTX else t0 + PAD_LEFT + 3
                e.activation(pad[:, c0:c0 + tn], ps_d[g % 4][:, 0:tn], ACT.Copy).then_inc(evac, 1)

            def silu(h, i):
                e.wait_ge(conv_ok, h * 3 + i + 1)
                line = cv
                for a, t0, n in ((0, 0, N_CTX), (LAT0, N_CTX, SEQ)):
                    dst = (qt[:, t0:t0 + n], kt[:, t0:t0 + n], line[:, a:a + n])[i]
                    x = e.activation(dst, line[:, a:a + n], ACT.Silu)
                x.then_inc(silu_ok, 1)

            def inverse_norm(h, i):
                e.wait_ge(nmm, h * 2 + i + 1)
                scale, bias = ((float(P), sh.eps[:, 1:2]), (1.0, sh.eps[:, 0:1]))[i]
                e.activation(nt[:], xflat[:, 0:T], ACT.Ln, bias=bias, scale=scale).then_inc(nln, 1)
                e.wait_ge(nln, h * 2 + i + 1)
                e.activation(nt[:], nt[:], ACT.Exp, scale=-0.5).then_inc(nex, 1)

            def rows(h, i):
                e.wait_ge(row_t, h * 2 + i + 1)
                dst = (krow, vrow)[i]
                e.activation(dst[:].rearrange("p c n -> p (c n)"), xflat[:, 0:T], ACT.Copy).then_inc(row_ok, 1)

            def inverse(h, b):
                n = len(BLOCKS[BATCHES[b][1]])
                bank = lambda i: ps_x[:, i, 0:n * P].rearrange("p (c n) -> p c n", n=P)
                e.wait_ge(dd_ok, h * 6 + b + 1)
                e.activation(dec[:, 0:n], dec[:, 0:n], ACT.Exp).then_inc(dec_ok, 1)
                e.wait_ge(t1_ps, h * 6 + b + 1)
                e.activation(tt[:, 0:n], bank(1), ACT.Copy).then_inc(tt_ok, 1)
                for l in range(1, 7):
                    e.wait_ge(x_ps, h * 42 + b * 7 + l)
                    e.activation(xs[:, 0:n], bank(3), ACT.Copy).then_inc(xs_ok, 1)
                    if l < 6:
                        e.wait_ge(u_ps, h * 36 + b * 6 + l)
                        e.activation(ut[:, 0:n], bank(2), ACT.Copy).then_inc(ut_ok, 1)
                e.wait_ge(u_ps, h * 36 + b * 6 + 6)
                e.activation(ut[:, 0:n], bank(2), ACT.Copy).then_inc(ut_ok, 1)
                e.wait_ge(x_ps, h * 42 + b * 7 + 7)
                e.activation(xs[:, 0:n], bank(3), ACT.Copy).then_inc(xs_ok, 1)

            def scan_step(h, s):
                cs = (FWD_ORDER[s], BWD_ORDER[s])
                e.wait_ge(y_ps, h * NCH + s + 1)
                for d, c in enumerate(cs):
                    x = e.activation(vn[:, d], ps_x[:, 1, d * P:d * P + P], ACT.Copy, scale=sh.beta[:, c, bass.ds(h + d * 8, 1)])
                x.then_inc(vn_ok, 1)

            with e.Fori(0, HEADS) as h:
                for i in range(3):
                    for g in range(3 * i, 3 * i + 3):
                        evacuate(h, g)
                    silu(h, i)
                inverse_norm(h, 0)
                inverse_norm(h, 1)
                rows(h, 0)
                rows(h, 1)
                for g in range(9, GROUPS):
                    evacuate(h, g)
                for b in range(6):
                    inverse(h, b)
                for s in range(NCH):
                    scan_step(h, s)
                e.wait_ge(osq, h * 2 + 2)
                e.activation(ors[:], oss[:], ACT.Ln, bias=sh.eps[:, 0:1], scale=1.0 / P).then_inc(oln, 1)
                e.wait_ge(oln, h + 1)
                e.activation(ors[:], ors[:], ACT.Exp, scale=-0.5).then_inc(oex, 1)
                e.wait_ge(y_step, h * 2 + 4)
                e.dma_start(sh.y_dn[bass.ds(h, 1)].rearrange("o p n -> (o p) n"), nt[:, 0:SEQ]).then_inc(y_out, 16)
                e.wait_ge(y_out, h * 16 + 16)



def rg_lru(nc, sh, io):
    with ExitStack() as ctx:
        sb = lambda n, s, d=F32: ctx.enter_context(nc.sbuf_tensor(n, s, d))
        sem = sh.sem
        PADN = N_CTX + SEQ + 6
        raw = sb("l_raw", [P, 2, KT, P])
        w_hi = sb("l_w_hi", [P, 2, KT, P], F32R)
        w_lo = sb("l_w_lo", [P, 2, KT, P], F32R)
        wg = sb("l_wg", [P, 4, P])
        pad = sb("l_pad", [P, PADN])
        xc = sb("l_xc", [P, T])
        r = sb("l_r", [P, 2, T])
        ig = sb("l_i", [P, 2, T])
        a = sb("l_a", [P, 2, T])
        q = sb("l_q", [P, 2, T])
        gy = sb("l_gy", [P, SEQ])
        gm = sb("l_gm", [P, 2, SEQ])
        y = sb("l_y", [P, SEQ])
        lam = sb("l_lam", [P, 6, 16])
        cols = sb("l_cols", [P, 10])
        ps_d = [ctx.enter_context(nc.psum_tensor(f"l_ps_d{i}", [P, 512], F32)) for i in range(3)]
        ps_g = [ctx.enter_context(nc.psum_tensor(f"l_ps_g{i}", [P, 512], F32)) for i in range(4)]
        w_in_ok = [sem(f"l_w_in{i}") for i in range(2)]
        w_hi_ok, w_split, mm_ok, evac = sem("l_w_hi_ok"), sem("l_w_split"), sem("l_mm_ok"), sem("l_evac")
        cols_ok = sem("l_cols_ok")
        zero, wg_in, gate_ps, gate_ok = sem("l_zero"), sem("l_wg_in"), sem("l_gate_ps"), sem("l_gate_ok")
        conv_step, xc_ok, lam_v, lam_s = sem("l_conv_step"), sem("l_xc_ok"), sem("l_lam_v"), sem("l_lam_s")
        a_ok, th_ok, a2_ok, m_ok, sq_ok, ix_ok, in_ok, h_ok, y_step, y_out, g_out = (
            sem(f"l_{x}") for x in ("a_ok", "tanh_ok", "a2_ok", "m_ok", "sqrt_ok", "ix_ok", "inp_ok", "h_ok", "y_step",
                                    "y_out", "g_done"))
        g_out = [sem(f"l_g_out{i}") for i in range(2)]
        block = ctx.enter_context(nc.Block())

        jobs = [(COL_XL, SEG_ALL), (COL_YL, SEG_LAT), (COL_MG, SEG_LAT), (COL_MG + D, SEG_LAT)]
        groups = [(j, t0, tn) for j, (_, segs) in enumerate(jobs) for t0, tn in segs]
        JOBS, GROUPS, GATES = len(jobs), len(groups), 12
        w_in = weight_view(io["w_in"][0])

        @block.sync
        def _(e):
            e.wait_ge(zero, 2)
            with e.Fori(0, KT) as m:
                for j, (col, _) in enumerate(jobs):
                    e.wait_ge(w_split, m * JOBS + j + 1)
                    e.dma_start(raw[:, j % 2], w_in[:, :, bass.ds(m * P + col, P)]).then_inc(w_in_ok[j % 2], 16)
                    if j == 0:
                        e.wait_ge(gate_ps, m * GATES + GATES)
                        for g, name in enumerate(("lru_w_rg", "lru_w_ig")):
                            for b in range(2):
                                src = io[name][0][:, bass.ds(m * 2 + b, 1)].rearrange("d o i j -> (o i) d j")
                                e.dma_start(wg[64 * b:64 * b + 64, 2 * g:2 * g + 2, 64 * b:64 * b + 64], src).then_inc(wg_in, 16)

        @block.gpsimd
        def _(e):
            e.memset(wg[:], 0.0).then_inc(zero, 1)
            e.memset(pad[:], 0.0).then_inc(zero, 1)
            e.sem_inc(w_split, 2)

            def split(m, j):
                e.wait_ge(w_in_ok[j % 2], m * 32 + 16 * (j // 2) + 16)
                e.wait_ge(mm_ok, m * GROUPS + (7, 9, 12, 14)[j])
                e.tensor_tensor(w_hi[:, j % 2], raw[:, j % 2], sh.ones[:].unsqueeze(1).broadcast_to([P, KT, P]),
                                ALU.mult).then_inc(w_hi_ok, 1)
                e.wait_ge(w_hi_ok, m * JOBS + j + 1)
                e.tensor_tensor(w_lo[:, j % 2], raw[:, j % 2], w_hi[:, j % 2].bitcast(F32), ALU.subtract).then_inc(w_split, 1)

            def products(m):
                for d in range(2):
                    e.wait_ge(a_ok, m * 2 + d + 1)
                    e.wait_ge(in_ok, m * 2 + d + 1)
                    e.tensor_tensor(q[:, d], a[:, d], a[:, d], ALU.mult).then_inc(a2_ok, 1)
                    e.tensor_tensor(ig[:, d], ig[:, d], xc[:], ALU.mult).then_inc(ix_ok, 1)

            with e.Fori(0, KT) as m:
                for j in range(JOBS):
                    split(m, j)
                products(m)

        @block.tensor
        def _(e):
            def project(m, g):
                j, t0, tn = groups[g]
                if g == 0 or groups[g - 1][0] != j:
                    e.wait_ge(w_split, m * JOBS + j + 3)
                e.wait_ge(evac, m * GROUPS + g + 7)
                n = 0
                for k in range(KT):
                    for w, u in ((w_hi, sh.u_hi), (w_lo, sh.u_hi), (w_hi, sh.u_lo)):
                        mm = e.matmul(ps_d[g % 3][:, 0:tn], w[:, j % 2, k, :], u[:, k, t0:t0 + tn],
                                      start=(n == 0), stop=(n == 3 * KT - 1))
                        n += 1
                mm.then_inc(mm_ok, 1)

            with e.Fori(0, KT) as m:
                for g in range(7):
                    project(m, g)
                e.wait_ge(wg_in, m * 64 + 64)
                e.wait_ge(xc_ok, m * 2 + 2)
                n = 0
                for g in range(4):
                    for t0, tn in SEG_ALL:
                        e.wait_ge(gate_ok, m * GATES + n + 9)
                        e.matmul(ps_g[n % 4][:, 0:tn], wg[:, g], xc[:, t0:t0 + tn], start=True, stop=True).then_inc(gate_ps, 1)
                        n += 1
                for g in range(7, GROUPS):
                    project(m, g)

        @block.vector
        def _(e):
            e.sem_inc(mm_ok, GROUPS)
            e.sem_inc(evac, GROUPS)
            e.sem_inc(gate_ps, GATES)
            e.sem_inc(gate_ok, GATES)
            e.sem_inc(in_ok, 2)
            e.tensor_scalar(lam[:, 0], sh.par[:, P_LAM:P_LAM + 16], -1.0, None, ALU.mult).then_inc(lam_v, 1)
            e.wait_ge(lam_s, 2)
            e.tensor_scalar(lam[:, 2], lam[:, 1], 1.0, None, ALU.add).then_inc(lam_v, 1)
            e.wait_ge(lam_v, 2)
            e.reciprocal(lam[:, 4], lam[:, 2]).then_inc(lam_v, 1)
            e.scalar_tensor_tensor(out=lam[:, 1], in0=lam[:, 2], scalar=-1.0, in1=lam[:, 1], op0=ALU.add,
                                   op1=ALU.subtract).then_inc(lam_v, 1)
            e.wait_ge(lam_v, 4)
            e.scalar_tensor_tensor(out=lam[:, 1], in0=lam[:, 1], scalar=-1.0, in1=lam[:, 4], op0=ALU.mult,
                                   op1=ALU.mult).then_inc(lam_v, 1)
            e.wait_ge(lam_v, 5)
            e.wait_ge(lam_s, 3)
            e.tensor_tensor(lam[:, 3], lam[:, 3], lam[:, 1], ALU.add).then_inc(lam_v, 1)
            e.wait_ge(lam_v, 6)
            e.scalar_tensor_tensor(out=lam[:, 0], in0=lam[:, 0], scalar=0.0, in1=lam[:, 3], op0=ALU.max,
                                   op1=ALU.add).then_inc(lam_v, 1)
            e.wait_ge(lam_v, 7)
            e.tensor_scalar(lam[:, 4], lam[:, 0], LRU_C, None, ALU.mult).then_inc(lam_v, 1)
            e.tensor_scalar(lam[:, 5], lam[:, 0], -LRU_C, None, ALU.mult).then_inc(lam_v, 1)

            def conv(m):
                e.wait_ge(evac, m * GROUPS + 3 + GROUPS)
                w = lambda t: sh.par[:, bass.ds(m + P_LRU_CONV + t * KT, 1)]
                b = sh.par[:, bass.ds(m + P_LRU_CONV_B, 1)]
                for i, (c0, t0, tn) in enumerate(((0, 0, N_CTX), (N_CTX + 3, N_CTX, SEQ))):
                    x = xc[:, t0:t0 + tn]
                    e.tensor_scalar(x, pad[:, c0:c0 + tn], w(0), b, ALU.mult, ALU.add).then_inc(conv_step, 1)
                    for t in range(1, W_CONV):
                        e.wait_ge(conv_step, m * 6 + 3 * i + t)
                        e.scalar_tensor_tensor(out=x, in0=pad[:, c0 + t:c0 + t + tn], scalar=w(t), in1=x, op0=ALU.mult,
                                               op1=ALU.add).then_inc(xc_ok if t == W_CONV - 1 else conv_step, 1)

            def scans(m):
                for d in range(2):
                    e.wait_ge(a2_ok, m * 2 + d + 1)
                    e.wait_ge(th_ok, m * 2 + d + 1)
                    e.scalar_tensor_tensor(out=q[:, d], in0=q[:, d], scalar=1.0, in1=r[:, d], op0=ALU.add,
                                           op1=ALU.mult).then_inc(m_ok, 1)
                for d in range(2):
                    e.wait_ge(sq_ok, m * 2 + d + 1)
                    e.wait_ge(ix_ok, m * 2 + d + 1)
                    e.tensor_tensor(ig[:, d], ig[:, d], q[:, d], ALU.mult).then_inc(in_ok, 1)
                    e.wait_ge(in_ok, m * 2 + d + 3)
                    if d == 0:
                        e.tensor_tensor_scan(r[:, 0], a[:, 0], ig[:, 0], 0.0, ALU.mult, ALU.add).then_inc(h_ok, 1)
                    else:
                        back = lambda x, lo, hi: x[:, 1, hi - 1:(lo - 1 if lo else None):-1]
                        e.tensor_tensor_scan(back(r, 0, N_CTX), back(a, 0, N_CTX), back(ig, 0, N_CTX), 0.0, ALU.mult,
                                             ALU.add).then_inc(h_ok, 1)
                        e.wait_ge(h_ok, m * 3 + 2)
                        e.tensor_tensor_scan(back(r, N_CTX, T), back(a, N_CTX, T), back(ig, N_CTX, T), r[:, 1, 0:1],
                                             ALU.mult, ALU.add).then_inc(h_ok, 1)
                e.wait_ge(h_ok, m * 3 + 3)
                e.wait_ge(y_out, m * 16 + 16)
                e.tensor_tensor(y[:], r[:, 0, N_CTX:T], r[:, 1, N_CTX:T], ALU.add).then_inc(y_step, 1)
                e.wait_ge(y_step, m * 2 + 1)
                e.tensor_tensor(y[:], y[:], gy[:], ALU.mult).then_inc(y_step, 1)

            e.sem_inc(y_out, 16)
            with e.Fori(0, KT) as m:
                conv(m)
                scans(m)

        @block.scalar
        def _(e):
            e.wait_ge(lam_v, 1)
            e.activation(lam[:, 1], lam[:, 0], ACT.Abs).then_inc(lam_s, 1)
            e.wait_ge(lam_s, 1)
            e.activation(lam[:, 1], lam[:, 1], ACT.Exp, scale=-1.0).then_inc(lam_s, 1)
            e.wait_ge(lam_v, 2)
            e.activation(lam[:, 3], lam[:, 2], ACT.Ln).then_inc(lam_s, 1)
            e.wait_ge(lam_v, 9)
            e.wait_ge(zero, 2)
            for i in range(2):
                e.sem_inc(g_out[i], 16)

            def evacuate(m, g):
                j, t0, tn = groups[g]
                e.wait_ge(mm_ok, m * GROUPS + g + 1 + GROUPS)
                src = ps_d[g % 3][:, 0:tn]
                if j == 0:
                    c0 = t0 + PAD_LEFT if t0 < N_CTX else t0 + PAD_LEFT + 3
                    e.activation(pad[:, c0:c0 + tn], src, ACT.Copy).then_inc(evac, 1)
                elif j == 1:
                    e.activation(gy[:, t0 - N_CTX:t0 - N_CTX + tn], src, ACT.Gelu_apprx_tanh).then_inc(evac, 1)
                else:
                    if t0 == N_CTX:
                        e.wait_ge(g_out[j - 2], m * 16 + 16)
                    e.activation(gm[:, j - 2, t0 - N_CTX:t0 - N_CTX + tn], src, ACT.Sigmoid,
                                 bias=cols[:, 2 + j:3 + j]).then_inc(evac, 1)

            of_tile = lambda x, lo, hi: x[:, lo:hi].rearrange("p (g m) -> p g m", m=KT)
            rows = lam[:].rearrange("p r n -> p (r n)")
            with e.Fori(0, KT) as m:
                for c0, src in ((0, of_tile(sh.par, P_B_RG, P_B_RG + 32)), (4, of_tile(sh.par, P_B_MERGE, P_B_MERGE + 16)),
                                (6, of_tile(rows, 64, 96))):
                    src = src[:, :, bass.ds(m, 1)]
                    e.activation(cols[:, c0:c0 + src.shape[1]].unsqueeze(2), src, ACT.Copy).then_inc(cols_ok, 1)
                e.wait_ge(cols_ok, m * 3 + 3)
                for g in range(3):
                    evacuate(m, g)
                for g in range(3, 5):
                    evacuate(m, g)
                for g in range(5, 7):
                    evacuate(m, g)
                e.wait_ge(evac, m * GROUPS + 7 + GROUPS)
                e.dma_start(sh.gates[bass.ds(m, 1)].rearrange("o p n -> (o p) n"), gm[:, 0]).then_inc(g_out[0], 16)
                n = 0
                for g, dst in enumerate((r, r, ig, ig)):
                    d = g % 2
                    for t0, tn in SEG_ALL:
                        e.wait_ge(gate_ps, m * GATES + n + 1 + GATES)
                        e.activation(dst[:, d, t0:t0 + tn], ps_g[n % 4][:, 0:tn], ACT.Sigmoid,
                                     bias=cols[:, g:g + 1]).then_inc(gate_ok, 1)
                        n += 1
                for d in range(2):
                    e.wait_ge(gate_ok, m * GATES + GATES + 12)
                    e.activation(a[:, d], r[:, d], ACT.Exp, scale=cols[:, 8 + d:9 + d]).then_inc(a_ok, 1)
                    e.activation(r[:, d], r[:, d], ACT.Tanh, scale=cols[:, 6 + d:7 + d]).then_inc(th_ok, 1)
                for d in range(2):
                    e.wait_ge(m_ok, m * 2 + d + 1)
                    e.activation(q[:, d], q[:, d], ACT.Sqrt).then_inc(sq_ok, 1)
                for g in range(7, GROUPS):
                    evacuate(m, g)
                e.wait_ge(evac, m * GROUPS + GROUPS + GROUPS)
                e.dma_start(sh.gates[bass.ds(m + KT, 1)].rearrange("o p n -> (o p) n"), gm[:, 1]).then_inc(g_out[1], 16)
                e.wait_ge(y_step, m * 2 + 2)
                e.dma_start(sh.y_lru[bass.ds(m, 1)].rearrange("o p n -> (o p) n"), y[:]).then_inc(y_out, 16)
            e.wait_ge(y_out, 16 + 16 * KT)
            for i in range(2):
                e.wait_ge(g_out[i], 16 + 16 * KT)


class WeightStream:

    def __init__(self, nc, sh, ctx, tag, slots):
        sb = lambda n, d: ctx.enter_context(nc.sbuf_tensor(f"{tag}_{n}", [P, slots, KT, P], d))
        self.raw, self.hi, self.lo = sb("raw", F32), sb("w_hi", F32R), sb("w_lo", F32R)
        self.loaded = [sh.sem(f"{tag}_w_loaded{i}") for i in range(slots)]
        self.hi_ok = [sh.sem(f"{tag}_w_hi_ok{i}") for i in range(slots)]
        self.split = [sh.sem(f"{tag}_w_split{i}") for i in range(slots)]

    def split_job(self, e, ones, slot, earlier, credit=0):
        e.wait_ge(self.loaded[slot], earlier * 16 + 16)
        e.tensor_tensor(self.hi[:, slot], self.raw[:, slot], ones.unsqueeze(1).broadcast_to([P, KT, P]),
                        ALU.mult).then_inc(self.hi_ok[slot], 1)
        e.wait_ge(self.hi_ok[slot], earlier + 1)
        e.tensor_tensor(self.lo[:, slot], self.raw[:, slot], self.hi[:, slot].bitcast(F32),
                        ALU.subtract).then_inc(self.split[slot], 1)


def merge(nc, sh, io):
    with ExitStack() as ctx:
        sb = lambda n, s, d=F32: ctx.enter_context(nc.sbuf_tensor(n, s, d))
        sem = sh.sem
        w = WeightStream(nc, sh, ctx, "m", 2)
        stage = sb("m_stage", [P, 2, SEQ])
        gate = sb("m_gate", [P, 2, SEQ])
        tmp = sb("m_tmp", [P, 2, 512])
        sq = sb("m_sq", [P, SEQ])
        sacc = sb("m_sacc", [P, SEQ])
        rs = sb("m_rs", [P, SEQ])
        tok = sb("m_tok", [P, KT, D])
        ps = [ctx.enter_context(nc.psum_tensor(f"m_ps{i}", [P, 512], F32)) for i in range(4)]
        ps_s = ctx.enter_context(nc.psum_tensor("m_ps_s", [P, 2, 512], F32))
        ps_t = [ctx.enter_context(nc.psum_tensor(f"m_ps_t{i}", [P, 512], F32)) for i in range(2)]
        y_in = [sem(f"m_y_in{i}") for i in range(2)]
        g_in = [sem(f"m_g_in{i}") for i in range(2)]
        tok_in, v_hi_ok, v_lo_ok, mm_ok, evac, part, gates_used = (
            sem(f"m_{x}") for x in ("tok_in", "v_hi_ok", "v_lo_ok", "mm_ok", "evac", "part", "gates_used"))
        sq_ok, sacc_ok, sum_ps, ln_ok, rs_ok, xt_ps, t_ok, h_ok, ut_ok = (
            sem(f"m_{x}") for x in ("sq_ok", "sacc_ok", "sum_ps", "ln_ok", "rs_ok", "xt_ps", "t_ok", "h_ok", "ut_ok"))
        block = ctx.enter_context(nc.Block())
        weights = [weight_view(io[n][0]) for n in ("w_branch_dn", "w_branch_lru", "w_out")]
        h2 = sh.h2

        @block.sync
        def _(e):
            for b in range(3):
                if b < 2:
                    for k in range(KT):
                        n = b * KT + k
                        if n >= 2:
                            e.wait_ge(v_lo_ok, n - 1)
                        e.dma_start(stage[:, k % 2], (sh.y_dn, sh.y_lru)[b][k]).then_inc(y_in[k % 2], 16)
                with e.Fori(0, KT // 2) as i:
                    for s in range(2):
                        e.wait_ge(w.split[s], i + b * KT // 2 + 1)
                        e.dma_start(w.raw[:, s], weights[b][:, :, bass.ds(i * 2 * P + s * P, P)]).then_inc(w.loaded[s], 16)
                        if b < 2:
                            e.wait_ge(gates_used, i * 2 + b * KT + s + 1)
                            e.dma_start(gate[:, s], sh.gates[bass.ds(i * 2 + b * KT + s, 1)].rearrange("o p n -> (o p) n")).then_inc(g_in[s], 16)

        @block.gpsimd
        def _(e):
            for s in range(2):
                e.sem_inc(w.split[s], 1)
            e.sem_inc(gates_used, 2)
            e.sem_inc(evac, 4)
            e.sem_inc(mm_ok, 4)
            for b in range(3):
                with e.Fori(0, KT // 2) as i:
                    for s in range(2):
                        e.wait_ge(mm_ok, i * 4 + b * 16 + 2 * s + 2)
                        w.split_job(e, sh.ones[:], s, i + b * KT // 2)

        @block.tensor
        def _(e):
            for b in range(3):
                e.wait_ge(v_lo_ok, (b + 1) * KT)
                with e.Fori(0, KT // 2) as i:
                    for s in range(2):
                        e.wait_ge(w.split[s], i + b * KT // 2 + 2)
                        for t in range(2):
                            g = 2 * s + t
                            e.wait_ge(evac, i * 4 + b * 16 + g + 1)
                            n = 0
                            for k in range(KT):
                                for wt, v in ((w.hi, sh.v_hi), (w.lo, sh.v_hi), (w.hi, sh.v_lo)):
                                    mm = e.matmul(ps[g][:], wt[:, s, k], v[:, k, t * 512:t * 512 + 512],
                                                  start=(n == 0), stop=(n == 3 * KT - 1))
                                    n += 1
                            mm.then_inc(mm_ok, 1)
            for r in range(2):
                e.wait_ge(sacc_ok, (r + 1) * KT)
                if r:
                    e.wait_ge(ln_ok, 1)
                for t in range(2):
                    mm = e.matmul(ps_s[:, t], sh.ones[:], sacc[:, t * 512:t * 512 + 512], start=True, stop=True)
                mm.then_inc(sum_ps, 1)
                if r == 0:
                    e.wait_ge(tok_in, 16)
                    for k in range(KT):
                        for t in range(2):
                            n = 2 * k + t
                            if n >= 2:
                                e.wait_ge(h_ok, n - 1)
                            for j in range(4):
                                tr = e.transpose(ps_t[t][:, j * P:j * P + P], tok[:, 4 * t + j, k * P:k * P + P], sh.ident[:])
                            tr.then_inc(xt_ps, 1)

        @block.vector
        def _(e):
            def split_lo(n, src):
                e.wait_ge(v_hi_ok, n + 1)
                k = n % KT
                e.tensor_tensor(sh.v_lo[:, k], src, sh.v_hi[:, k].bitcast(F32), ALU.subtract).then_inc(v_lo_ok, 1)

            for b in range(2):
                for k in range(KT):
                    split_lo(b * KT + k, stage[:, k % 2])
                with e.Fori(0, KT // 2) as i:
                    for s in range(2):
                        e.wait_ge(g_in[s], i * 16 + b * 64 + 16)
                        for t in range(2):
                            g = 2 * s + t
                            e.wait_ge(mm_ok, i * 4 + b * 16 + g + 1 + 4)
                            dst = h2[:, bass.ds(i * 2 + s, 1), t * 512:t * 512 + 512].rearrange("p o n -> p (o n)")
                            gt = gate[:, s, t * 512:t * 512 + 512]
                            if b == 0:
                                e.tensor_tensor(dst, ps[g][:], gt, ALU.mult).then_inc(evac, 1)
                            else:
                                e.tensor_tensor(tmp[:, t], ps[g][:], gt, ALU.mult).then_inc(evac, 1)
                                e.wait_ge(evac, i * 4 + 16 + g + 1 + 4)
                                e.tensor_tensor(dst, dst, tmp[:, t], ALU.add).then_inc(part, 1)
                        if b == 0:
                            e.wait_ge(evac, i * 4 + 2 * s + 2 + 4)
                        else:
                            e.wait_ge(part, i * 4 + 2 * s + 2)
                        e.sem_inc(gates_used, 1)
            for k in range(KT):
                split_lo(2 * KT + k, h2[:, k])
            for k in range(KT):
                e.wait_ge(sq_ok, k + 1)
                if k:
                    e.wait_ge(sacc_ok, k)
                    e.tensor_tensor(sacc[:], sacc[:], sq[:], ALU.add).then_inc(sacc_ok, 1)
                else:
                    e.tensor_copy(sacc[:], sq[:]).then_inc(sacc_ok, 1)
            e.wait_ge(rs_ok, 1)
            for k in range(KT):
                e.scalar_tensor_tensor(out=h2[:, k], in0=h2[:, k], scalar=sh.post_mix[:, k:k + 1], in1=rs[:],
                                       op0=ALU.mult, op1=ALU.mult).then_inc(t_ok, 1)
                e.wait_ge(t_ok, k + 1)
                for t in range(2):
                    e.wait_ge(xt_ps, 2 * k + t + 1)
                    e.tensor_tensor(h2[:, k, t * 512:t * 512 + 512], h2[:, k, t * 512:t * 512 + 512], ps_t[t][:], ALU.add).then_inc(h_ok, 1)
                e.wait_ge(sq_ok, KT + k + 1)
                if k:
                    e.wait_ge(sacc_ok, KT + k)
                    e.tensor_tensor(sacc[:], sacc[:], sq[:], ALU.add).then_inc(sacc_ok, 1)
                else:
                    e.wait_ge(sum_ps, 1)
                    e.tensor_copy(sacc[:], sq[:]).then_inc(sacc_ok, 1)
            e.wait_ge(rs_ok, 2)
            for k in range(KT):
                e.wait_ge(h_ok, 2 * KT)
                if k >= 2:
                    e.wait_ge(v_lo_ok, 3 * KT + k - 1)
                e.scalar_tensor_tensor(out=stage[:, k % 2], in0=h2[:, k], scalar=sh.pre_ffn[:, k:k + 1], in1=rs[:],
                                       op0=ALU.mult, op1=ALU.mult).then_inc(t_ok, 1)
                if k:
                    split_lo(3 * KT + k - 1, stage[:, (k - 1) % 2])
            split_lo(4 * KT - 1, stage[:, 1])

        @block.scalar
        def _(e):
            e.dma_start(tok[:], io["x"][0].rearrange("(t p) d -> p t d", p=P)).then_inc(tok_in, 16)
            for b in range(2):
                for k in range(KT):
                    e.wait_ge(y_in[k % 2], 16 * (k // 2) + 64 * b + 16)
                    if b:
                        e.wait_ge(mm_ok, 20)
                    e.activation(sh.v_hi[:, k], stage[:, k % 2], ACT.Copy).then_inc(v_hi_ok, 1)
            e.wait_ge(part, 16)
            e.wait_ge(mm_ok, 36)
            for k in range(KT):
                e.activation(sh.v_hi[:, k], h2[:, k], ACT.Copy).then_inc(v_hi_ok, 1)
            for i in range(KT):
                for t in range(2):
                    g = 2 * (i % 2) + t
                    e.wait_ge(mm_ok, 36 + 2 * i + t + 1)
                    if t == 0:
                        e.wait_ge(v_lo_ok, 2 * KT + i + 1)
                    e.activation(h2[:, i, t * 512:t * 512 + 512], ps[g][:], ACT.Copy).then_inc(evac, 1)
                e.wait_ge(evac, 32 + 2 * i + 2 + 4)
                if i:
                    e.wait_ge(sacc_ok, i)
                e.activation(sq[:], h2[:, i], ACT.Square).then_inc(sq_ok, 1)
            for r in range(2):
                e.wait_ge(sum_ps, r + 1)
                if r:
                    e.wait_ge(h_ok, 2 * KT)
                    e.wait_ge(t_ok, KT)
                e.activation(rs[:], ps_s[:].rearrange("p t n -> p (t n)"), ACT.Ln, bias=sh.eps[:, 0:1], scale=1.0 / D).then_inc(ln_ok, 1)
                e.wait_ge(ln_ok, r + 1)
                e.activation(rs[:], rs[:], ACT.Exp, scale=-0.5).then_inc(rs_ok, 1)
                if r == 0:
                    for k in range(KT):
                        e.wait_ge(h_ok, 2 * k + 2)
                        e.wait_ge(sacc_ok, KT + k)
                        e.activation(sq[:], h2[:, k], ACT.Square).then_inc(sq_ok, 1)
            for k in range(KT):
                e.wait_ge(t_ok, KT + k + 1)
                e.activation(stage[:, k % 2], stage[:, k % 2], ACT.Identity, bias=sh.m[:, 3 * KT + k, 0:1]).then_inc(ut_ok, 1)
                e.wait_ge(ut_ok, k + 1)
                e.activation(sh.v_hi[:, k], stage[:, k % 2], ACT.Copy).then_inc(v_hi_ok, 1)


def conv_ffn(nc, sh, io, out):
    with ExitStack() as ctx:
        sb = lambda n, s, d=F32: ctx.enter_context(nc.sbuf_tensor(n, s, d))
        sem = sh.sem
        w = WeightStream(nc, sh, ctx, "f", 3)
        img = sb("f_img", [P, ROWS + 2, GRID_W + 2])
        cacc = sb("f_cacc", [P, ROWS, GRID_W])
        ge = sb("f_ge", [P, SEQ])
        f = sb("f_f", [P, SEQ])
        f_hi = sb("f_hi", [P, 2, SEQ], F32R)
        f_lo = sb("f_lo", [P, 2, SEQ], F32R)
        acc = sb("f_acc", [P, KT, SEQ])
        rs = img[:].rearrange("p a b -> p (a b)")[:, 0:SEQ]
        ps_g = [ctx.enter_context(nc.psum_tensor(f"f_ps_g{i}", [P, 512], F32)) for i in range(2)]
        ps_v = [ctx.enter_context(nc.psum_tensor(f"f_ps_v{i}", [P, 512], F32)) for i in range(2)]
        ps_d = [ctx.enter_context(nc.psum_tensor(f"f_ps_d{i}", [P, 512], F32)) for i in range(4)]
        zero, gate_ps, gate_ok, val_ps, tap, ge_ok, f_ok, fh_ok, fl_ok, down_ps, down_ok = (
            sem(f"f_{x}") for x in ("zero", "gate_ps", "gate_ok", "val_ps", "tap", "ge_ok", "f_ok", "fh_ok", "fl_ok",
                                    "down_ps", "down_ok"))
        sq_ok, sacc_ok, sum_ps, ln_ok, rs_ok, t_ok, o_ok, ot_ps, ot_ok = (
            sem(f"f_{x}") for x in ("sq_ok", "sacc_ok", "sum_ps", "ln_ok", "rs_ok", "t_ok", "o_ok", "ot_ps", "ot_ok"))
        stored = [sem(f"f_stored{i}") for i in range(2)]
        block = ctx.enter_context(nc.Block())
        TURNS = FF_TILES // 2
        w_up = weight_view(io["w_up"][0])
        w_down = io["w_down"][0]

        def jobs(g, up, down):
            todo = [("gate", 0, 0, g * 2)] * up
            todo += [("down", 0, 1, g * 2 - 1), ("down", 1, 2, g * 2 - 1)] * down
            todo += [("val", 0, 0, g * 2 + 1), ("gate", 1, 1, g * 2), ("val", 1, 2, g * 2)] * up
            return todo

        def acc_rows(t):
            return (ge, f)[t % 2][:]

        def slot_free(e, g, kind, i):
            first = isinstance(g, int) and g == 0
            if kind == "gate" and i == 0 and not first:
                e.wait_ge(val_ps, g * 4 - 2)
            elif kind == "val" and i == 0:
                e.wait_ge(gate_ps, g * 4 + 2)
            elif kind == "down":
                e.wait_ge((gate_ps, val_ps)[i], g * 4)
            elif i == 1 and not first:
                e.wait_ge(down_ps, g * 16)

        def turns(e, body):
            body(0, 1, 0)
            with e.Fori(1, TURNS) as g:
                body(g, 1, 1)
            body(TURNS, 0, 1)

        @block.sync
        def _(e):
            def body(g, up, down):
                for kind, i, slot, earlier in jobs(g, up, down):
                    if not (isinstance(earlier, int) and earlier == 0):
                        e.wait_ge(w.split[slot], earlier)
                    if kind == "down":
                        rows = w_down[bass.ds(g * 2 * P + (i - 2) * P, P)]
                        e.dma_start(w.raw[:, slot].rearrange("p k n -> p (k n)"), rows).then_inc(w.loaded[slot], 16)
                    else:
                        c0 = i * P + (D_FF if kind == "val" else 0)
                        e.dma_start(w.raw[:, slot], w_up[:, :, bass.ds(g * 2 * P + c0, P)]).then_inc(w.loaded[slot], 16)
            turns(e, body)
            for t in range(KT):
                e.wait_ge(ot_ok, 2 * t + 2)
                e.dma_start(out[0, t * P:t * P + P, :], acc_rows(t)).then_inc(stored[t % 2], 16)
            e.wait_ge(stored[0], 64)
            e.wait_ge(stored[1], 64)

        @block.gpsimd
        def _(e):
            e.memset(img[:], 0.0).then_inc(zero, 1)

            def low(g, i):
                e.wait_ge(fh_ok, g * 2 + i + 1)
                e.tensor_tensor(f_lo[:, i], f[:], f_hi[:, i].bitcast(F32), ALU.subtract).then_inc(fl_ok, 1)

            def body(g, up, down):
                for kind, i, slot, earlier in jobs(g, up, down):
                    if kind == "down" and i == 0:
                        low(g - 1, 1)
                    if kind == "val" and i == 1:
                        low(g, 0)
                    slot_free(e, g, kind, i)
                    w.split_job(e, sh.ones[:], slot, earlier)

            turns(e, body)

        @block.tensor
        def _(e):
            e.sem_inc(gate_ok, 2)
            e.sem_inc(f_ok, 2)
            e.sem_inc(down_ok, 4)

            def up_job(g, kind, i, slot, earlier):
                e.wait_ge(w.split[slot], earlier + 1)
                for t in range(2):
                    n = 0
                    if kind == "gate":
                        e.wait_ge(gate_ok, g * 4 + i * 2 + t + 1)
                    else:
                        e.wait_ge(f_ok, g * 4 + i * 2 + t + 1)
                    for k in range(KT):
                        for wt, v in ((w.hi, sh.v_hi), (w.lo, sh.v_hi), (w.hi, sh.v_lo)):
                            mm = e.matmul((ps_g if kind == "gate" else ps_v)[t][:], wt[:, slot, k], v[:, k, t * 512:t * 512 + 512],
                                          start=(n == 0), stop=(n == 3 * KT - 1))
                            n += 1
                    mm.then_inc(gate_ps if kind == "gate" else val_ps, 1)

            def down_jobs(g):
                e.wait_ge(w.split[1], g * 2)
                e.wait_ge(w.split[2], g * 2)
                e.wait_ge(fl_ok, g * 2 + 1)
                for n in range(KT):
                    for t in range(2):
                        grp = 2 * n + t
                        e.wait_ge(down_ok, g * 16 + grp - 16 + 1)
                        m = 0
                        for i, s in ((0, 1), (1, 2)):
                            for wt, v in ((w.hi, f_hi), (w.lo, f_hi), (w.hi, f_lo)):
                                mm = e.matmul(ps_d[grp % 4][:], wt[:, s, n], v[:, i, t * 512:t * 512 + 512],
                                              start=(m == 0), stop=(m == 5))
                                m += 1
                        mm.then_inc(down_ps, 1)

            def body(g, up, down):
                for kind, i, slot, earlier in jobs(g, up, down):
                    if kind != "down":
                        up_job(g, kind, i, slot, earlier)
                    elif i == 0:
                        down_jobs(g)
            turns(e, body)
            e.wait_ge(sacc_ok, KT)
            for t in range(2):
                mm = e.matmul(ps_g[t][:], sh.ones[:], cacc[:].rearrange("p a b -> p (a b)")[:, t * 512:t * 512 + 512], start=True, stop=True)
            mm.then_inc(sum_ps, 1)
            e.wait_ge(o_ok, KT)
            for t in range(KT):
                for half in range(2):
                    n = 2 * t + half
                    if n >= 4:
                        e.wait_ge(ot_ok, n - 3)
                    for j in range(4):
                        tr = e.transpose(ps_d[n % 4][:, j * P:j * P + P], acc[:, 4 * half + j, t * P:t * P + P], sh.ident[:])
                    tr.then_inc(ot_ps, 1)

        @block.vector
        def _(e):
            def conv_tap(g, i, t):
                if t == 0:
                    e.wait_ge(gate_ok, g * 4 + 2 * i + 2 + 2)
                    e.wait_ge(ge_ok, g * 2 + i + 1)
                else:
                    e.wait_ge(tap, g * 18 + i * 9 + t)
                src = img[:, t // 3:t // 3 + ROWS, t % 3:t % 3 + GRID_W]
                wt = sh.par[:, bass.ds(g * 2 + P_FFN_DW + t * FF_TILES + i, 1)]
                if t == 0:
                    e.tensor_scalar(cacc[:], src, wt, sh.par[:, bass.ds(g * 2 + P_FFN_DW_B + i, 1)], ALU.mult, ALU.add).then_inc(tap, 1)
                else:
                    e.scalar_tensor_tensor(out=cacc[:], in0=src, scalar=wt, in1=cacc[:], op0=ALU.mult, op1=ALU.add).then_inc(tap, 1)

            def down_part(g, grp):
                n, t = grp // 2, grp % 2
                e.wait_ge(down_ps, g * 16 + grp - 16 + 1)
                dst = acc[:, n, t * 512:t * 512 + 512]
                e.tensor_tensor(dst, dst, ps_d[grp % 4][:], ALU.add).then_inc(down_ok, 1)

            def product(g, i):
                e.wait_ge(ge_ok, g * 2 + i + 2)
                for t in range(2):
                    e.wait_ge(val_ps, g * 4 + 2 * i + t + 1)
                    if t == 0:
                        e.wait_ge(fl_ok, g * 2 + i + 1)
                    e.tensor_tensor(f[:, t * 512:t * 512 + 512], ge[:, t * 512:t * 512 + 512], ps_v[t][:], ALU.mult).then_inc(f_ok, 1)

            def body(g, up, down):
                for grp in range(16):
                    if down:
                        down_part(g, grp)
                    if up and grp < 9:
                        conv_tap(g, 0, grp)
                if up:
                    product(g, 0)
                    for t in range(9):
                        conv_tap(g, 1, t)
                    product(g, 1)

            e.memset(acc[:], 0.0).then_inc(zero, 1)
            e.wait_ge(zero, 2)
            e.sem_inc(ge_ok, 1)
            turns(e, body)
            for k in range(KT):
                e.wait_ge(sq_ok, k + 1)
                if k == 0:
                    e.tensor_copy(cacc[:].rearrange("p a b -> p (a b)"), ge[:]).then_inc(sacc_ok, 1)
                else:
                    e.wait_ge(sacc_ok, k)
                    e.tensor_tensor(cacc[:].rearrange("p a b -> p (a b)"), cacc[:].rearrange("p a b -> p (a b)"), ge[:], ALU.add).then_inc(sacc_ok, 1)
            e.wait_ge(rs_ok, 1)
            for k in range(KT):
                e.scalar_tensor_tensor(out=acc[:, k], in0=acc[:, k], scalar=sh.post_ffn[:, k:k + 1], in1=rs[:],
                                       op0=ALU.mult, op1=ALU.mult).then_inc(t_ok, 1)
                e.wait_ge(t_ok, k + 1)
                e.tensor_tensor(acc[:, k], acc[:, k], sh.h2[:, k], ALU.add).then_inc(o_ok, 1)

        @block.scalar
        def _(e):
            e.wait_ge(zero, 2)
            e.sem_inc(fl_ok, 1)

            def gate_out(g, i):
                for t in range(2):
                    e.wait_ge(gate_ps, g * 4 + 2 * i + t + 1)
                    e.activation(img[:, 1 + 8 * t:9 + 8 * t, 1:1 + GRID_W], ps_g[t][:].rearrange("p (a b) -> p a b", b=GRID_W),
                                 ACT.Copy).then_inc(gate_ok, 1)

            def gelu(g, i):
                e.wait_ge(tap, g * 18 + 9 * i + 9)
                e.activation(ge[:], cacc[:].rearrange("p a b -> p (a b)"), ACT.Gelu_apprx_tanh).then_inc(ge_ok, 1)

            def f_high(g, i):
                e.wait_ge(f_ok, g * 4 + 2 * i + 2 + 2)
                if not (isinstance(g, int) and g == 0):
                    e.wait_ge(down_ps, g * 16)
                e.activation(f_hi[:, i], f[:], ACT.Copy).then_inc(fh_ok, 1)

            def body(g, up, down):
                if up:
                    gate_out(g, 0)
                    gelu(g, 0)
                    f_high(g, 0)
                    gate_out(g, 1)
                    gelu(g, 1)
                    f_high(g, 1)
            turns(e, body)
            for k in range(KT):
                e.wait_ge(down_ok, 4 + 16 * TURNS)
                if k:
                    e.wait_ge(sacc_ok, k)
                e.activation(ge[:], acc[:, k], ACT.Square).then_inc(sq_ok, 1)
            e.wait_ge(sum_ps, 1)
            for t in range(2):
                e.activation(rs[:, t * 512:t * 512 + 512], ps_g[t][:], ACT.Ln, bias=sh.eps[:, 0:1], scale=1.0 / D).then_inc(ln_ok, 1)
            e.wait_ge(ln_ok, 2)
            e.activation(rs[:], rs[:], ACT.Exp, scale=-0.5).then_inc(rs_ok, 1)
            for t in range(KT):
                if t >= 2:
                    e.wait_ge(stored[t % 2], 16 * (t // 2))
                for half in range(2):
                    e.wait_ge(ot_ps, 2 * t + half + 1)
                    e.activation(acc_rows(t)[:, half * 512:half * 512 + 512], ps_d[(2 * t + half) % 4][:], ACT.Copy).then_inc(ot_ok, 1)


def build(nc, io, out):
    sh = Shared()
    with ExitStack() as ctx:
        sb = lambda n, s, d=F32: ctx.enter_context(nc.sbuf_tensor(n, s, d))
        sh.held = []

        def take(name):
            sh.held.append(nc.alloc_semaphore(name))
            return sh.held[-1]

        sh.sem = take
        sh.par = sb("par", [P, N_PAR])
        sh.m = sb("m_ada", [P, 48, 2])
        sh.pre_mix = sb("v_pre_mix", [P, 2, KT])
        sh.post_mix = sb("v_post_mix", [P, KT])
        sh.pre_ffn = sb("v_pre_ffn", [P, KT])
        sh.post_ffn = sb("v_post_ffn", [P, KT])
        sh.ident = sb("ident", [P, P])
        sh.ones = sb("ones", [P, P])
        sh.warm = sb("warm", [P, 2])
        sh.eps = sb("eps", [P, 2])
        sh.y_dn = nc.dram_tensor("y_dn_scratch", (HEADS, P, SEQ), F32).ap()
        sh.y_lru = nc.dram_tensor("y_lru_scratch", (KT, P, SEQ), F32).ap()
        sh.gates = nc.dram_tensor("gate_scratch", (2 * KT, P, SEQ), F32).ap()
        with ExitStack() as mixers:
            sh.u_hi = mixers.enter_context(nc.sbuf_tensor("u_hi", [P, KT, T], F32R))
            sh.u_lo = mixers.enter_context(nc.sbuf_tensor("u_lo", [P, KT, T], F32R))
            norm_and_modulate(nc, sh, io)
            end_phase(nc, sh)
            with ExitStack() as heads:
                hb = lambda n, s, d=F32: heads.enter_context(nc.sbuf_tensor(n, s, d))
                sh.off = hb("mask_off", [P, 2, P])
                sh.strict = hb("mask_strict", [P, 2, P], BF16)
                sh.level = hb("mask_level", [P, 2, 7, P], BF16)
                sh.ident_r = hb("ident_r", [P, 2, P], F32R)
                per_token = lambda n: hb(n, [P, NCH, 16])
                sh.gcol, sh.eg, sh.neg_eg = per_token("gcol"), per_token("eg"), per_token("neg_eg")
                sh.eg_tot, sh.k_decay = per_token("eg_tot"), per_token("k_decay")
                sh.beta, sh.neg_beta = per_token("beta"), per_token("neg_beta")
                sh.grow = hb("grow", [16, T])
                with ExitStack() as tri:
                    sh.tri = tri.enter_context(nc.sbuf_tensor("mask_tri", [P, 2, P], F32))
                    sh.last_row = tri.enter_context(nc.sbuf_tensor("last_row", [P, 2, P], F32))
                    decay_gates(nc, sh, io)
                    end_phase(nc, sh)
                deltanet(nc, sh, io)
                end_phase(nc, sh)
            rg_lru(nc, sh, io)
            end_phase(nc, sh)
        sh.h2 = sb("h2", [P, KT, SEQ])
        sh.v_hi = sb("v_hi", [P, KT, SEQ], F32R)
        sh.v_lo = sb("v_lo", [P, KT, SEQ], F32R)
        merge(nc, sh, io)
        end_phase(nc, sh)
        conv_ffn(nc, sh, io, out)


_INS = ["x", "c", "ctx", "c_ctx", "w_ada", "b_ada", "g_pre_mix", "g_post_mix", "g_pre_ffn", "g_post_ffn", "w_in",
        "b_merge", "dn_conv", "dn_a_log", "dn_dt_bias", "dn_onorm", "lru_conv", "lru_conv_b", "lru_w_rg", "lru_b_rg",
        "lru_w_ig", "lru_b_ig", "lru_lambda", "w_branch_dn", "w_branch_lru", "w_out", "w_up", "ffn_dw", "ffn_dw_b",
        "w_down"]
_OUTS = [((1, 1024, 1024), "float32")]


def kernel(**inputs):
    import numpy as _np
    import concourse.bacc as _bacc
    from concourse import mybir as _mybir
    from concourse.bass_utils import run_bass_kernel_spmd as _run

    nc = _bacc.Bacc("TRN2", target_bir_lowering=False, num_devices=1)
    arrays, io = {}, {}
    for name in _INS:
        a = _np.ascontiguousarray(inputs[name])
        arrays[f"in_{name}_dram"] = a
        io[name] = nc.dram_tensor(f"in_{name}_dram", a.shape, _mybir.dt.from_np(a.dtype), kind="ExternalInput").ap()
    outs = []
    for i, (shape, dtype) in enumerate(_OUTS):
        dt = _mybir.dt.from_np(_np.dtype(dtype))
        outs.append(nc.dram_tensor(f"out_{i}_dram", shape, dt, kind="ExternalOutput").ap())
    build(nc, io, outs[0])
    r = _run(nc, [arrays], core_ids=[0])
    return r.results[0]["out_0_dram"]
```

```python
from contextlib import ExitStack

import concourse.bass as bass
from concourse import mybir

F32 = mybir.dt.float32
F32R = mybir.dt.float32r
BF16 = mybir.dt.bfloat16
ALU = mybir.AluOpType
ACT = mybir.ActivationFunctionType
AX_X = mybir.AxisListType.X

P = 128
D = 1024
KT = D // P
N_CTX = 256
SEQ = 1024
T = N_CTX + SEQ
HEADS = 8
CH = 128
NCH = T // CH
CTX_CH = N_CTX // CH
W_CONV = 4
PAD_LEFT = 2
D_FF = 4 * D
FF_TILES = D_FF // P
GRID_W = 64
ROWS = SEQ // GRID_W
EPS = 1e-6
LRU_C = 8.0
OFF = -1e30

SEG_ALL = [(0, 256), (256, 512), (768, 512)]
SEG_LAT = [(256, 512), (768, 512)]

COL_Q, COL_K, COL_V, COL_Z = 0, D, 2 * D, 3 * D
COL_AB = 4 * D
COL_XL = COL_AB + 32
COL_YL = COL_XL + D
COL_MG = COL_YL + D

PB_ADA, P_PRE_MIX, P_POST_MIX, P_PRE_FFN, P_POST_FFN, P_B_MERGE, P_C, P_C_CTX = 0, 48, 56, 64, 72, 80, 96, 104
P_LRU_CONV, P_LRU_CONV_B, P_B_RG, P_B_IG, P_LAM, P_ONORM = 112, 144, 152, 168, 184, 200
P_DN_CONV, P_FFN_DW, P_FFN_DW_B = 201, 297, 585
N_PAR = 617


class Shared:
    pass


def end_phase(nc, sh):
    nc.clear_and_free_semaphores(sh.held)
    sh.held.clear()
    nc.all_engine_barrier()


def weight_view(w):
    return w.rearrange("(k p) n -> p k n", p=P)


def norm_and_modulate(nc, sh, io):
    with ExitStack() as ctx:
        sb = lambda n, s, d=F32: ctx.enter_context(nc.sbuf_tensor(n, s, d))
        sem = sh.sem
        rows = sb("a_rows", [P, 7, P])
        ada_w = sb("a_ada_w", [P, 2, KT, 512])
        tok = sb("a_tok", [P, NCH, D])
        sq_junk = sb("a_sq", [P, D])
        ss = sb("a_ss", [P, NCH])
        rms = sb("a_rms", [P, NCH])
        rstd = sb("a_rstd", [P, NCH])
        ut = sb("a_ut", [P, 2, 512])
        ps_par = [ctx.enter_context(nc.psum_tensor(f"a_ps_par{i}", [P, 512], F32)) for i in range(2)]
        ps_m = ctx.enter_context(nc.psum_tensor("a_ps_m", [P, 512], F32))
        ps_t = [ctx.enter_context(nc.psum_tensor(f"a_ps_t{i}", [P, 512], F32)) for i in range(4)]
        rows_in = sem("a_rows_in")
        tok_in = sem("a_tok_in")
        ada_in = [sem(f"a_ada_in{i}") for i in range(2)]
        ada_used = sem("a_ada_used")
        consts = sem("a_consts")
        par_t = sem("a_par_transposed")
        par_ok = sem("a_par_ready")
        silu_ok = sem("a_silu_ready")
        m_ok = sem("a_m_ready")
        vec_ok = sem("a_vectors_ready")
        sq_ok = sem("a_squares_ready")
        rms_ok = sem("a_rms_ready")
        rstd_ok = sem("a_rstd_ready")
        scaled = sem("a_rows_scaled")
        tr_ok = sem("a_tile_transposed")
        ut_ok = sem("a_u_ready")
        uh_ok = sem("a_u_high_ready")
        ul_ok = sem("a_u_low_ready")
        block = ctx.enter_context(nc.Block())

        row = lambda name: io[name].rearrange("l (r p) -> (l r) p", p=P)
        row_loads = [
            (0, 0, row("b_ada")), (0, 48, row("g_pre_mix")), (0, 56, row("g_post_mix")),
            (0, 64, row("g_pre_ffn")), (0, 72, row("g_post_ffn")), (0, 80, row("b_merge")),
            (0, 96, row("c")), (0, 104, io["c_ctx"].rearrange("(r p) -> r p", p=P)),
            (1, 0, io["lru_conv"].rearrange("l k (r p) -> (l k r) p", p=P)), (1, 32, row("lru_conv_b")),
            (1, 40, io["lru_b_rg"].rearrange("l d (r p) -> (l d r) p", p=P)),
            (1, 56, io["lru_b_ig"].rearrange("l d (r p) -> (l d r) p", p=P)),
            (1, 72, io["lru_lambda"].rearrange("l d (r p) -> (l d r) p", p=P)),
            (1, 88, row("dn_onorm")),
            (2, 0, io["dn_conv"].rearrange("l k (r p) -> (l k r) p", p=P)),
        ]
        dw = io["ffn_dw"].rearrange("l a b (r p) -> (l a b r) p", p=P)
        row_loads += [(3 + i, 0, dw[96 * i:96 * i + 96]) for i in range(3)]
        row_loads.append((6, 0, row("ffn_dw_b")))
        row_tiles = [(0, 112, 0, 0), (1, 89, 0, 112), (2, 96, 0, P_DN_CONV), (3, 96, 0, P_FFN_DW),
                     (4, 96, 0, P_FFN_DW + 96), (5, 96, 1, 0), (6, 32, 1, 96)]
        split = P_FFN_DW + 192

        @block.sync
        def _(e):
            for tile, r0, src in row_loads:
                e.dma_start(rows[r0:r0 + src.shape[0], tile, :], src).then_inc(rows_in, 16)
            ada = weight_view(io["w_ada"][0])
            with e.Fori(0, 2) as i:
                for s in range(2):
                    e.wait_ge(ada_used, i * 2 + s + 1)
                    e.dma_start(ada_w[:, s], ada[:, :, bass.ds(i * 1024 + s * 512, 512)]).then_inc(ada_in[s], 16)

        @block.scalar
        def _(e):
            e.dma_start(tok[:, 0:CTX_CH, :], io["ctx"][0].rearrange("(t p) d -> p t d", p=P)).then_inc(tok_in, 16)
            e.dma_start(tok[:, CTX_CH:, :], io["x"][0].rearrange("(t p) d -> p t d", p=P)).then_inc(tok_in, 16)
            e.wait_ge(par_ok, 2)
            e.activation(sh.silu_c[:, :, 0], sh.par[:, P_C:P_C + KT], ACT.Silu).then_inc(silu_ok, 1)
            e.activation(sh.silu_c[:, :, 1], sh.par[:, P_C_CTX:P_C_CTX + KT], ACT.Silu).then_inc(silu_ok, 1)
            e.wait_ge(tok_in, 32)
            for t in range(NCH):
                if t:
                    e.wait_ge(sq_ok, t)
                e.activation(sq_junk[:], tok[:, t, :], ACT.Square, accum_out=ss[:, t:t + 1]).then_inc(sq_ok, 1)
            e.wait_ge(sq_ok, NCH)
            e.wait_ge(consts, 6)
            e.activation(rms[:], ss[:], ACT.Sqrt, bias=sh.eps[:, 0:1], scale=1.0 / D).then_inc(rms_ok, 1)
            e.wait_ge(vec_ok, 2)
            n = 0
            for k in range(KT):
                for t0, tn in SEG_ALL:
                    s = 1 if t0 == 0 else 0
                    e.wait_ge(tr_ok, n + 1)
                    if n >= 2:
                        e.wait_ge(ul_ok, n - 1)
                    e.activation(ut[:, n % 2, 0:tn], ps_t[n % 4][:, 0:tn], ACT.Identity,
                                 bias=sh.m[:, k, s:s + 1], scale=sh.pre_mix[:, s, k:k + 1]).then_inc(ut_ok, 1)
                    n += 1

        @block.gpsimd
        def _(e):
            build_constants(e, sh, consts)

        @block.tensor
        def _(e):
            e.wait_ge(rows_in, 16 * len(row_loads))
            e.wait_ge(consts, 6)
            for tile, nr, bank, c0 in row_tiles:
                e.transpose(ps_par[bank][:, c0:c0 + nr], rows[0:nr, tile, :], sh.ident[0:nr, 0:nr]).then_inc(par_t, 1)
            e.sem_inc(ada_used, 2)
            e.wait_ge(silu_ok, 2)
            with e.Fori(0, 2) as i:
                for s in range(2):
                    e.wait_ge(ada_in[s], i * 16 + 16)
                    for b in range(4):
                        for k in range(KT):
                            mm = e.matmul(ps_m[:, bass.ds(i * 16 + s * 8 + b * 2, 2)], ada_w[:, s, k, b * P:b * P + P],
                                          sh.silu_c[:, k, :], start=(k == 0), stop=(k == KT - 1))
                    mm.then_inc(ada_used, 1)
            e.wait_ge(scaled, NCH)
            n = 0
            for k in range(KT):
                for t0, tn in SEG_ALL:
                    if n >= 4:
                        e.wait_ge(ut_ok, n - 3)
                    for j in range(tn // P):
                        tr = e.transpose(ps_t[n % 4][:, j * P:j * P + P], tok[:, t0 // P + j, k * P:k * P + P],
                                         sh.ident[:])
                    tr.then_inc(tr_ok, 1)
                    n += 1

        @block.vector
        def _(e):
            e.memset(sh.eps[:, 0:1], EPS).then_inc(consts, 1)
            e.memset(sh.eps[:, 1:2], P * EPS).then_inc(consts, 1)
            e.wait_ge(par_t, len(row_tiles))
            e.tensor_copy(sh.par[:, 0:split], ps_par[0][:, 0:split]).then_inc(par_ok, 1)
            e.tensor_copy(sh.par[:, split:N_PAR], ps_par[1][:, 0:P]).then_inc(par_ok, 1)
            e.wait_ge(rms_ok, 1)
            e.reciprocal(rstd[:], rms[:]).then_inc(rstd_ok, 1)
            e.wait_ge(rstd_ok, 1)
            for t in range(NCH):
                e.tensor_scalar(tok[:, t, :], tok[:, t, :], rstd[:, t:t + 1], None, ALU.mult).then_inc(scaled, 1)
            e.wait_ge(par_ok, 2)
            e.wait_ge(ada_used, 6)
            e.tensor_tensor(sh.m[:, 0:2 * KT], ps_m[:, 0:4 * KT].rearrange("p (n s) -> p n s", s=2),
                            sh.par[:, PB_ADA:PB_ADA + 2 * KT].unsqueeze(2).broadcast_to([P, 2 * KT, 2]), ALU.add).then_inc(m_ok, 1)
            e.wait_ge(m_ok, 1)
            m = sh.m
            for s in range(2):
                e.scalar_tensor_tensor(out=sh.pre_mix[:, s, :], in0=m[:, KT:2 * KT, s], scalar=1.0,
                                       in1=sh.par[:, P_PRE_MIX:P_PRE_MIX + KT], op0=ALU.add, op1=ALU.mult).then_inc(vec_ok, 1)
            n = 0
            for k in range(KT):
                for t0, tn in SEG_ALL:
                    e.wait_ge(ut_ok, n + 1)
                    e.tensor_copy(sh.u_hi[:, k, t0:t0 + tn], ut[:, n % 2, 0:tn]).then_inc(uh_ok, 1)
                    e.wait_ge(uh_ok, n + 1)
                    e.tensor_tensor(sh.u_lo[:, k, t0:t0 + tn], ut[:, n % 2, 0:tn],
                                    sh.u_hi[:, k, t0:t0 + tn].bitcast(F32), ALU.subtract).then_inc(ul_ok, 1)
                    n += 1


def build_constants(e, sh, consts):
    e.memset(sh.ident[:], 0.0).then_inc(consts, 1)
    e.memset(sh.ones[:], 1.0).then_inc(consts, 1)
    e.wait_ge(consts, 4)
    e.affine_select(out=sh.ident[:], in_=sh.ident[:], compare_op=ALU.not_equal, fill=1.0, base=0,
                    pattern=[[-1, P]], channel_multiplier=1).then_inc(consts, 1)
    e.memset(sh.warm[:], 0.0).then_inc(consts, 1)


def build_triangles(e, sh, consts, base):
    e.memset(sh.tri[:], 1.0)
    e.memset(sh.off[:], 0.0)
    e.memset(sh.strict[:], 1.0)
    e.memset(sh.last_row[:], 1.0)
    e.memset(sh.level[:], 0.0).then_inc(consts, 1)
    e.wait_ge(consts, base + 1)
    for d, sign in ((0, 1), (1, -1)):
        for tile, shift, fill in ((sh.tri, 0, 0.0), (sh.off, 0, OFF), (sh.strict, -1, 0.0)):
            e.affine_select(out=tile[:, d], in_=tile[:, d], compare_op=ALU.is_ge, fill=fill, base=shift,
                            pattern=[[sign, P]], channel_multiplier=-sign)
        end = P - 1 if d == 0 else 0
        e.affine_select(out=sh.last_row[:, d], in_=sh.last_row[:, d], compare_op=ALU.is_equal, fill=0.0,
                        base=-end, pattern=[[0, P]], channel_multiplier=1)
    for d in range(2):
        for l in range(7):
            b = 1 << l
            half = 1 - d
            view = sh.level[:, d, l, :].rearrange("p (n t b) -> p n t b", t=2, b=b)[:, :, half, :]
            last = e.memset(view, 1.0)
    last.then_inc(consts, 1)
    e.wait_ge(consts, base + 2)
    for step in range(2):
        for d in range(2):
            for l in range(7):
                b = 1 << l
                half = 1 - d
                view = sh.level[:, d, l, :].rearrange("p (n t b) -> p n t b", t=2, b=b)[:, :, half, :]
                low = 0 if d == 0 else b
                if step == 0:
                    last = e.affine_select(out=view, in_=view, compare_op=ALU.is_ge, fill=0.0, base=-low,
                                           pattern=[[-2 * b, P // (2 * b)], [0, b]], channel_multiplier=1)
                else:
                    last = e.affine_select(out=view, in_=view, compare_op=ALU.is_ge, fill=0.0, base=low + b - 1,
                                           pattern=[[2 * b, P // (2 * b)], [0, b]], channel_multiplier=-1)
        last.then_inc(consts, 1)
        e.wait_ge(consts, base + 3 + step)


def decay_gates(nc, sh, io):
    with ExitStack() as ctx:
        sb = lambda n, s, d=F32: ctx.enter_context(nc.sbuf_tensor(n, s, d))
        sem = sh.sem
        raw = sb("g_raw", [P, KT, P])
        w_hi = sb("g_w_hi", [P, KT, P], F32R)
        w_lo = sb("g_w_lo", [P, KT, P], F32R)
        a_log = sb("g_a_log", [32, 1])
        dt_b = sb("g_dt_bias", [32, 1])
        neg_a = sb("g_neg_a", [32, 1])
        ab = sb("g_ab", [32, T])
        x = sb("g_x", [32, T])
        em = sb("g_em", [32, T])
        up = sb("g_up", [32, T])
        ln = sb("g_ln", [32, T])
        rec = sb("g_rec", [32, T])
        beta_r = sb("g_beta_r", [32, T])
        gb = sb("g_gb", [P, NCH, 64])
        diff = sb("g_diff", [P, NCH, 16])
        grow = sb("g_rows", [16, T])
        ps = ctx.enter_context(nc.psum_tensor("g_ps", [P, 3, 512], F32))
        ps_gb = ctx.enter_context(nc.psum_tensor("g_ps_gb", [P, 2, 512], F32))
        ps_c = ctx.enter_context(nc.psum_tensor("g_ps_c", [P, 512], F32))
        loaded, small_in, hi, lo = sem("g_loaded"), sem("g_small_in"), sem("g_hi"), sem("g_lo")
        consts, zeroed = sem("g_consts"), sem("g_zeroed")
        ab_mm, dve, act = sem("g_ab_mm"), sem("g_dve_step"), sem("g_act_step")
        gb_t, cum_mm, tot_mm, row_t = sem("g_gb_t"), sem("g_cum_mm"), sem("g_tot_mm"), sem("g_row_t")
        grow_out = sem("g_rows_out")
        block = ctx.enter_context(nc.Block())

        @block.sync
        def _(e):
            e.dma_start(raw[:], weight_view(io["w_in"][0])[:, :, COL_AB:COL_AB + P]).then_inc(loaded, 16)
            e.wait_ge(zeroed, 2)
            e.dma_start(a_log[0:16, :], io["dn_a_log"][0].rearrange("d (h o) -> (d h) o", o=1)).then_inc(small_in, 16)
            e.dma_start(dt_b[0:16, :], io["dn_dt_bias"][0].rearrange("d (h o) -> (d h) o", o=1)).then_inc(small_in, 16)
            e.wait_ge(dve, 22)
            e.dma_start(sh.grow_d, grow[:]).then_inc(grow_out, 16)
            e.wait_ge(grow_out, 16)

        @block.gpsimd
        def _(e):
            e.memset(a_log[:], 0.0).then_inc(zeroed, 1)
            e.memset(dt_b[:], 0.0).then_inc(zeroed, 1)
            build_triangles(e, sh, consts, 0)

        @block.tensor
        def _(e):
            e.wait_ge(lo, 1)
            for s, (t0, tn) in enumerate(SEG_ALL):
                n = 0
                for k in range(KT):
                    for w, u in ((w_hi, sh.u_hi), (w_lo, sh.u_hi), (w_hi, sh.u_lo)):
                        mm = e.matmul(ps[:, s, 0:tn], w[:, k, :], u[:, k, t0:t0 + tn], start=(n == 0), stop=(n == 23))
                        n += 1
                mm.then_inc(ab_mm, 1)
            e.wait_ge(dve, 12)
            e.wait_ge(act, 5)
            for c in range(NCH):
                for half, src in ((0, x), (32, beta_r)):
                    o = (c % 5) * 64 + half
                    tr = e.transpose(ps_gb[:, c // 5, o:o + 32], src[:, c * P:c * P + P], sh.ident[0:32, 0:32])
            tr.then_inc(gb_t, 1)
            e.wait_ge(dve, 14)
            e.wait_ge(consts, 4)
            for d in range(2):
                mm = e.matmul(ps_c[:, d * 80:d * 80 + 80], sh.tri[:, d, :], gb[:, :, d * 8:d * 8 + 8],
                              start=True, stop=True)
            mm.then_inc(cum_mm, 1)
            e.wait_ge(dve, 16)
            for d in range(2):
                mm = e.matmul(ps_c[:, 160 + d * 80:240 + d * 80], sh.last_row[:, d, :], sh.gcol[:, :, d * 8:d * 8 + 8],
                              start=True, stop=True)
            mm.then_inc(tot_mm, 1)
            for c in range(NCH):
                tr = e.transpose(ps[0:16, c // 4, (c % 4) * P:(c % 4) * P + P], sh.gcol[:, c, :], sh.ident[:])
            tr.then_inc(row_t, 1)

        @block.vector
        def _(e):
            e.wait_ge(loaded, 16)
            e.tensor_copy(w_hi[:], raw[:]).then_inc(hi, 1)
            e.wait_ge(hi, 1)
            e.tensor_tensor(w_lo[:], raw[:], w_hi[:].bitcast(F32), ALU.subtract).then_inc(lo, 1)
            for s, (t0, tn) in enumerate(SEG_ALL):
                e.wait_ge(ab_mm, s + 1)
                e.tensor_copy(ab[:, t0:t0 + tn], ps[0:32, s, 0:tn]).then_inc(dve, 1)
            e.wait_ge(dve, 3)
            e.wait_ge(small_in, 32)
            e.tensor_scalar(x[:], ab[:], dt_b[:, 0:1], None, ALU.add).then_inc(dve, 1)
            e.wait_ge(act, 2)
            e.tensor_scalar(up[:], em[:], 1.0, None, ALU.add).then_inc(dve, 1)
            e.wait_ge(dve, 5)
            e.reciprocal(rec[:], up[:]).then_inc(dve, 1)
            e.scalar_tensor_tensor(out=em[:], in0=up[:], scalar=-1.0, in1=em[:], op0=ALU.add, op1=ALU.subtract).then_inc(dve, 1)
            e.wait_ge(dve, 7)
            e.scalar_tensor_tensor(out=em[:], in0=em[:], scalar=-1.0, in1=rec[:], op0=ALU.mult, op1=ALU.mult).then_inc(dve, 1)
            e.wait_ge(act, 3)
            e.wait_ge(dve, 8)
            e.tensor_tensor(ln[:], ln[:], em[:], ALU.add).then_inc(dve, 1)
            e.wait_ge(dve, 9)
            e.scalar_tensor_tensor(out=x[:], in0=x[:], scalar=0.0, in1=ln[:], op0=ALU.max, op1=ALU.add).then_inc(dve, 1)
            e.wait_ge(act, 4)
            e.tensor_scalar(neg_a[:], neg_a[:], -1.0, None, ALU.mult).then_inc(dve, 1)
            e.wait_ge(dve, 11)
            e.tensor_scalar(x[:], x[:], neg_a[:, 0:1], None, ALU.mult).then_inc(dve, 1)
            e.wait_ge(gb_t, 1)
            for i in range(2):
                e.tensor_copy(gb[:, 5 * i:5 * i + 5, :], ps_gb[:, i, 0:320].rearrange("p (c n) -> p c n", c=5)).then_inc(dve, 1)
            e.wait_ge(dve, 14)
            e.wait_ge(cum_mm, 1)
            for d in range(2):
                e.tensor_copy(sh.gcol[:, :, d * 8:d * 8 + 8], ps_c[:, d * 80:d * 80 + 80].rearrange("p (c h) -> p c h", c=NCH)).then_inc(dve, 1)
            e.tensor_copy(sh.beta[:], gb[:, :, 48:64]).then_inc(dve, 1)
            e.tensor_scalar(sh.neg_beta[:], gb[:, :, 48:64], -1.0, None, ALU.mult).then_inc(dve, 1)
            e.wait_ge(tot_mm, 1)
            e.wait_ge(dve, 16)
            for d in range(2):
                e.tensor_tensor(diff[:, :, d * 8:d * 8 + 8], ps_c[:, 160 + d * 80:240 + d * 80].rearrange("p (c h) -> p c h", c=NCH),
                                sh.gcol[:, :, d * 8:d * 8 + 8], ALU.subtract).then_inc(dve, 1)
            e.wait_ge(act, 6)
            e.tensor_scalar(sh.neg_eg[:], sh.eg[:], -1.0, None, ALU.mult).then_inc(dve, 1)
            e.wait_ge(row_t, 1)
            e.tensor_copy(grow[:], ps[0:16, :, :].rearrange("p b n -> p (b n)")[:, 0:T]).then_inc(dve, 1)
            e.tensor_copy(sh.ident_r[:, 0], sh.ident[:])
            e.tensor_scalar(sh.ident_r[:, 1], sh.ident[:], -1.0, None, ALU.mult)

        @block.scalar
        def _(e):
            e.wait_ge(dve, 4)
            e.activation(em[:], x[:], ACT.Abs).then_inc(act, 1)
            e.wait_ge(act, 1)
            e.activation(em[:], em[:], ACT.Exp, scale=-1.0).then_inc(act, 1)
            e.wait_ge(dve, 5)
            e.activation(ln[:], up[:], ACT.Ln).then_inc(act, 1)
            e.wait_ge(small_in, 32)
            e.activation(neg_a[:], a_log[:], ACT.Exp).then_inc(act, 1)
            e.activation(beta_r[:], ab[:], ACT.Sigmoid).then_inc(act, 1)
            e.wait_ge(dve, 16)
            e.activation(sh.eg[:], sh.gcol[:], ACT.Exp).then_inc(act, 1)
            e.wait_ge(dve, 20)
            for d in range(2):
                e.activation(sh.eg_tot[:, :, d * 8:d * 8 + 8], ps_c[:, 160 + d * 80:240 + d * 80].rearrange("p (c h) -> p c h", c=NCH), ACT.Exp)
            e.activation(sh.k_decay[:], diff[:], ACT.Exp).then_inc(act, 1)


SUBSTEPS = 18
PIECES = 88
SHARES = [15, 15, 10] + [15, 6] * 5 + [15, 15] + [15, 10, 10]
FWD_ORDER = list(range(NCH))
BWD_ORDER = [1, 0] + list(range(NCH - 1, CTX_CH - 1, -1))
RING = [0, 1, 0, 1, 2]


def batch_chunks(ib):
    back = sorted(BWD_ORDER[2 * ib:2 * ib + 2])
    return [(0, 2 * ib), (0, 2 * ib + 1), (1, back[0]), (1, back[1])]


def deltanet(nc, sh, io):
    with ExitStack() as ctx:
        sb = lambda n, s, d=F32: ctx.enter_context(nc.sbuf_tensor(n, s, d))
        bank = lambda n: ctx.enter_context(nc.psum_tensor(n, [P, 512], F32))
        sem = sh.sem
        PADN = N_CTX + SEQ + 6
        CVN = PADN - 3
        LAT0 = N_CTX + 3
        LINE = ((0, 0, N_CTX), (LAT0, N_CTX, SEQ))
        SUMS = ((0, 256), (LAT0, 512), (LAT0 + 512, 512))
        raw = sb("d_raw", [P, 2, KT, P])
        w_hi = sb("d_w_hi", [P, 2, KT, P], F32R)
        w_lo = sb("d_w_lo", [P, 2, KT, P], F32R)
        pad = sb("d_pad", [P, PADN])
        cv = sb("d_cv", [P, CVN])
        nt = sb("d_nt", [P, CVN])
        vt = sb("d_vt", [P, T])
        zs = sb("d_zs", [P, SEQ])
        qt = sb("d_qt", [P, T])
        kt = sb("d_kt", [P, T])
        krow = sb("d_krow", [P, NCH, P])
        vrow = sb("d_vrow", [P, NCH, P])
        uf = sb("d_uf", [P, 3, 4, P])
        att = sb("d_att", [P, 3, 4, P])
        rbt = sb("d_rbt", [P, 4, P])
        dec = sb("d_dec", [P, 4, P])
        at = sb("d_at", [P, 4, P])
        ah = sb("d_ah", [P, 4, P], F32R)
        al = sb("d_al", [P, 4, P], F32R)
        am = sb("d_am", [P, 2, 4, P], F32R)
        tt = sb("d_tt", [P, 4, P], F32R)
        ut = sb("d_ut", [P, 4, P], F32R)
        xs = sb("d_xs", [P, 4, P], F32R)
        st = sb("d_state", [P, 2, P])
        rr = sb("d_rr", [P, 2, P])
        vn = sb("d_vn", [P, 2, P])
        kd = sb("d_kd", [P, 2, 2, P])
        o = sb("d_o", [P, NCH - CTX_CH, P])
        oss = sb("d_oss", [P, NCH - CTX_CH])
        ors = sb("d_ors", [P, NCH - CTX_CH])
        ps_d = [bank("d_ps_d0"), bank("d_ps_d1")]
        ps_t, ps_u, ps_x, ps_s, ps_o, ps_m = (bank(f"d_ps_{x}") for x in "tuxsom")
        of4 = lambda b: b[:].rearrange("p (c n) -> p c n", n=P)

        w_in_ok = [sem(f"d_w_in{i}") for i in range(2)]
        w_hi_ok = [sem(f"d_w_hi_ok{i}") for i in range(2)]
        w_split = [sem(f"d_w_split{i}") for i in range(2)]
        mm_ok, evac, pad0 = sem("d_mm_ok"), sem("d_evac"), sem("d_pad0")
        conv_step, conv_ok, silu_ok = sem("d_conv_step"), sem("d_conv_ok"), sem("d_silu_ok")
        nsq, nex, nrm = (sem(f"d_norm_{x}") for x in ("sq", "exp", "ok"))
        k_out, kta_in, ktb_in, misc_ps, misc_ok = (sem(f"d_{x}") for x in ("k_out", "kta_in", "ktb_in", "misc_ps", "misc_ok"))
        rb_in, dd_ok, dec_ok, kk_ps, at_ok = (sem(f"d_{x}") for x in ("rb_in", "dd_ok", "dec_ok", "kk_ps", "at_ok"))
        ats_ok, ah_ok, al_ok, am_ok = (sem(f"d_{x}") for x in ("ats_ok", "ah_ok", "al_ok", "am_ok"))
        u1_ok, t1_ps, tt_ok, x_ps, xs_ok, t_ps, u_ps, ut_ok, uf_ps, uf_ok = (
            sem(f"d_{x}") for x in ("u1_ok", "t1_ps", "tt_ok", "x_ps", "xs_ok", "t_ps", "u_ps", "ut_ok", "uf_ps", "uf_ok"))
        st_ok, ks_ps, r_ok, y_ps, vn_ok, o_ps, su_ps, kd_ok, o_step = (
            sem(f"d_{x}") for x in ("state_ok", "ks_ps", "r_ok", "y_ps", "vn_ok", "o_ps", "su_ps", "kd_ok", "o_step"))
        osq, oln, oex, orow, y_ok, y_out = (sem(f"d_{x}") for x in ("osq", "oln", "oex", "orow", "y_ok", "y_out"))
        block = ctx.enter_context(nc.Block())

        LAST = HEADS - 1
        w_in = weight_view(io["w_in"][0])

        def wait(e, s, value):
            if not (isinstance(value, int) and value <= 0):
                e.wait_ge(s, value)

        FIRST_GROUPS = [(j, t0, tn) for j in range(3) for t0, tn in SEG_ALL]
        GROUPS = [(j, t0, tn) for j in range(4) for t0, tn in (SEG_LAT if j == 2 else SEG_ALL)]
        Z_ONLY = [(2, t0, tn) for t0, tn in SEG_LAT]
        N_FIRST, N_GROUPS = len(FIRST_GROUPS), len(GROUPS)

        def group_number(h, g):
            return g if h is None else h * N_GROUPS + (g + N_FIRST)

        K, V, Z, Q = range(4)

        def misc_number(h, name):
            first = ["kn0", "kn1", "kn2", "rows0"]
            turn = ["kr1", "kr2", "vr1", "vr2", "qn0", "qn1", "qn2", "kq1", "kq2", "kn0", "kn1", "kn2", "kq3", "kq4",
                    "rows0", "y0", "y1"]
            if h is None:
                return first.index(name)
            if isinstance(h, int) and h == LAST:
                turn = [x for x in turn if x[:2] not in ("kn", "ro")]
            return h * 17 + (4 + turn.index(name))

        def first_piece(sub):
            part = (sub // SUBSTEPS * sum(SHARES) + sum(SHARES[:sub % SUBSTEPS])) / (5 * sum(SHARES))
            columns = [GROUPS[p // KT][2] for p in range(PIECES)]
            return sum(sum(columns[:p + 1]) <= part * sum(columns) + 1 for p in range(PIECES))

        PLACES = [first_piece(sub) for sub in range(5 * SUBSTEPS + 1)]

        def pieces(sub):
            return range(PLACES[sub], PLACES[sub + 1])

        def groups_done(b, i):
            place = lambda g: next(x for x in range(5 * SUBSTEPS) if PLACES[x + 1] >= (g + 1) * KT)
            behind = {0: 8, 3: SUBSTEPS + 13}
            return [g for g in range(N_GROUPS) if max(place(g), behind.get(g, 0)) == b * SUBSTEPS + i]

        @block.sync
        def _(e):
            def weights(slot, job, col):
                wait(e, w_split[slot], job)
                e.dma_start(raw[:, slot], w_in[:, :, col]).then_inc(w_in_ok[slot], 16)

            def spread_g(hh, ib, n):
                wait(e, dd_ok, n)
                for d, c in (batch_chunks(ib)[0], batch_chunks(ib)[2]):
                    row = sh.grow_d[bass.ds(hh + d * HEADS, 1), c * P:c * P + 2 * P]
                    e.dma_start(rbt[:, 2 * d:2 * d + 2, :].rearrange("p c n -> p (c n)"), row.broadcast_to([P, 2 * P])).then_inc(rb_in, 16)

            def load_k(hh, part):
                lo, hi = ((0, N_CTX), (N_CTX, T))[part]
                src = sh.k_scratch[bass.ds(hh, 1), :, lo:hi].rearrange("o p n -> (o p) n")
                e.dma_start(kt[:, lo:hi], src).then_inc((kta_in, ktb_in)[part], 16)

            cols = lambda base, h, ahead: bass.ds(h * P + (base + ahead * P), P)
            weights(0, 0, cols(COL_K, 0, 0))
            weights(1, 0, cols(COL_V, 0, 0))
            spread_g(0, 0, 0)
            weights(1, 1, cols(COL_Q, 0, 0))
            weights(0, 1, cols(COL_K, 0, 1))
            e.wait_ge(k_out, 32)
            load_k(0, 0)
            load_k(0, 1)
            spread_g(0, 1, 1)

            def turn(h, more):
                for b in range(5):
                    if b < 3:
                        spread_g(h, b + 2, h * 5 + b + 2)
                    elif more:
                        spread_g(h + 1, b - 3, h * 5 + b + 2)
                    if more and b < 4:
                        slot, job, col = ((1, h * 2 + 2, cols(COL_V, h, 1)), (0, h * 2 + 2, cols(COL_Z, h, 0)),
                                          (1, h * 2 + 3, cols(COL_Q, h, 1)), (0, h * 2 + 3, cols(COL_K, h, 2)))[b]
                        weights(slot, job, col)
                    elif b == 0:
                        weights(0, h * 2 + 2, cols(COL_Z, h, 0))
                    if more and b == 3:
                        e.wait_ge(k_out, h * 32 + 64)
                        e.wait_ge(ks_ps, h * NCH + 4)
                        load_k(h + 1, 0)
                    if more and b == 4:
                        e.wait_ge(ks_ps, h * NCH + NCH)
                        load_k(h + 1, 1)
            with e.Fori(0, LAST) as h:
                turn(h, True)
            turn(LAST, False)

        @block.gpsimd
        def _(e):
            e.memset(pad[:], 0.0).then_inc(pad0, 1)
            e.sem_inc(y_out, 16)

            def split(slot, job, products):
                e.wait_ge(w_in_ok[slot], job * 16 + 16)
                wait(e, mm_ok, products)
                e.tensor_tensor(w_hi[:, slot], raw[:, slot], sh.ones[:].unsqueeze(1).broadcast_to([P, KT, P]),
                                ALU.mult).then_inc(w_hi_ok[slot], 1)
                e.wait_ge(w_hi_ok[slot], job + 1)
                e.tensor_tensor(w_lo[:, slot], raw[:, slot], w_hi[:, slot].bitcast(F32),
                                ALU.subtract).then_inc(w_split[slot], 1)

            def square(conv_no, norm_no):
                e.wait_ge(silu_ok, conv_no + 1)
                wait(e, nrm, norm_no)
                e.tensor_tensor(nt[:], cv[:], cv[:], ALU.mult).then_inc(nsq, 1)

            of_dirs = lambda x: x.rearrange("p (d i) n -> p d i n", d=2)
            spread = lambda m: m.unsqueeze(2).broadcast_to([P, 2, 2, P])

            def level(n, l):
                if l == 0:
                    e.wait_ge(at_ok, n + 1)
                    wait(e, x_ps, n * 7 - 1)
                elif l == 2:
                    e.wait_ge(u1_ok, n + 1)
                elif l > 2:
                    e.wait_ge(x_ps, n * 7 + l - 2)
                e.tensor_tensor(of_dirs(am[:, l % 2]), of_dirs(at[:]), spread(sh.level[:, :, l, :]), ALU.mult).then_inc(am_ok, 1)

            def parts_of_a(n):
                e.tensor_tensor(of_dirs(at[:]), of_dirs(at[:]), spread(sh.strict[:]), ALU.mult).then_inc(ats_ok, 1)
                e.wait_ge(ats_ok, n + 1)
                wait(e, x_ps, n * 7)
                e.tensor_tensor(ah[:], at[:], sh.ones[:].unsqueeze(1).broadcast_to([P, 4, P]), ALU.mult).then_inc(ah_ok, 1)
                e.wait_ge(ah_ok, n + 1)
                e.tensor_tensor(al[:], at[:], ah[:].bitcast(F32), ALU.subtract).then_inc(al_ok, 1)

            def key_decay(h, s):
                e.wait_ge(misc_ok, h * 17 + 4 if s < CTX_CH else misc_number(h, "kr2") + 1)
                wait(e, su_ps, h * NCH + s - 1 if s else 0)
                e.wait_ge(pad0, 1)
                for d, c in enumerate((FWD_ORDER[s], BWD_ORDER[s])):
                    k = e.tensor_tensor(kd[:, s % 2, d], krow[:, c], sh.k_decay[:, c, bass.ds(h + d * 8, 1)].broadcast_to([P, P]),
                                        ALU.mult)
                k.then_inc(kd_ok, 1)

            def batch(h, b, more):
                n = h * 5 + b + 1
                inv = more or b < 4
                for i in range(SUBSTEPS):
                    if i == 0:
                        key_decay(h, 2 * b)
                        if inv:
                            level(n, 0)
                    if i in (1, 3, 5, 7, 9, 11) and inv:
                        level(n, (i + 1) // 2)
                    if i == 4:
                        key_decay(h, 2 * b + 1)
                    if i == 12 and inv:
                        parts_of_a(n)
                    if (b, i) == (0, 8):
                        e.wait_ge(y_out, h * 16 + 16)
                        square(h * 3 + 2, h * 2 + 1)
                    if more and (b, i) == (1, 14):
                        square(h * 3 + 3, h * 2 + 2)
                    if more and (b, i) == (0, 6):
                        split(1, h * 2 + 2, group_number(h, 0))
                    if more and (b, i) == (1, 10):
                        split(0, h * 2 + 2, group_number(h, 3))
                    if more and (b, i) == (2, 16):
                        split(1, h * 2 + 3, group_number(h, 6))
                    if more and (b, i) == (3, 16):
                        split(0, h * 2 + 3, group_number(h, 8))
                    if not more and (b, i) == (0, 2):
                        split(0, h * 2 + 2, group_number(h, 0))

            split(0, 0, 0)
            split(1, 0, 0)
            split(1, 1, 6)
            split(0, 1, 3)
            square(0, 0)
            level(0, 0)
            for l in range(1, 7):
                level(0, l)
            parts_of_a(0)
            with e.Fori(0, LAST) as h:
                for b in range(5):
                    batch(h, b, True)
            for b in range(5):
                batch(LAST, b, False)

        @block.tensor
        def _(e):
            def product(h, g, k, groups, slot, split_no):
                j, t0, tn = groups[g]
                if k == 0:
                    no = group_number(h, g)
                    e.wait_ge(w_split[slot], split_no + 1)
                    wait(e, evac, no if g == 0 and h is not None else no - 1)
                for n, (w, u) in enumerate(((w_hi, sh.u_hi), (w_lo, sh.u_hi), (w_hi, sh.u_lo))):
                    mm = e.matmul(ps_d[g % 2][:, 0:tn], w[:, slot, k, :], u[:, k, t0:t0 + tn],
                                  start=(k == 0 and n == 0), stop=(k == KT - 1 and n == 2))
                if k == KT - 1:
                    mm.then_inc(mm_ok, 1)

            def shared_bank(h, name):
                wait(e, misc_ok, misc_number(h, name))

            def norm_sums(h, name, norm_no, i):
                shared_bank(h, f"{name}{i}")
                e.wait_ge(nsq, norm_no + 1)
                c0, n = SUMS[i]
                e.matmul(ps_m[:, 0:n], sh.ones[:], nt[:, c0:c0 + n], start=True, stop=True).then_inc(misc_ps, 1)

            def to_rows(h, name, srcs):
                shared_bank(h, name)
                for x, (src, c) in enumerate(srcs):
                    tr = e.transpose(ps_m[:, x * P:x * P + P], src[:, c * P:c * P + P], sh.ident[:])
                tr.then_inc(misc_ps, 1)

            def keys_by_keys(ib, n):
                wait(e, xs_ok, n * 7)
                for x, (d, c) in enumerate(batch_chunks(ib)):
                    kc = kt[:, c * P:c * P + P]
                    mm = e.matmul(ps_x[:, x * P:x * P + P], kc, kc, start=True, stop=True)
                mm.then_inc(kk_ps, 1)

            def keys_by_queries(h, ib):
                shared_bank(h, f"kq{ib}")
                e.wait_ge(nrm, h * 2 + 2)
                for x, (d, c) in enumerate(batch_chunks(ib)):
                    mm = e.matmul(ps_m[:, x * P:x * P + P], kt[:, c * P:c * P + P], qt[:, c * P:c * P + P], start=True, stop=True)
                mm.then_inc(misc_ps, 1)

            q = lambda b, x: b[:, x * P:x * P + P]

            def add_identity_product(bank, sign, of, first=True):
                e.matmul(bank[:], sh.ident_r[:, sign], of[:].rearrange("p c n -> p (c n)"), start=first, stop=False)

            def first_transpose(n):
                wait(e, uf_ok, n)
                e.wait_ge(u1_ok, n + 1)
                for x in range(4):
                    tr = e.transpose(q(ps_t, x), ut[:, x].bitcast(F32), sh.ident[:])
                tr.then_inc(t1_ps, 1)

            def level_x(n, l):
                e.wait_ge(am_ok, n * 7 + l + 1)
                e.wait_ge(tt_ok, n * 7 + l)
                for x in range(4):
                    mm = e.matmul(q(ps_x, x), am[:, l % 2, x], tt[:, x], start=True, stop=True)
                mm.then_inc(x_ps, 1)

            def level_t(n, l):
                e.wait_ge(xs_ok, n * 7 + l)
                if l > 1:
                    e.wait_ge(ut_ok, n * 6 + l - 1)
                for x in range(4):
                    mm = e.matmul(q(ps_t, x), ut[:, x], xs[:, x], start=True, stop=True)
                mm.then_inc(t_ps, 1)
                if l < 6:
                    add_identity_product(ps_u, 0, ut)
                    for x in range(4):
                        mm = e.matmul(q(ps_u, x), xs[:, x], ut[:, x], start=False, stop=(x == 3))
                    mm.then_inc(u_ps, 1)

            def newton_r(n):
                e.wait_ge(tt_ok, n * 7 + 7)
                for x in range(4):
                    tr = e.transpose(q(ps_u, x), tt[:, x].bitcast(F32), sh.ident[:])
                tr.then_inc(u_ps, 1)
                e.wait_ge(al_ok, n + 1)
                e.matmul(ps_x[:], sh.ident_r[:, 0], sh.ident_r[:, 0].unsqueeze(1).broadcast_to([P, 4, P]), start=True, stop=False)
                add_identity_product(ps_x, 1, tt, first=False)
                for x in range(4):
                    e.matmul(q(ps_x, x), ah[:, x], tt[:, x], start=False, stop=False)
                    mm = e.matmul(q(ps_x, x), al[:, x], tt[:, x], start=False, stop=(x == 3))
                mm.then_inc(x_ps, 1)

            def newton_u(n):
                e.wait_ge(xs_ok, n * 7 + 7)
                e.wait_ge(ut_ok, n * 6 + 6)
                add_identity_product(ps_t, 0, ut)
                for x in range(4):
                    mm = e.matmul(q(ps_t, x), xs[:, x], ut[:, x], start=False, stop=(x == 3))
                mm.then_inc(uf_ps, 1)

            def state_products(h, s):
                e.wait_ge(st_ok, h * NCH + s + 1)
                for d, c in enumerate((FWD_ORDER[s], BWD_ORDER[s])):
                    mm = e.matmul(q(ps_s, d), kt[:, c * P:c * P + P], st[:, d], start=True, stop=True)
                mm.then_inc(ks_ps, 1)
                if s >= CTX_CH:
                    e.wait_ge(o_step, h * 32 + (s - CTX_CH) * 4 + 32)
                    for d, c in enumerate((FWD_ORDER[s], BWD_ORDER[s])):
                        e.matmul(q(ps_o, d), qt[:, c * P:c * P + P], st[:, d], start=True, stop=True)

            def solve(h, s):
                e.wait_ge(uf_ok, h * 5 + s // 2 + 1)
                e.wait_ge(r_ok, h * NCH + s + 1)
                for d in range(2):
                    x = s % 2 if d == 0 else 3 - s % 2
                    mm = e.matmul(q(ps_s, d + 2), uf[:, RING[s // 2], x], rr[:, d], start=True, stop=True)
                mm.then_inc(y_ps, 1)

            def new_state(h, s):
                e.wait_ge(vn_ok, h * NCH + s + 1)
                e.wait_ge(kd_ok, h * NCH + s + 1)
                for d in range(2):
                    mm = e.matmul(q(ps_s, d), kd[:, s % 2, d], vn[:, d], start=True, stop=True)
                mm.then_inc(su_ps, 1)
                if s >= CTX_CH:
                    for d in range(2):
                        x = s % 2 if d == 0 else 3 - s % 2
                        mm = e.matmul(q(ps_o, d + 2), att[:, RING[s // 2], x], vn[:, d], start=True, stop=True)
                    mm.then_inc(o_ps, 1)

            def head_rows(h, half):
                e.wait_ge(orow, h + 1)
                shared_bank(h, f"y{half}")
                for x in range(4):
                    tr = e.transpose(q(ps_m, x), o[:, 4 * half + x], sh.ident[:])
                tr.then_inc(misc_ps, 1)

            def dense(h, b, i, more):
                if more:
                    for p in pieces(b * SUBSTEPS + i):
                        j = GROUPS[p // KT][0]
                        slot = (0, 1, 0, 1)[j]
                        product(h, p // KT, p % KT, GROUPS, slot, h * 2 + (1, 2, 2, 3)[j])
                elif b < 2:
                    for p in range(16 * (b * 14 + i - 4) // 28, 16 * (b * 14 + i - 3) // 28) if 4 <= i < SUBSTEPS else ():
                        product(h, p // KT, p % KT, Z_ONLY, 0, h * 2 + 2)

            def batch(h, b, more):
                n = h * 5 + b + 1
                inv = more or b < 4
                s = 2 * b
                for i in range(SUBSTEPS):
                    if i == 0:
                        state_products(h, s)
                        if inv:
                            if b == 0:
                                e.wait_ge(ktb_in, h * 16 + 16)
                            if b == 4:
                                e.wait_ge(kta_in, h * 16 + 32)
                            keys_by_keys((b + 1) % 5, n)
                    if i == 1:
                        solve(h, s)
                    if i == 2:
                        new_state(h, s)
                        if inv:
                            first_transpose(n)
                    if i in (3, 5, 7, 9, 11, 13) and inv:
                        level_x(n, (i - 1) // 2)
                    if i in (4, 6, 8, 10, 12, 14) and inv:
                        level_t(n, (i - 2) // 2)
                    if i == 4:
                        state_products(h, s + 1)
                    if i == 5:
                        solve(h, s + 1)
                    if i == 6:
                        new_state(h, s + 1)
                    if i == 15 and inv:
                        newton_r(n)
                    if i == (17 if b == 0 else 15) and b < 4:
                        keys_by_queries(h, b + 1)
                    if i == 16 and inv:
                        newton_u(n)
                    if b == 0:
                        if i in (7, 8, 9, 10):
                            src, c0 = ((kt, 2), (kt, 6), (vt, 2), (vt, 6))[i - 7]
                            to_rows(h, ("kr1", "kr2", "vr1", "vr2")[i - 7], [(src, c0 + x) for x in range(4)])
                        if i in (11, 12, 13):
                            norm_sums(h, "qn", h * 2 + 1, i - 11)
                    if more and b == 1 and i >= 16:
                        norm_sums(h, "kn", h * 2 + 2, i - 16)
                    if more and b == 2 and i == 0:
                        norm_sums(h, "kn", h * 2 + 2, 2)
                    if more and (b, i) == (4, 8):
                        to_rows(h, "rows0", [(kt, 0), (kt, 1), (vt, 0), (vt, 1)])
                    if b == 4 and i in (15, 17):
                        head_rows(h, (i - 15) // 2)
                    dense(h, b, i, more)

            for g in range(N_FIRST):
                for k in range(KT):
                    product(None, g, k, FIRST_GROUPS, (0, 1, 1)[FIRST_GROUPS[g][0]], (0, 0, 1)[FIRST_GROUPS[g][0]])
                if g == 5:
                    for i in range(3):
                        norm_sums(None, "kn", 0, i)
            e.wait_ge(kta_in, 16)
            keys_by_keys(0, 0)
            e.wait_ge(silu_ok, 2)
            to_rows(None, "rows0", [(kt, 0), (kt, 1), (vt, 0), (vt, 1)])
            first_transpose(0)
            for l in range(1, 7):
                level_x(0, l)
                level_t(0, l)
            newton_r(0)
            newton_u(0)
            with e.Fori(0, LAST) as h:
                for b in range(5):
                    batch(h, b, True)
            for b in range(5):
                batch(LAST, b, False)

        @block.vector
        def _(e):
            e.sem_inc(o_step, 32)

            def tap(conv_no, j, hh, t, evacuated, cv_free=None):
                if t == 0:
                    e.wait_ge(evac, evacuated)
                    if cv_free is not None:
                        e.wait_ge(*cv_free)
                w = sh.par[:, bass.ds(hh + P_DN_CONV + t * 24 + j * 8, 1)]
                if t == 0:
                    e.tensor_scalar(cv[:], pad[:, 0:CVN], w, None, ALU.mult).then_inc(conv_step, 1)
                    return
                e.wait_ge(conv_step, conv_no * 3 + t)
                e.scalar_tensor_tensor(out=cv[:], in0=pad[:, t:t + CVN], scalar=w, in1=cv[:], op0=ALU.mult,
                                       op1=ALU.add).then_inc(conv_ok if t == W_CONV - 1 else conv_step, 1)

            def normalise(norm_no, compact):
                e.wait_ge(nex, norm_no + 1)
                for a, t0, n in LINE:
                    dst = compact[:, t0:t0 + n] if compact is not None else cv[:, a:a + n]
                    x = e.tensor_tensor(dst, cv[:, a:a + n], nt[:, a:a + n], ALU.mult)
                x.then_inc(nrm, 1)

            def exponents(hh, ib, n):
                e.wait_ge(rb_in, n * 32 + 32)
                for x, (d, c) in enumerate(batch_chunks(ib)):
                    y = e.scalar_tensor_tensor(out=dec[:, x], in0=rbt[:, x], scalar=sh.gcol[:, c, bass.ds(hh + d * 8, 1)],
                                               in1=sh.off[:, d], op0=ALU.subtract, op1=ALU.min)
                y.then_inc(dd_ok, 1)

            def minus_a(hh, ib, n):
                e.wait_ge(dec_ok, n + 1)
                e.wait_ge(kk_ps, n + 1)
                wait(e, al_ok, n)
                for x, (d, c) in enumerate(batch_chunks(ib)):
                    y = e.scalar_tensor_tensor(out=at[:, x], in0=of4(ps_x)[:, x], scalar=sh.neg_beta[:, c, bass.ds(hh + d * 8, 1)],
                                               in1=dec[:, x], op0=ALU.mult, op1=ALU.mult)
                y.then_inc(at_ok, 1)

            def first_u(n):
                e.wait_ge(am_ok, n * 7 + 1)
                wait(e, uf_ps, n)
                e.tensor_tensor(ut[:], am[:, 0].bitcast(F32), sh.ident[:].unsqueeze(1).broadcast_to([P, 4, P]),
                                ALU.add).then_inc(u1_ok, 1)

            def add_t(n, l):
                e.wait_ge(t_ps, n * 6 + l)
                e.tensor_tensor(tt[:], tt[:].bitcast(F32), of4(ps_t), ALU.add).then_inc(tt_ok, 1)

            def attention(h, ib):
                e.wait_ge(misc_ps, misc_number(h, f"kq{ib}") + 1)
                e.tensor_tensor(att[:, RING[ib]], of4(ps_m), dec[:], ALU.mult).then_inc(misc_ok, 1)

            def keep_u(ib, n):
                e.wait_ge(uf_ps, n + 1)
                e.tensor_copy(uf[:, RING[ib]], of4(ps_t)).then_inc(uf_ok, 1)

            def residual(h, s):
                e.wait_ge(ks_ps, h * NCH + s + 1)
                for d, c in enumerate((FWD_ORDER[s], BWD_ORDER[s])):
                    if s >= CTX_CH and d == 0:
                        e.wait_ge(misc_ok, misc_number(h, "vr2") + 1)
                    x = e.scalar_tensor_tensor(out=rr[:, d], in0=of4(ps_s)[:, d], scalar=sh.neg_eg[:, c, bass.ds(h + d * 8, 1)],
                                               in1=vrow[:, c], op0=ALU.mult, op1=ALU.add)
                x.then_inc(r_ok, 1)

            def new_state(h, s):
                e.wait_ge(su_ps, h * NCH + s + 1)
                if s < NCH - 1:
                    for d, c in enumerate((FWD_ORDER[s], BWD_ORDER[s])):
                        x = e.scalar_tensor_tensor(out=st[:, d], in0=st[:, d], scalar=sh.eg_tot[:, c, bass.ds(h + d * 8, 1)],
                                                   in1=of4(ps_s)[:, d], op0=ALU.mult, op1=ALU.add)
                    x.then_inc(st_ok, 1)

            def outputs(h, s):
                if s < CTX_CH:
                    return
                e.wait_ge(o_ps, h * 8 + s - CTX_CH + 1)
                o0 = h * 32 + (s - CTX_CH) * 4 + 32
                e.wait_ge(o_step, o0)
                for d, c in enumerate((FWD_ORDER[s], BWD_ORDER[s])):
                    oc = o[:, c - CTX_CH]
                    g = sh.eg[:, c, bass.ds(h + d * 8, 1)]
                    if (c < 6) == (d == 0):
                        e.tensor_scalar(oc, of4(ps_o)[:, d], g, None, ALU.mult).then_inc(o_step, 1)
                    else:
                        e.scalar_tensor_tensor(out=oc, in0=of4(ps_o)[:, d], scalar=g, in1=oc, op0=ALU.mult,
                                               op1=ALU.add).then_inc(o_step, 1)
                for d, c in enumerate((FWD_ORDER[s], BWD_ORDER[s])):
                    oc = o[:, c - CTX_CH]
                    e.wait_ge(o_step, o0 + 1 + d)
                    e.tensor_tensor(oc, oc, of4(ps_o)[:, d + 2], ALU.add).then_inc(o_step, 1)

            def conv_parts(h, b, i, more):
                if b == 0 and i in (1, 3, 5, 6):
                    tap(h * 3 + 2, 0, h, (1, 3, 5, 6).index(i), group_number(h, 0), (silu_ok, h * 3 + 2))
                if (b, i) == (0, 14):
                    normalise(h * 2 + 1, qt)
                if more and b == 1 and i in (8, 9, 10, 11):
                    tap(h * 3 + 3, 1, h + 1, i - 8, group_number(h, 3))
                if more and (b, i) == (2, 3):
                    normalise(h * 2 + 2, None)
                if more and (b, i) in ((2, 17), (3, 5), (3, 7), (3, 9)):
                    t = ((2, 17), (3, 5), (3, 7), (3, 9)).index((b, i))
                    tap(h * 3 + 4, 2, h + 1, t, group_number(h, 6), (k_out, h * 32 + 64))

            def head_output(h, i):
                sqv = nt[:, 0:SEQ].rearrange("p (c n) -> p c n", n=P)
                if i == 8:
                    e.memset(st[:], 0.0).then_inc(st_ok, 1)
                    e.wait_ge(o_step, h * 32 + 64)
                    e.tensor_tensor(sqv, o[:], o[:], ALU.mult).then_inc(osq, 1)
                if i == 9:
                    e.wait_ge(osq, h * 2 + 1)
                    e.tensor_reduce(oss[:], sqv, AX_X, ALU.add).then_inc(osq, 1)
                if i == 13:
                    e.wait_ge(oex, h + 1)
                    e.tensor_tensor(o[:], o[:], ors[:].unsqueeze(2).broadcast_to([P, NCH - CTX_CH, P]), ALU.mult).then_inc(orow, 1)
                if i in (15, 17):
                    half = (i - 15) // 2
                    e.wait_ge(misc_ps, misc_number(h, f"y{half}") + 1)
                    cols = slice(half * 512, half * 512 + 512)
                    e.scalar_tensor_tensor(out=nt[:, cols], in0=ps_m[:], scalar=sh.par[:, P_ONORM:P_ONORM + 1],
                                           in1=zs[:, cols], op0=ALU.mult, op1=ALU.mult).then_inc(misc_ok, 1)

            def batch(h, b, more):
                n = h * 5 + b + 1
                inv = more or b < 4
                hh, ib = (h, b + 1) if b < 4 else (h + 1, 0)
                s = 2 * b
                for i in range(SUBSTEPS):
                    if i == 0:
                        if inv:
                            if b:
                                e.wait_ge(misc_ok, misc_number(h, f"kq{b}") + 1)
                            exponents(hh, ib, n)
                        residual(h, s)
                        if inv:
                            minus_a(hh, ib, n)
                    if i == 1 and inv:
                        first_u(n)
                    if i == 2:
                        new_state(h, s)
                        outputs(h, s)
                    if i in (4, 6, 8, 10, 12, 14) and inv:
                        add_t(n, (i - 2) // 2)
                    if i == 4:
                        residual(h, s + 1)
                    if i == 6:
                        new_state(h, s + 1)
                        outputs(h, s + 1)
                    if i == (17 if b == 0 else 15) and b < 4:
                        attention(h, b + 1)
                    if i == 16 and inv:
                        keep_u(ib, n)
                    if b == 4:
                        head_output(h, i)
                    conv_parts(h, b, i, more)

            e.memset(st[:], 0.0).then_inc(st_ok, 1)
            for t in range(4):
                tap(0, 1, 0, t, 3)
            normalise(0, None)
            for t in range(4):
                tap(1, 2, 0, t, 6, (k_out, 32))
            exponents(0, 0, 0)
            minus_a(0, 0, 0)
            first_u(0)
            for l in range(1, 7):
                add_t(0, l)
            keep_u(0, 0)
            with e.Fori(0, LAST) as h:
                for b in range(5):
                    batch(h, b, True)
            for b in range(5):
                batch(LAST, b, False)

        @block.scalar
        def _(e):
            e.wait_ge(pad0, 1)

            def evacuate(h, g, groups, is_z, pad_free):
                _, t0, tn = groups[g]
                e.wait_ge(mm_ok, group_number(h, g) + 1)
                if is_z:
                    e.activation(zs[:, t0 - N_CTX:t0 - N_CTX + tn], ps_d[g % 2][:, 0:tn], ACT.Silu).then_inc(evac, 1)
                    return
                if pad_free is not None:
                    wait(e, conv_ok, pad_free)
                c0 = t0 + PAD_LEFT if t0 < N_CTX else t0 + PAD_LEFT + 3
                e.activation(pad[:, c0:c0 + tn], ps_d[g % 2][:, 0:tn], ACT.Copy).then_inc(evac, 1)

            def silu(conv_no, dst):
                e.wait_ge(conv_ok, conv_no + 1)
                if dst is None:
                    e.activation(cv[:], cv[:], ACT.Silu).then_inc(silu_ok, 1)
                    return
                for a, t0, n in LINE:
                    x = e.activation(dst[:, t0:t0 + n], cv[:, a:a + n], ACT.Silu)
                x.then_inc(silu_ok, 1)

            def norm_log(h, name, norm_no, i, is_q):
                e.wait_ge(misc_ps, misc_number(h, f"{name}{i}") + 1)
                scale, bias = (float(P), sh.eps[:, 1:2]) if is_q else (1.0, sh.eps[:, 0:1])
                c0, n = SUMS[i]
                e.activation(nt[:, c0:c0 + n], ps_m[:, 0:n], ACT.Ln, bias=bias, scale=scale).then_inc(misc_ok, 1)

            def norm_exp(h, name):
                e.wait_ge(misc_ok, misc_number(h, f"{name}2") + 1)
                for a, _, n in LINE:
                    x = e.activation(nt[:, a:a + n], nt[:, a:a + n], ACT.Exp, scale=-0.5)
                x.then_inc(nex, 1)

            def rows(h, name, dst):
                e.wait_ge(misc_ps, misc_number(h, name) + 1)
                e.activation(dst, of4(ps_m), ACT.Copy).then_inc(misc_ok, 1)

            def first_rows(h):
                e.wait_ge(misc_ps, misc_number(h, "rows0") + 1)
                e.activation(krow[:, 0:2], of4(ps_m)[:, 0:2], ACT.Copy)
                e.activation(vrow[:, 0:2], of4(ps_m)[:, 2:4], ACT.Copy).then_inc(misc_ok, 1)

            def store_k(hh, norm_no):
                e.wait_ge(nrm, norm_no + 1)
                for a, t0, n in LINE:
                    dst = sh.k_scratch[bass.ds(hh, 1), :, t0:t0 + n].rearrange("o p n -> (o p) n")
                    e.dma_start(dst, cv[:, a:a + n]).then_inc(k_out, 16)

            def decays(n):
                e.wait_ge(dd_ok, n + 1)
                e.activation(dec[:], dec[:], ACT.Exp).then_inc(dec_ok, 1)

            def copy_t(n):
                e.wait_ge(t1_ps, n + 1)
                e.activation(tt[:], of4(ps_t), ACT.Copy).then_inc(tt_ok, 1)

            def copy_x(n, l):
                e.wait_ge(x_ps, n * 7 + l)
                e.activation(xs[:], of4(ps_x), ACT.Copy).then_inc(xs_ok, 1)

            def copy_u(n, l):
                e.wait_ge(u_ps, n * 6 + l)
                e.activation(ut[:], of4(ps_u), ACT.Copy).then_inc(ut_ok, 1)

            def new_values(h, s):
                e.wait_ge(y_ps, h * NCH + s + 1)
                for d, c in enumerate((FWD_ORDER[s], BWD_ORDER[s])):
                    x = e.activation(vn[:, d], of4(ps_s)[:, d + 2], ACT.Copy, scale=sh.beta[:, c, bass.ds(h + d * 8, 1)])
                x.then_inc(vn_ok, 1)

            def batch(h, b, more):
                n = h * 5 + b + 1
                inv = more or b < 4
                s = 2 * b
                for i in range(SUBSTEPS):
                    if i == 0 and inv:
                        decays(n)
                    if i == 1:
                        new_values(h, s)
                    if i == 2 and inv:
                        copy_t(n)
                    if i in (3, 5, 7, 9, 11, 13) and inv:
                        copy_x(n, (i - 1) // 2)
                    if i == 5:
                        new_values(h, s + 1)
                    if i in (4, 6, 8, 10, 12) and inv:
                        copy_u(n, (i - 2) // 2)
                    if i == 15 and inv:
                        copy_u(n, 6)
                        copy_x(n, 7)
                    if b == 0:
                        if i == 7:
                            silu(h * 3 + 2, None)
                        if i in (7, 8, 9, 10):
                            dst = (krow, krow, vrow, vrow)[i - 7]
                            c0 = (2, 6, 2, 6)[i - 7]
                            rows(h, ("kr1", "kr2", "vr1", "vr2")[i - 7], dst[:, c0:c0 + 4])
                        if i in (11, 12, 13):
                            norm_log(h, "qn", h * 2 + 1, i - 11, True)
                        if i == 13:
                            norm_exp(h, "qn")
                    if more and b == 1:
                        if i == 13:
                            silu(h * 3 + 3, None)
                        if i >= 16:
                            norm_log(h, "kn", h * 2 + 2, i - 16, False)
                    if more and (b, i) == (2, 0):
                        norm_log(h, "kn", h * 2 + 2, 2, False)
                        norm_exp(h, "kn")
                    if more and (b, i) == (2, 4):
                        store_k(h + 1, h * 2 + 2)
                    if more and (b, i) == (3, 11):
                        silu(h * 3 + 4, vt)
                    if more and (b, i) == (4, 8):
                        first_rows(h)
                    if (b, i) == (4, 11):
                        head_norm(h)
                    if more:
                        for g in groups_done(b, i):
                            j = GROUPS[g][0]
                            evacuate(h, g, GROUPS, j == Z, h * 3 + (3, 4, 0, 5)[j])
                    elif (b, i) in ((1, 3), (2, 3)):
                        evacuate(h, b - 1, Z_ONLY, True, None)

            def head_norm(h):
                e.wait_ge(osq, h * 2 + 2)
                e.activation(ors[:], oss[:], ACT.Ln, bias=sh.eps[:, 0:1], scale=1.0 / P).then_inc(oln, 1)
                e.wait_ge(oln, h + 1)
                e.activation(ors[:], ors[:], ACT.Exp, scale=-0.5).then_inc(oex, 1)

            def store_output(h):
                e.wait_ge(misc_ok, misc_number(h, "y1") + 1)
                e.dma_start(sh.y_dn[bass.ds(h, 1)].rearrange("o p n -> (o p) n"), nt[:, 0:SEQ]).then_inc(y_out, 16)

            for g in range(3):
                evacuate(None, g, FIRST_GROUPS, False, 0)
            silu(0, None)
            for g in range(3, 6):
                evacuate(None, g, FIRST_GROUPS, False, 1)
            for i in range(3):
                norm_log(None, "kn", 0, i, False)
            norm_exp(None, "kn")
            store_k(0, 0)
            silu(1, vt)
            for g in range(6, 9):
                evacuate(None, g, FIRST_GROUPS, False, 2)
            decays(0)
            first_rows(None)
            copy_t(0)
            for l in range(1, 7):
                copy_x(0, l)
                if l < 6:
                    copy_u(0, l)
            copy_u(0, 6)
            copy_x(0, 7)
            with e.Fori(0, LAST) as h:
                for b in range(5):
                    batch(h, b, True)
                store_output(h)
            for b in range(5):
                batch(LAST, b, False)
            store_output(LAST)
            e.wait_ge(y_out, 16 + 16 * HEADS)


def rg_lru(nc, sh, io):
    with ExitStack() as ctx:
        sb = lambda n, s, d=F32: ctx.enter_context(nc.sbuf_tensor(n, s, d))
        sem = sh.sem
        PADN = N_CTX + SEQ + 6
        raw = sb("l_raw", [P, 2, KT, P])
        w_hi = sb("l_w_hi", [P, 2, KT, P], F32R)
        w_lo = sb("l_w_lo", [P, 2, KT, P], F32R)
        ada_w = sb("l_ada_w", [P, KT, 512])
        wg = sb("l_wg", [P, 4, P])
        pad = sb("l_pad", [P, PADN])
        xc = sb("l_xc", [P, T])
        r = sb("l_r", [P, 2, T])
        ig = sb("l_i", [P, 2, T])
        a = sb("l_a", [P, 2, T])
        q = sb("l_q", [P, 2, T])
        gy = sb("l_gy", [P, SEQ])
        gm = sb("l_gm", [P, 2, SEQ])
        y = sb("l_y", [P, SEQ])
        lam = sb("l_lam", [P, 6, 16])
        cols = sb("l_cols", [P, 10])
        ps_d = [ctx.enter_context(nc.psum_tensor(f"l_ps_d{i}", [P, 512], F32)) for i in range(3)]
        ps_g = [ctx.enter_context(nc.psum_tensor(f"l_ps_g{i}", [P, 512], F32)) for i in range(4)]
        ps_m = ctx.enter_context(nc.psum_tensor("l_ps_m", [P, 512], F32))
        ada_in, ada_used, m_done = sem("l_ada_in"), sem("l_ada_used"), sem("l_m_ready")
        w_in_ok = [sem(f"l_w_in{i}") for i in range(2)]
        w_hi_ok, w_split, mm_ok, evac = sem("l_w_hi_ok"), sem("l_w_split"), sem("l_mm_ok"), sem("l_evac")
        cols_ok = sem("l_cols_ok")
        zero, wg_in, gate_ps, gate_ok = sem("l_zero"), sem("l_wg_in"), sem("l_gate_ps"), sem("l_gate_ok")
        conv_step, xc_ok, lam_v, lam_s = sem("l_conv_step"), sem("l_xc_ok"), sem("l_lam_v"), sem("l_lam_s")
        a_ok, th_ok, a2_ok, m_ok, sq_ok, ix_ok, in_ok, h_ok, y_step, y_out, g_out = (
            sem(f"l_{x}") for x in ("a_ok", "tanh_ok", "a2_ok", "m_ok", "sqrt_ok", "ix_ok", "inp_ok", "h_ok", "y_step",
                                    "y_out", "g_done"))
        g_out = [sem(f"l_g_out{i}") for i in range(2)]
        block = ctx.enter_context(nc.Block())

        jobs = [(COL_XL, SEG_ALL), (COL_YL, SEG_LAT), (COL_MG, SEG_LAT), (COL_MG + D, SEG_LAT)]
        groups = [(j, t0, tn) for j, (_, segs) in enumerate(jobs) for t0, tn in segs]
        JOBS, GROUPS, GATES = len(jobs), len(groups), 12
        w_in = weight_view(io["w_in"][0])

        @block.sync
        def _(e):
            e.wait_ge(zero, 2)
            with e.Fori(0, KT) as m:
                for j, (col, _) in enumerate(jobs):
                    e.wait_ge(w_split, m * JOBS + j + 1)
                    e.dma_start(raw[:, j % 2], w_in[:, :, bass.ds(m * P + col, P)]).then_inc(w_in_ok[j % 2], 16)
                    if j == 0:
                        e.wait_ge(gate_ps, m * GATES + GATES)
                        for g, name in enumerate(("lru_w_rg", "lru_w_ig")):
                            for b in range(2):
                                src = io[name][0][:, bass.ds(m * 2 + b, 1)].rearrange("d o i j -> (o i) d j")
                                e.dma_start(wg[64 * b:64 * b + 64, 2 * g:2 * g + 2, 64 * b:64 * b + 64], src).then_inc(wg_in, 16)

        @block.gpsimd
        def _(e):
            e.memset(wg[:], 0.0).then_inc(zero, 1)
            e.memset(pad[:], 0.0).then_inc(zero, 1)
            e.sem_inc(w_split, 2)

            def split(m, j):
                e.wait_ge(w_in_ok[j % 2], m * 32 + 16 * (j // 2) + 16)
                e.wait_ge(mm_ok, m * GROUPS + (7, 9, 12, 14)[j])
                e.tensor_tensor(w_hi[:, j % 2], raw[:, j % 2], sh.ones[:].unsqueeze(1).broadcast_to([P, KT, P]),
                                ALU.mult).then_inc(w_hi_ok, 1)
                e.wait_ge(w_hi_ok, m * JOBS + j + 1)
                e.tensor_tensor(w_lo[:, j % 2], raw[:, j % 2], w_hi[:, j % 2].bitcast(F32), ALU.subtract).then_inc(w_split, 1)

            def products(m):
                for d in range(2):
                    e.wait_ge(a_ok, m * 2 + d + 1)
                    e.wait_ge(in_ok, m * 2 + d + 1)
                    e.tensor_tensor(q[:, d], a[:, d], a[:, d], ALU.mult).then_inc(a2_ok, 1)
                    e.tensor_tensor(ig[:, d], ig[:, d], xc[:], ALU.mult).then_inc(ix_ok, 1)

            with e.Fori(0, KT) as m:
                for j in range(JOBS):
                    split(m, j)
                products(m)

        @block.tensor
        def _(e):
            def project(m, g):
                j, t0, tn = groups[g]
                if g == 0 or groups[g - 1][0] != j:
                    e.wait_ge(w_split, m * JOBS + j + 3)
                e.wait_ge(evac, m * GROUPS + g + 7)
                n = 0
                for k in range(KT):
                    for w, u in ((w_hi, sh.u_hi), (w_lo, sh.u_hi), (w_hi, sh.u_lo)):
                        mm = e.matmul(ps_d[g % 3][:, 0:tn], w[:, j % 2, k, :], u[:, k, t0:t0 + tn],
                                      start=(n == 0), stop=(n == 3 * KT - 1))
                        n += 1
                mm.then_inc(mm_ok, 1)

            with e.Fori(0, KT) as m:
                for g in range(7):
                    project(m, g)
                e.wait_ge(wg_in, m * 64 + 64)
                e.wait_ge(xc_ok, m * 2 + 2)
                n = 0
                for g in range(4):
                    for t0, tn in SEG_ALL:
                        e.wait_ge(gate_ok, m * GATES + n + 9)
                        e.matmul(ps_g[n % 4][:, 0:tn], wg[:, g], xc[:, t0:t0 + tn], start=True, stop=True).then_inc(gate_ps, 1)
                        n += 1
                for g in range(7, GROUPS):
                    project(m, g)
                e.wait_ge(ada_in, m * 16 + 16)
                for b in range(4):
                    for k in range(KT):
                        mm = e.matmul(ps_m[:, bass.ds(m * 8 + b * 2, 2)], ada_w[:, k, b * P:b * P + P], sh.silu_c[:, k, :],
                                      start=(k == 0), stop=(k == KT - 1))
                mm.then_inc(ada_used, 1)

        @block.vector
        def _(e):
            e.sem_inc(mm_ok, GROUPS)
            e.sem_inc(evac, GROUPS)
            e.sem_inc(gate_ps, GATES)
            e.sem_inc(gate_ok, GATES)
            e.sem_inc(in_ok, 2)
            e.tensor_scalar(lam[:, 0], sh.par[:, P_LAM:P_LAM + 16], -1.0, None, ALU.mult).then_inc(lam_v, 1)
            e.wait_ge(lam_s, 2)
            e.tensor_scalar(lam[:, 2], lam[:, 1], 1.0, None, ALU.add).then_inc(lam_v, 1)
            e.wait_ge(lam_v, 2)
            e.reciprocal(lam[:, 4], lam[:, 2]).then_inc(lam_v, 1)
            e.scalar_tensor_tensor(out=lam[:, 1], in0=lam[:, 2], scalar=-1.0, in1=lam[:, 1], op0=ALU.add,
                                   op1=ALU.subtract).then_inc(lam_v, 1)
            e.wait_ge(lam_v, 4)
            e.scalar_tensor_tensor(out=lam[:, 1], in0=lam[:, 1], scalar=-1.0, in1=lam[:, 4], op0=ALU.mult,
                                   op1=ALU.mult).then_inc(lam_v, 1)
            e.wait_ge(lam_v, 5)
            e.wait_ge(lam_s, 3)
            e.tensor_tensor(lam[:, 3], lam[:, 3], lam[:, 1], ALU.add).then_inc(lam_v, 1)
            e.wait_ge(lam_v, 6)
            e.scalar_tensor_tensor(out=lam[:, 0], in0=lam[:, 0], scalar=0.0, in1=lam[:, 3], op0=ALU.max,
                                   op1=ALU.add).then_inc(lam_v, 1)
            e.wait_ge(lam_v, 7)
            e.tensor_scalar(lam[:, 4], lam[:, 0], LRU_C, None, ALU.mult).then_inc(lam_v, 1)
            e.tensor_scalar(lam[:, 5], lam[:, 0], -LRU_C, None, ALU.mult).then_inc(lam_v, 1)

            def conv(m):
                e.wait_ge(evac, m * GROUPS + 3 + GROUPS)
                w = lambda t: sh.par[:, bass.ds(m + P_LRU_CONV + t * KT, 1)]
                b = sh.par[:, bass.ds(m + P_LRU_CONV_B, 1)]
                for i, (c0, t0, tn) in enumerate(((0, 0, N_CTX), (N_CTX + 3, N_CTX, SEQ))):
                    x = xc[:, t0:t0 + tn]
                    e.tensor_scalar(x, pad[:, c0:c0 + tn], w(0), b, ALU.mult, ALU.add).then_inc(conv_step, 1)
                    for t in range(1, W_CONV):
                        e.wait_ge(conv_step, m * 6 + 3 * i + t)
                        e.scalar_tensor_tensor(out=x, in0=pad[:, c0 + t:c0 + t + tn], scalar=w(t), in1=x, op0=ALU.mult,
                                               op1=ALU.add).then_inc(xc_ok if t == W_CONV - 1 else conv_step, 1)

            def scans(m):
                for d in range(2):
                    e.wait_ge(a2_ok, m * 2 + d + 1)
                    e.wait_ge(th_ok, m * 2 + d + 1)
                    e.scalar_tensor_tensor(out=q[:, d], in0=q[:, d], scalar=1.0, in1=r[:, d], op0=ALU.add,
                                           op1=ALU.mult).then_inc(m_ok, 1)
                for d in range(2):
                    e.wait_ge(sq_ok, m * 2 + d + 1)
                    e.wait_ge(ix_ok, m * 2 + d + 1)
                    e.tensor_tensor(ig[:, d], ig[:, d], q[:, d], ALU.mult).then_inc(in_ok, 1)
                    e.wait_ge(in_ok, m * 2 + d + 3)
                    if d == 0:
                        e.tensor_tensor_scan(r[:, 0], a[:, 0], ig[:, 0], 0.0, ALU.mult, ALU.add).then_inc(h_ok, 1)
                    else:
                        back = lambda x, lo, hi: x[:, 1, hi - 1:(lo - 1 if lo else None):-1]
                        e.tensor_tensor_scan(back(r, 0, N_CTX), back(a, 0, N_CTX), back(ig, 0, N_CTX), 0.0, ALU.mult,
                                             ALU.add).then_inc(h_ok, 1)
                        e.wait_ge(h_ok, m * 3 + 2)
                        e.tensor_tensor_scan(back(r, N_CTX, T), back(a, N_CTX, T), back(ig, N_CTX, T), r[:, 1, 0:1],
                                             ALU.mult, ALU.add).then_inc(h_ok, 1)
                e.wait_ge(h_ok, m * 3 + 3)
                e.wait_ge(y_out, m * 16 + 16)
                e.tensor_tensor(y[:], r[:, 0, N_CTX:T], r[:, 1, N_CTX:T], ALU.add).then_inc(y_step, 1)
                e.wait_ge(y_step, m * 2 + 1)
                e.tensor_tensor(y[:], y[:], gy[:], ALU.mult).then_inc(y_step, 1)

            e.sem_inc(y_out, 16)
            with e.Fori(0, KT) as m:
                conv(m)
                scans(m)
            e.wait_ge(ada_used, KT + 1)
            e.tensor_tensor(sh.m[:, 2 * KT:], ps_m[:, 0:8 * KT].rearrange("p (n s) -> p n s", s=2),
                            sh.par[:, PB_ADA + 2 * KT:PB_ADA + 6 * KT].unsqueeze(2).broadcast_to([P, 4 * KT, 2]),
                            ALU.add).then_inc(m_done, 1)
            e.wait_ge(m_done, 1)
            e.tensor_tensor(sh.post_mix[:], sh.m[:, 2 * KT:3 * KT, 0], sh.par[:, P_POST_MIX:P_POST_MIX + KT],
                            ALU.mult).then_inc(m_done, 1)
            e.scalar_tensor_tensor(out=sh.pre_ffn[:], in0=sh.m[:, 4 * KT:5 * KT, 0], scalar=1.0,
                                   in1=sh.par[:, P_PRE_FFN:P_PRE_FFN + KT], op0=ALU.add, op1=ALU.mult).then_inc(m_done, 1)
            e.tensor_tensor(sh.post_ffn[:], sh.m[:, 5 * KT:6 * KT, 0], sh.par[:, P_POST_FFN:P_POST_FFN + KT],
                            ALU.mult).then_inc(m_done, 1)

        @block.scalar
        def _(e):
            e.wait_ge(lam_v, 1)
            e.activation(lam[:, 1], lam[:, 0], ACT.Abs).then_inc(lam_s, 1)
            e.wait_ge(lam_s, 1)
            e.activation(lam[:, 1], lam[:, 1], ACT.Exp, scale=-1.0).then_inc(lam_s, 1)
            e.wait_ge(lam_v, 2)
            e.activation(lam[:, 3], lam[:, 2], ACT.Ln).then_inc(lam_s, 1)
            e.wait_ge(lam_v, 9)
            e.wait_ge(zero, 2)
            for i in range(2):
                e.sem_inc(g_out[i], 16)

            def evacuate(m, g):
                j, t0, tn = groups[g]
                e.wait_ge(mm_ok, m * GROUPS + g + 1 + GROUPS)
                src = ps_d[g % 3][:, 0:tn]
                if j == 0:
                    c0 = t0 + PAD_LEFT if t0 < N_CTX else t0 + PAD_LEFT + 3
                    e.activation(pad[:, c0:c0 + tn], src, ACT.Copy).then_inc(evac, 1)
                elif j == 1:
                    e.activation(gy[:, t0 - N_CTX:t0 - N_CTX + tn], src, ACT.Gelu_apprx_tanh).then_inc(evac, 1)
                else:
                    if t0 == N_CTX:
                        e.wait_ge(g_out[j - 2], m * 16 + 16)
                    e.activation(gm[:, j - 2, t0 - N_CTX:t0 - N_CTX + tn], src, ACT.Sigmoid,
                                 bias=cols[:, 2 + j:3 + j]).then_inc(evac, 1)

            e.sem_inc(ada_used, 1)
            ada = weight_view(io["w_ada"][0])
            of_tile = lambda x, lo, hi: x[:, lo:hi].rearrange("p (g m) -> p g m", m=KT)
            rows = lam[:].rearrange("p r n -> p (r n)")

            def store_y(m):
                e.wait_ge(y_step, m * 2 + 2)
                e.dma_start(sh.y_lru[bass.ds(m, 1)].rearrange("o p n -> (o p) n"), y[:]).then_inc(y_out, 16)

            def turn(m, first):
                e.wait_ge(ada_used, m + 1)
                e.dma_start(ada_w[:], ada[:, :, bass.ds(m * 512 + 2 * D, 512)]).then_inc(ada_in, 16)
                for c0, src in ((0, of_tile(sh.par, P_B_RG, P_B_RG + 32)), (4, of_tile(sh.par, P_B_MERGE, P_B_MERGE + 16)),
                                (6, of_tile(rows, 64, 96))):
                    src = src[:, :, bass.ds(m, 1)]
                    e.activation(cols[:, c0:c0 + src.shape[1]].unsqueeze(2), src, ACT.Copy).then_inc(cols_ok, 1)
                e.wait_ge(cols_ok, m * 3 + 3)
                for g in range(3):
                    evacuate(m, g)
                if not first:
                    store_y(m - 1)
                for g in range(3, 7):
                    evacuate(m, g)
                e.wait_ge(evac, m * GROUPS + 7 + GROUPS)
                e.dma_start(sh.gates[bass.ds(m, 1)].rearrange("o p n -> (o p) n"), gm[:, 0]).then_inc(g_out[0], 16)
                n = 0
                for g, dst in enumerate((r, r, ig, ig)):
                    d = g % 2
                    for t0, tn in SEG_ALL:
                        e.wait_ge(gate_ps, m * GATES + n + 1 + GATES)
                        e.activation(dst[:, d, t0:t0 + tn], ps_g[n % 4][:, 0:tn], ACT.Sigmoid,
                                     bias=cols[:, g:g + 1]).then_inc(gate_ok, 1)
                        n += 1
                for d in range(2):
                    e.wait_ge(gate_ok, m * GATES + GATES + 12)
                    e.activation(a[:, d], r[:, d], ACT.Exp, scale=cols[:, 8 + d:9 + d]).then_inc(a_ok, 1)
                    e.activation(r[:, d], r[:, d], ACT.Tanh, scale=cols[:, 6 + d:7 + d]).then_inc(th_ok, 1)
                for g in range(7, GROUPS):
                    evacuate(m, g)
                e.wait_ge(evac, m * GROUPS + GROUPS + GROUPS)
                e.dma_start(sh.gates[bass.ds(m + KT, 1)].rearrange("o p n -> (o p) n"), gm[:, 1]).then_inc(g_out[1], 16)
                for d in range(2):
                    e.wait_ge(m_ok, m * 2 + d + 1)
                    e.activation(q[:, d], q[:, d], ACT.Sqrt).then_inc(sq_ok, 1)

            turn(0, True)
            with e.Fori(1, KT) as m:
                turn(m, False)
            store_y(KT - 1)
            e.wait_ge(y_out, 16 + 16 * KT)
            for i in range(2):
                e.wait_ge(g_out[i], 16 + 16 * KT)


class WeightStream:

    def __init__(self, nc, sh, ctx, tag, slots):
        sb = lambda n, d: ctx.enter_context(nc.sbuf_tensor(f"{tag}_{n}", [P, slots, KT, P], d))
        self.raw, self.hi, self.lo = sb("raw", F32), sb("w_hi", F32R), sb("w_lo", F32R)
        self.loaded = [sh.sem(f"{tag}_w_loaded{i}") for i in range(slots)]
        self.hi_ok = [sh.sem(f"{tag}_w_hi_ok{i}") for i in range(slots)]
        self.split = [sh.sem(f"{tag}_w_split{i}") for i in range(slots)]

    def split_job(self, e, ones, slot, earlier, credit=0):
        e.wait_ge(self.loaded[slot], earlier * 16 + 16)
        e.tensor_tensor(self.hi[:, slot], self.raw[:, slot], ones.unsqueeze(1).broadcast_to([P, KT, P]),
                        ALU.mult).then_inc(self.hi_ok[slot], 1)
        e.wait_ge(self.hi_ok[slot], earlier + 1)
        e.tensor_tensor(self.lo[:, slot], self.raw[:, slot], self.hi[:, slot].bitcast(F32),
                        ALU.subtract).then_inc(self.split[slot], 1)


def merge(nc, sh, io):
    with ExitStack() as ctx:
        sb = lambda n, s, d=F32: ctx.enter_context(nc.sbuf_tensor(n, s, d))
        sem = sh.sem
        w = WeightStream(nc, sh, ctx, "m", 2)
        stage = sb("m_stage", [P, 2, SEQ])
        gate = sb("m_gate", [P, 2, SEQ])
        tmp = sb("m_tmp", [P, 2, 512])
        sq = sb("m_sq", [P, 2, SEQ])
        sacc = sb("m_sacc", [P, SEQ])
        rs = sb("m_rs", [P, SEQ])
        tok = sb("m_tok", [P, KT, D])
        ps = [ctx.enter_context(nc.psum_tensor(f"m_ps{i}", [P, 512], F32)) for i in range(4)]
        ps_s = ctx.enter_context(nc.psum_tensor("m_ps_s", [P, 2, 512], F32))
        ps_t = [ctx.enter_context(nc.psum_tensor(f"m_ps_t{i}", [P, 512], F32)) for i in range(2)]
        y_in = [sem(f"m_y_in{i}") for i in range(2)]
        g_in = [sem(f"m_g_in{i}") for i in range(2)]
        tok_in, v_hi_ok, v_lo_ok, mm_ok, evac, part, gates_used = (
            sem(f"m_{x}") for x in ("tok_in", "v_hi_ok", "v_lo_ok", "mm_ok", "evac", "part", "gates_used"))
        sq_ok, sacc_ok, sum_ps, ln_ok, rs_ok, xt_ps, t_ok, h_ok, ut_ok = (
            sem(f"m_{x}") for x in ("sq_ok", "sacc_ok", "sum_ps", "ln_ok", "rs_ok", "xt_ps", "t_ok", "h_ok", "ut_ok"))
        block = ctx.enter_context(nc.Block())
        weights = [weight_view(io[n][0]) for n in ("w_branch_dn", "w_branch_lru", "w_out")]
        h2 = sh.h2

        @block.sync
        def _(e):
            for b in range(3):
                if b < 2:
                    for k in range(KT):
                        n = b * KT + k
                        if n >= 2:
                            e.wait_ge(v_lo_ok, n - 1)
                        e.dma_start(stage[:, k % 2], (sh.y_dn, sh.y_lru)[b][k]).then_inc(y_in[k % 2], 16)
                with e.Fori(0, KT // 2) as i:
                    for s in range(2):
                        e.wait_ge(w.split[s], i + b * KT // 2 + 1)
                        e.dma_start(w.raw[:, s], weights[b][:, :, bass.ds(i * 2 * P + s * P, P)]).then_inc(w.loaded[s], 16)
                        if b < 2:
                            e.wait_ge(gates_used, i * 2 + b * KT + s + 1)
                            e.dma_start(gate[:, s], sh.gates[bass.ds(i * 2 + b * KT + s, 1)].rearrange("o p n -> (o p) n")).then_inc(g_in[s], 16)

        @block.gpsimd
        def _(e):
            for s in range(2):
                e.sem_inc(w.split[s], 1)
            e.sem_inc(gates_used, 2)
            e.sem_inc(evac, 4)
            e.sem_inc(mm_ok, 4)
            for b in range(3):
                with e.Fori(0, KT // 2) as i:
                    for s in range(2):
                        e.wait_ge(mm_ok, i * 4 + b * 16 + 2 * s + 2)
                        w.split_job(e, sh.ones[:], s, i + b * KT // 2)
            e.wait_ge(sum_ps, 1)
            for k in range(1, KT):
                e.wait_ge(sq_ok, KT + k + 1)
                if k > 1:
                    e.wait_ge(sacc_ok, KT + k - 1)
                e.tensor_tensor(sacc[:], sq[:, 0] if k == 1 else sacc[:], sq[:, k % 2], ALU.add).then_inc(sacc_ok, 1)

        @block.tensor
        def _(e):
            for b in range(3):
                with e.Fori(0, KT // 2) as i:
                    for s in range(2):
                        e.wait_ge(w.split[s], i + b * KT // 2 + 2)
                        for t in range(2):
                            g = 2 * s + t
                            e.wait_ge(evac, i * 4 + b * 16 + g + 1)
                            n = 0
                            for k in range(KT):
                                if g == 0:
                                    e.wait_ge(v_lo_ok, b * KT + k + 1)
                                for wt, v in ((w.hi, sh.v_hi), (w.lo, sh.v_hi), (w.hi, sh.v_lo)):
                                    mm = e.matmul(ps[g][:], wt[:, s, k], v[:, k, t * 512:t * 512 + 512],
                                                  start=(n == 0), stop=(n == 3 * KT - 1))
                                    n += 1
                            mm.then_inc(mm_ok, 1)
            for r in range(2):
                e.wait_ge(sacc_ok, (KT, 2 * KT - 1)[r])
                if r:
                    e.wait_ge(ln_ok, 1)
                for t in range(2):
                    mm = e.matmul(ps_s[:, t], sh.ones[:], sacc[:, t * 512:t * 512 + 512], start=True, stop=True)
                mm.then_inc(sum_ps, 1)
                if r == 0:
                    e.wait_ge(tok_in, 16)
                    for k in range(KT):
                        for t in range(2):
                            n = 2 * k + t
                            if n >= 2:
                                e.wait_ge(h_ok, n - 1)
                            for j in range(4):
                                tr = e.transpose(ps_t[t][:, j * P:j * P + P], tok[:, 4 * t + j, k * P:k * P + P], sh.ident[:])
                            tr.then_inc(xt_ps, 1)

        @block.vector
        def _(e):
            def split_lo(n, src):
                e.wait_ge(v_hi_ok, n + 1)
                k = n % KT
                e.tensor_tensor(sh.v_lo[:, k], src, sh.v_hi[:, k].bitcast(F32), ALU.subtract).then_inc(v_lo_ok, 1)

            for b in range(2):
                for k in range(KT):
                    split_lo(b * KT + k, stage[:, k % 2])
                with e.Fori(0, KT // 2) as i:
                    for s in range(2):
                        e.wait_ge(g_in[s], i * 16 + b * 64 + 16)
                        for t in range(2):
                            g = 2 * s + t
                            e.wait_ge(mm_ok, i * 4 + b * 16 + g + 1 + 4)
                            dst = h2[:, bass.ds(i * 2 + s, 1), t * 512:t * 512 + 512].rearrange("p o n -> p (o n)")
                            gt = gate[:, s, t * 512:t * 512 + 512]
                            if b == 0:
                                e.tensor_tensor(dst, ps[g][:], gt, ALU.mult).then_inc(evac, 1)
                            else:
                                e.tensor_tensor(tmp[:, t], ps[g][:], gt, ALU.mult).then_inc(evac, 1)
                                e.wait_ge(evac, i * 4 + 16 + g + 1 + 4)
                                e.tensor_tensor(dst, dst, tmp[:, t], ALU.add).then_inc(part, 1)
                        if b == 0:
                            e.wait_ge(evac, i * 4 + 2 * s + 2 + 4)
                        else:
                            e.wait_ge(part, i * 4 + 2 * s + 2)
                        e.sem_inc(gates_used, 1)
            for k in range(KT):
                split_lo(2 * KT + k, h2[:, k])
            for k in range(KT):
                e.wait_ge(sq_ok, k + 1)
                if k:
                    e.wait_ge(sacc_ok, k)
                    e.tensor_tensor(sacc[:], sacc[:], sq[:, k % 2], ALU.add).then_inc(sacc_ok, 1)
                else:
                    e.tensor_copy(sacc[:], sq[:, 0]).then_inc(sacc_ok, 1)
            e.wait_ge(rs_ok, 1)
            for k in range(KT):
                e.scalar_tensor_tensor(out=h2[:, k], in0=h2[:, k], scalar=sh.post_mix[:, k:k + 1], in1=rs[:],
                                       op0=ALU.mult, op1=ALU.mult).then_inc(t_ok, 1)
                e.wait_ge(t_ok, k + 1)
                for t in range(2):
                    e.wait_ge(xt_ps, 2 * k + t + 1)
                    e.tensor_tensor(h2[:, k, t * 512:t * 512 + 512], h2[:, k, t * 512:t * 512 + 512], ps_t[t][:], ALU.add).then_inc(h_ok, 1)
            e.wait_ge(rs_ok, 2)
            for k in range(KT):
                e.wait_ge(h_ok, 2 * KT)
                if k >= 2:
                    e.wait_ge(v_lo_ok, 3 * KT + k - 1)
                e.scalar_tensor_tensor(out=stage[:, k % 2], in0=h2[:, k], scalar=sh.pre_ffn[:, k:k + 1], in1=rs[:],
                                       op0=ALU.mult, op1=ALU.mult).then_inc(t_ok, 1)
                if k:
                    split_lo(3 * KT + k - 1, stage[:, (k - 1) % 2])
            split_lo(4 * KT - 1, stage[:, 1])

        @block.scalar
        def _(e):
            e.dma_start(tok[:], io["x"][0].rearrange("(t p) d -> p t d", p=P)).then_inc(tok_in, 16)
            for b in range(2):
                for k in range(KT):
                    e.wait_ge(y_in[k % 2], 16 * (k // 2) + 64 * b + 16)
                    if b:
                        e.wait_ge(mm_ok, 20)
                    e.activation(sh.v_hi[:, k], stage[:, k % 2], ACT.Copy).then_inc(v_hi_ok, 1)
            e.wait_ge(part, 16)
            e.wait_ge(mm_ok, 36)
            for k in range(KT):
                e.activation(sh.v_hi[:, k], h2[:, k], ACT.Copy).then_inc(v_hi_ok, 1)
            for i in range(KT):
                for t in range(2):
                    g = 2 * (i % 2) + t
                    e.wait_ge(mm_ok, 36 + 2 * i + t + 1)
                    if t == 0:
                        e.wait_ge(v_lo_ok, 2 * KT + i + 1)
                    e.activation(h2[:, i, t * 512:t * 512 + 512], ps[g][:], ACT.Copy).then_inc(evac, 1)
                e.wait_ge(evac, 32 + 2 * i + 2 + 4)
                if i >= 2:
                    e.wait_ge(sacc_ok, i - 1)
                e.activation(sq[:, i % 2], h2[:, i], ACT.Square).then_inc(sq_ok, 1)
            for r in range(2):
                e.wait_ge(sum_ps, r + 1)
                if r:
                    e.wait_ge(h_ok, 2 * KT)
                    e.wait_ge(t_ok, KT)
                e.activation(rs[:], ps_s[:].rearrange("p t n -> p (t n)"), ACT.Ln, bias=sh.eps[:, 0:1], scale=1.0 / D).then_inc(ln_ok, 1)
                e.wait_ge(ln_ok, r + 1)
                e.activation(rs[:], rs[:], ACT.Exp, scale=-0.5).then_inc(rs_ok, 1)
                if r == 0:
                    for k in range(KT):
                        e.wait_ge(h_ok, 2 * k + 2)
                        e.wait_ge(sacc_ok, KT + (max(k - 2, 1) if k >= 2 else 0))
                        e.activation(sq[:, k % 2], h2[:, k], ACT.Square).then_inc(sq_ok, 1)
            for k in range(KT):
                e.wait_ge(t_ok, KT + k + 1)
                e.activation(stage[:, k % 2], stage[:, k % 2], ACT.Identity, bias=sh.m[:, 3 * KT + k, 0:1]).then_inc(ut_ok, 1)
                e.wait_ge(ut_ok, k + 1)
                e.activation(sh.v_hi[:, k], stage[:, k % 2], ACT.Copy).then_inc(v_hi_ok, 1)


def conv_ffn(nc, sh, io, out):
    with ExitStack() as ctx:
        sb = lambda n, s, d=F32: ctx.enter_context(nc.sbuf_tensor(n, s, d))
        sem = sh.sem
        w = WeightStream(nc, sh, ctx, "f", 3)
        img = sb("f_img", [P, ROWS + 2, GRID_W + 2])
        cacc = sb("f_cacc", [P, ROWS, GRID_W])
        ge = sb("f_ge", [P, SEQ])
        f = sb("f_f", [P, SEQ])
        f_hi = sb("f_hi", [P, 2, SEQ], F32R)
        f_lo = sb("f_lo", [P, 2, SEQ], F32R)
        acc = sb("f_acc", [P, KT, SEQ])
        rs = img[:].rearrange("p a b -> p (a b)")[:, 0:SEQ]
        ps_g = [ctx.enter_context(nc.psum_tensor(f"f_ps_g{i}", [P, 512], F32)) for i in range(2)]
        ps_v = [ctx.enter_context(nc.psum_tensor(f"f_ps_v{i}", [P, 512], F32)) for i in range(2)]
        ps_d = [ctx.enter_context(nc.psum_tensor(f"f_ps_d{i}", [P, 512], F32)) for i in range(4)]
        zero, gate_ps, gate_ok, val_ps, tap, ge_ok, f_ok, fh_ok, fl_ok, down_ps, down_ok = (
            sem(f"f_{x}") for x in ("zero", "gate_ps", "gate_ok", "val_ps", "tap", "ge_ok", "f_ok", "fh_ok", "fl_ok",
                                    "down_ps", "down_ok"))
        sq_ok, sacc_ok, sum_ps, ln_ok, rs_ok, t_ok, o_ok, ot_ps, ot_ok = (
            sem(f"f_{x}") for x in ("sq_ok", "sacc_ok", "sum_ps", "ln_ok", "rs_ok", "t_ok", "o_ok", "ot_ps", "ot_ok"))
        stored = [sem(f"f_stored{i}") for i in range(2)]
        block = ctx.enter_context(nc.Block())
        TURNS = FF_TILES // 2
        w_up = weight_view(io["w_up"][0])
        w_down = io["w_down"][0]

        def jobs(g, up, down):
            todo = [("gate", 0, 0, g * 2)] * up
            todo += [("down", 0, 1, g * 2 - 1), ("down", 1, 2, g * 2 - 1)] * down
            todo += [("val", 0, 0, g * 2 + 1), ("gate", 1, 1, g * 2), ("val", 1, 2, g * 2)] * up
            return todo

        def acc_rows(t):
            return (ge, f)[t % 2][:]

        def slot_free(e, g, kind, i):
            first = isinstance(g, int) and g == 0
            if kind == "gate" and i == 0 and not first:
                e.wait_ge(val_ps, g * 4 - 2)
            elif kind == "val" and i == 0:
                e.wait_ge(gate_ps, g * 4 + 2)
            elif kind == "down":
                e.wait_ge((gate_ps, val_ps)[i], g * 4)
            elif i == 1 and not first:
                e.wait_ge(down_ps, g * 16)

        def turns(e, body):
            body(0, 1, 0)
            with e.Fori(1, TURNS) as g:
                body(g, 1, 1)
            body(TURNS, 0, 1)

        @block.sync
        def _(e):
            def body(g, up, down):
                for kind, i, slot, earlier in jobs(g, up, down):
                    if not (isinstance(earlier, int) and earlier == 0):
                        e.wait_ge(w.split[slot], earlier)
                    if kind == "down":
                        rows = w_down[bass.ds(g * 2 * P + (i - 2) * P, P)]
                        e.dma_start(w.raw[:, slot].rearrange("p k n -> p (k n)"), rows).then_inc(w.loaded[slot], 16)
                    else:
                        c0 = i * P + (D_FF if kind == "val" else 0)
                        e.dma_start(w.raw[:, slot], w_up[:, :, bass.ds(g * 2 * P + c0, P)]).then_inc(w.loaded[slot], 16)
            turns(e, body)
            for t in range(KT):
                e.wait_ge(ot_ok, 2 * t + 2)
                e.dma_start(out[0, t * P:t * P + P, :], acc_rows(t)).then_inc(stored[t % 2], 16)
            e.wait_ge(stored[0], 64)
            e.wait_ge(stored[1], 64)

        @block.gpsimd
        def _(e):
            e.memset(img[:], 0.0).then_inc(zero, 1)

            def low(g, i):
                e.wait_ge(fh_ok, g * 2 + i + 1)
                e.tensor_tensor(f_lo[:, i], f[:], f_hi[:, i].bitcast(F32), ALU.subtract).then_inc(fl_ok, 1)

            def body(g, up, down):
                for kind, i, slot, earlier in jobs(g, up, down):
                    if kind == "val" and i == 1:
                        low(g, 0)
                    slot_free(e, g, kind, i)
                    w.split_job(e, sh.ones[:], slot, earlier)
                    if kind == "down" and i == 1:
                        low(g - 1, 1)

            turns(e, body)

        @block.tensor
        def _(e):
            e.sem_inc(gate_ok, 2)
            e.sem_inc(f_ok, 2)
            e.sem_inc(down_ok, 4)

            def up_job(g, kind, i, slot, earlier):
                e.wait_ge(w.split[slot], earlier + 1)
                for t in range(2):
                    n = 0
                    if kind == "gate":
                        e.wait_ge(gate_ok, g * 4 + i * 2 + t + 1)
                    else:
                        e.wait_ge(f_ok, g * 4 + i * 2 + t + 1)
                    for k in range(KT):
                        for wt, v in ((w.hi, sh.v_hi), (w.lo, sh.v_hi), (w.hi, sh.v_lo)):
                            mm = e.matmul((ps_g if kind == "gate" else ps_v)[t][:], wt[:, slot, k], v[:, k, t * 512:t * 512 + 512],
                                          start=(n == 0), stop=(n == 3 * KT - 1))
                            n += 1
                    mm.then_inc(gate_ps if kind == "gate" else val_ps, 1)

            def down_jobs(g):
                e.wait_ge(w.split[1], g * 2)
                e.wait_ge(w.split[2], g * 2)
                e.wait_ge(fl_ok, g * 2 + 1)
                for n in range(KT):
                    for t in range(2):
                        grp = 2 * n + t
                        e.wait_ge(down_ok, g * 16 + grp - 16 + 1)
                        m = 0
                        for i, s in ((0, 1), (1, 2)):
                            for wt, v in ((w.hi, f_hi), (w.lo, f_hi), (w.hi, f_lo)):
                                mm = e.matmul(ps_d[grp % 4][:], wt[:, s, n], v[:, i, t * 512:t * 512 + 512],
                                              start=(m == 0), stop=(m == 5))
                                m += 1
                        mm.then_inc(down_ps, 1)

            def body(g, up, down):
                for kind, i, slot, earlier in jobs(g, up, down):
                    if kind != "down":
                        up_job(g, kind, i, slot, earlier)
                    elif i == 0:
                        down_jobs(g)
            turns(e, body)
            e.wait_ge(sacc_ok, KT)
            for t in range(2):
                mm = e.matmul(ps_g[t][:], sh.ones[:], cacc[:].rearrange("p a b -> p (a b)")[:, t * 512:t * 512 + 512], start=True, stop=True)
            mm.then_inc(sum_ps, 1)
            e.wait_ge(o_ok, KT)
            for t in range(KT):
                for half in range(2):
                    n = 2 * t + half
                    if n >= 4:
                        e.wait_ge(ot_ok, n - 3)
                    for j in range(4):
                        tr = e.transpose(ps_d[n % 4][:, j * P:j * P + P], acc[:, 4 * half + j, t * P:t * P + P], sh.ident[:])
                    tr.then_inc(ot_ps, 1)

        @block.vector
        def _(e):
            def conv_tap(g, i, t):
                if t == 0:
                    e.wait_ge(gate_ok, g * 4 + 2 * i + 2 + 2)
                    e.wait_ge(ge_ok, g * 2 + i + 1)
                else:
                    e.wait_ge(tap, g * 18 + i * 9 + t)
                src = img[:, t // 3:t // 3 + ROWS, t % 3:t % 3 + GRID_W]
                wt = sh.par[:, bass.ds(g * 2 + P_FFN_DW + t * FF_TILES + i, 1)]
                if t == 0:
                    e.tensor_scalar(cacc[:], src, wt, sh.par[:, bass.ds(g * 2 + P_FFN_DW_B + i, 1)], ALU.mult, ALU.add).then_inc(tap, 1)
                else:
                    e.scalar_tensor_tensor(out=cacc[:], in0=src, scalar=wt, in1=cacc[:], op0=ALU.mult, op1=ALU.add).then_inc(tap, 1)

            def down_part(g, grp):
                n, t = grp // 2, grp % 2
                e.wait_ge(down_ps, g * 16 + grp - 16 + 1)
                dst = acc[:, n, t * 512:t * 512 + 512]
                e.tensor_tensor(dst, dst, ps_d[grp % 4][:], ALU.add).then_inc(down_ok, 1)

            def product(g, i):
                e.wait_ge(ge_ok, g * 2 + i + 2)
                for t in range(2):
                    e.wait_ge(val_ps, g * 4 + 2 * i + t + 1)
                    if t == 0:
                        e.wait_ge(fl_ok, g * 2 + i + 1)
                    e.tensor_tensor(f[:, t * 512:t * 512 + 512], ge[:, t * 512:t * 512 + 512], ps_v[t][:], ALU.mult).then_inc(f_ok, 1)

            def square_sum(k):
                e.wait_ge(sq_ok, k + 1)
                sums, square = cacc[:].rearrange("p a b -> p (a b)"), (ge, f)[k % 2][:]
                if k == 0:
                    e.tensor_copy(sums, square).then_inc(sacc_ok, 1)
                else:
                    e.wait_ge(sacc_ok, k)
                    e.tensor_tensor(sums, sums, square, ALU.add).then_inc(sacc_ok, 1)

            def body(g, up, down):
                taps_ahead = 7 if down else 0
                for grp in range(16 * down):
                    down_part(g, grp)
                    if up and grp % 2 and grp // 2 < taps_ahead:
                        conv_tap(g, 0, grp // 2)
                    if not up and grp % 2 and grp > 1:
                        square_sum(grp // 2 - 1)
                if up:
                    for t in range(taps_ahead, 9):
                        conv_tap(g, 0, t)
                    product(g, 0)
                    for t in range(9):
                        conv_tap(g, 1, t)
                    product(g, 1)

            e.memset(acc[:], 0.0).then_inc(zero, 1)
            e.wait_ge(zero, 2)
            e.sem_inc(ge_ok, 1)
            turns(e, body)
            square_sum(KT - 1)
            e.wait_ge(rs_ok, 1)
            for k in range(KT):
                e.scalar_tensor_tensor(out=acc[:, k], in0=acc[:, k], scalar=sh.post_ffn[:, k:k + 1], in1=rs[:],
                                       op0=ALU.mult, op1=ALU.mult).then_inc(t_ok, 1)
                e.wait_ge(t_ok, k + 1)
                e.tensor_tensor(acc[:, k], acc[:, k], sh.h2[:, k], ALU.add).then_inc(o_ok, 1)

        @block.scalar
        def _(e):
            e.wait_ge(zero, 2)
            e.sem_inc(fl_ok, 1)

            def gate_out(g, i):
                for t in range(2):
                    e.wait_ge(gate_ps, g * 4 + 2 * i + t + 1)
                    e.activation(img[:, 1 + 8 * t:9 + 8 * t, 1:1 + GRID_W], ps_g[t][:].rearrange("p (a b) -> p a b", b=GRID_W),
                                 ACT.Copy).then_inc(gate_ok, 1)

            def gelu(g, i):
                e.wait_ge(tap, g * 18 + 9 * i + 9)
                e.activation(ge[:], cacc[:].rearrange("p a b -> p (a b)"), ACT.Gelu_apprx_tanh).then_inc(ge_ok, 1)

            def f_high(g, i):
                e.wait_ge(f_ok, g * 4 + 2 * i + 2 + 2)
                if not (isinstance(g, int) and g == 0):
                    e.wait_ge(down_ps, g * 16)
                e.activation(f_hi[:, i], f[:], ACT.Copy).then_inc(fh_ok, 1)

            def body(g, up, down):
                if up:
                    gate_out(g, 0)
                    gelu(g, 0)
                    f_high(g, 0)
                    gate_out(g, 1)
                    gelu(g, 1)
                    f_high(g, 1)
            turns(e, body)
            for k in range(KT):
                e.wait_ge(down_ok, 4 + 16 * (TURNS - 1) + 2 * k + 2)
                if k >= 2:
                    e.wait_ge(sacc_ok, k - 1)
                e.activation((ge, f)[k % 2][:], acc[:, k], ACT.Square).then_inc(sq_ok, 1)
            e.wait_ge(sum_ps, 1)
            for t in range(2):
                e.activation(rs[:, t * 512:t * 512 + 512], ps_g[t][:], ACT.Ln, bias=sh.eps[:, 0:1], scale=1.0 / D).then_inc(ln_ok, 1)
            e.wait_ge(ln_ok, 2)
            e.activation(rs[:], rs[:], ACT.Exp, scale=-0.5).then_inc(rs_ok, 1)
            for t in range(KT):
                if t >= 2:
                    e.wait_ge(stored[t % 2], 16 * (t // 2))
                for half in range(2):
                    e.wait_ge(ot_ps, 2 * t + half + 1)
                    e.activation(acc_rows(t)[:, half * 512:half * 512 + 512], ps_d[(2 * t + half) % 4][:], ACT.Copy).then_inc(ot_ok, 1)


def build(nc, io, out):
    sh = Shared()
    with ExitStack() as ctx:
        sb = lambda n, s, d=F32: ctx.enter_context(nc.sbuf_tensor(n, s, d))
        sh.held = []

        def take(name):
            sh.held.append(nc.alloc_semaphore(name))
            return sh.held[-1]

        sh.sem = take
        sh.par = sb("par", [P, N_PAR])
        sh.m = sb("m_ada", [P, 48, 2])
        sh.pre_mix = sb("v_pre_mix", [P, 2, KT])
        sh.post_mix = sb("v_post_mix", [P, KT])
        sh.pre_ffn = sb("v_pre_ffn", [P, KT])
        sh.post_ffn = sb("v_post_ffn", [P, KT])
        sh.silu_c = sb("silu_c", [P, KT, 2])
        sh.ident = sb("ident", [P, P])
        sh.ones = sb("ones", [P, P])
        sh.warm = sb("warm", [P, 2])
        sh.eps = sb("eps", [P, 2])
        sh.grow_d = nc.dram_tensor("decay_scratch", (16, T), F32).ap()
        sh.k_scratch = nc.dram_tensor("k_scratch", (HEADS, P, T), F32).ap()
        sh.y_dn = nc.dram_tensor("y_dn_scratch", (HEADS, P, SEQ), F32).ap()
        sh.y_lru = nc.dram_tensor("y_lru_scratch", (KT, P, SEQ), F32).ap()
        sh.gates = nc.dram_tensor("gate_scratch", (2 * KT, P, SEQ), F32).ap()
        with ExitStack() as mixers:
            sh.u_hi = mixers.enter_context(nc.sbuf_tensor("u_hi", [P, KT, T], F32R))
            sh.u_lo = mixers.enter_context(nc.sbuf_tensor("u_lo", [P, KT, T], F32R))
            norm_and_modulate(nc, sh, io)
            end_phase(nc, sh)
            with ExitStack() as heads:
                hb = lambda n, s, d=F32: heads.enter_context(nc.sbuf_tensor(n, s, d))
                sh.off = hb("mask_off", [P, 2, P])
                sh.strict = hb("mask_strict", [P, 2, P], BF16)
                sh.level = hb("mask_level", [P, 2, 7, P], BF16)
                sh.ident_r = hb("ident_r", [P, 2, P], F32R)
                per_token = lambda n: hb(n, [P, NCH, 16])
                sh.gcol, sh.eg, sh.neg_eg = per_token("gcol"), per_token("eg"), per_token("neg_eg")
                sh.eg_tot, sh.k_decay = per_token("eg_tot"), per_token("k_decay")
                sh.beta, sh.neg_beta = per_token("beta"), per_token("neg_beta")
                with ExitStack() as tri:
                    sh.tri = tri.enter_context(nc.sbuf_tensor("mask_tri", [P, 2, P], F32))
                    sh.last_row = tri.enter_context(nc.sbuf_tensor("last_row", [P, 2, P], F32))
                    decay_gates(nc, sh, io)
                    end_phase(nc, sh)
                deltanet(nc, sh, io)
                end_phase(nc, sh)
            rg_lru(nc, sh, io)
            end_phase(nc, sh)
        sh.h2 = sb("h2", [P, KT, SEQ])
        sh.v_hi = sb("v_hi", [P, KT, SEQ], F32R)
        sh.v_lo = sb("v_lo", [P, KT, SEQ], F32R)
        merge(nc, sh, io)
        end_phase(nc, sh)
        conv_ffn(nc, sh, io, out)


_INS = ["x", "c", "ctx", "c_ctx", "w_ada", "b_ada", "g_pre_mix", "g_post_mix", "g_pre_ffn", "g_post_ffn", "w_in",
        "b_merge", "dn_conv", "dn_a_log", "dn_dt_bias", "dn_onorm", "lru_conv", "lru_conv_b", "lru_w_rg", "lru_b_rg",
        "lru_w_ig", "lru_b_ig", "lru_lambda", "w_branch_dn", "w_branch_lru", "w_out", "w_up", "ffn_dw", "ffn_dw_b",
        "w_down"]
_OUTS = [((1, 1024, 1024), "float32")]


def kernel(**inputs):
    import numpy as _np
    import concourse.bacc as _bacc
    from concourse import mybir as _mybir
    from concourse.bass_utils import run_bass_kernel_spmd as _run

    nc = _bacc.Bacc("TRN2", target_bir_lowering=False, num_devices=1)
    arrays, io = {}, {}
    for name in _INS:
        a = _np.ascontiguousarray(inputs[name])
        arrays[f"in_{name}_dram"] = a
        io[name] = nc.dram_tensor(f"in_{name}_dram", a.shape, _mybir.dt.from_np(a.dtype), kind="ExternalInput").ap()
    outs = []
    for i, (shape, dtype) in enumerate(_OUTS):
        dt = _mybir.dt.from_np(_np.dtype(dtype))
        outs.append(nc.dram_tensor(f"out_{i}_dram", shape, dt, kind="ExternalOutput").ap())
    build(nc, io, outs[0])
    r = _run(nc, [arrays], core_ids=[0])
    return r.results[0]["out_0_dram"]
```
